# Optimizing a Trainium2 kernel written in Bass

```python
import math
import jax, jax.numpy as jnp
from jax import lax
import numpy as np

D_MODEL = 1024
BATCH = 1
SEQ = 256
DEPTH = 1

HEAD_DIM = 64
MIX_WIDTH = D_MODEL
ATT_HEADS = 8
GDN_HEADS = 8
ATT_WIDTH = ATT_HEADS * HEAD_DIM
GDN_WIDTH = GDN_HEADS * HEAD_DIM
MOBA_BLOCK = 256
MOBA_TOPK = 3
MOBA_QCHUNK = 32
GDN_CHUNK = 64
CONV_WIDTH = 4
D_FF = 4 * D_MODEL
REL_BUCKETS = 32
REL_MAX_EXACT = 16
REL_MAX_DIST = 128
EPS = 1e-6
IN_SIZES = [ATT_WIDTH, ATT_WIDTH, ATT_WIDTH, 3 * GDN_WIDTH, GDN_WIDTH, GDN_HEADS, GDN_HEADS]
IN_COLS = sum(IN_SIZES)


def rms_norm(x, w):
    xf = x.astype(jnp.float32)
    y = xf * lax.rsqrt(jnp.mean(xf * xf, axis=-1, keepdims=True) + EPS)
    return (y * w.astype(jnp.float32)).astype(x.dtype)

def l2_normalize(x):
    xf = x.astype(jnp.float32)
    return xf * lax.rsqrt(jnp.sum(xf * xf, axis=-1, keepdims=True) + EPS)

def rel_bucket(dist):
    d = jnp.maximum(dist, 0)
    large = REL_MAX_EXACT + (
        jnp.log(jnp.maximum(d, 1).astype(jnp.float32) / REL_MAX_EXACT)
        / math.log(REL_MAX_DIST / REL_MAX_EXACT)
        * (REL_BUCKETS - REL_MAX_EXACT)
    ).astype(jnp.int32)
    large = jnp.minimum(large, REL_BUCKETS - 1)
    return jnp.where(d < REL_MAX_EXACT, d, large)

def moba_attention(q, k, v, rel_bias):
    B, S, H, dh = q.shape
    nb = -(-S // MOBA_BLOCK)
    s_pad = nb * MOBA_BLOCK
    qh = q.transpose(0, 2, 1, 3)
    pad = ((0, 0), (0, 0), (0, s_pad - S), (0, 0))
    kh = jnp.pad(k.transpose(0, 2, 1, 3), pad)
    vh = jnp.pad(v.transpose(0, 2, 1, 3), pad)
    kb = kh.reshape(B, H, nb, MOBA_BLOCK, dh)
    vb = vh.reshape(B, H, nb, MOBA_BLOCK, dh)
    kmean = jnp.mean(kb.astype(jnp.float32), axis=3)
    rel_bias = rel_bias.astype(jnp.float32)

    gate = jnp.einsum('bhsd,bhnd->bhsn', qh.astype(jnp.float32), kmean)
    pos = jnp.arange(S)
    n_past = pos // MOBA_BLOCK
    past = jnp.arange(nb)[None, :] < n_past[:, None]
    gate = jnp.where(past, gate, -jnp.inf)
    kk = min(MOBA_TOPK, nb)
    _, sel = lax.top_k(gate, kk)
    sel_valid = jnp.arange(kk)[None, :] < jnp.minimum(n_past, MOBA_TOPK)[:, None]

    nc = S // MOBA_QCHUNK
    q_c = qh.reshape(B, H, nc, MOBA_QCHUNK, dh).transpose(2, 0, 1, 3, 4)
    sel_c = sel.reshape(B, H, nc, MOBA_QCHUNK, kk).transpose(2, 0, 1, 3, 4)
    valid_c = sel_valid.reshape(nc, MOBA_QCHUNK, kk)
    scale = HEAD_DIM ** -0.5
    off = jnp.arange(MOBA_BLOCK)
    head_idx = jnp.arange(H)[:, None, None, None]
    gather_blocks = jax.vmap(jax.vmap(lambda blocks, idx: blocks[idx]))

    def chunk_fn(args):
        c, qc, sc, vc = args
        q0 = c * MOBA_QCHUNK
        qpos = q0 + jnp.arange(MOBA_QCHUNK)
        own = q0 // MOBA_BLOCK
        k_own = lax.dynamic_slice_in_dim(kb, own, 1, axis=2)[:, :, 0]
        v_own = lax.dynamic_slice_in_dim(vb, own, 1, axis=2)[:, :, 0]
        d_own = qpos[:, None] - (own * MOBA_BLOCK + off)[None, :]
        l_own = jnp.einsum('bhqd,bhkd->bhqk', qc, k_own).astype(jnp.float32) * scale
        l_own = l_own + rel_bias[:, rel_bucket(d_own)]
        l_own = jnp.where(d_own >= 0, l_own, -jnp.inf)
        k_sel = gather_blocks(kb, sc)
        v_sel = gather_blocks(vb, sc)
        d_sel = qpos[:, None, None] - (sc[..., None] * MOBA_BLOCK + off)
        l_sel = jnp.einsum('bhqd,bhqnkd->bhqnk', qc, k_sel).astype(jnp.float32) * scale
        l_sel = l_sel + rel_bias[head_idx, rel_bucket(d_sel)]
        l_sel = jnp.where(vc[:, :, None], l_sel, -jnp.inf)
        logits = jnp.concatenate(
            [l_own, l_sel.reshape(B, H, MOBA_QCHUNK, kk * MOBA_BLOCK)], axis=-1)
        p = jax.nn.softmax(logits, axis=-1)
        p_own = p[..., :MOBA_BLOCK].astype(v.dtype)
        p_sel = p[..., MOBA_BLOCK:].reshape(B, H, MOBA_QCHUNK, kk, MOBA_BLOCK).astype(v.dtype)
        return (jnp.einsum('bhqk,bhkd->bhqd', p_own, v_own)
                + jnp.einsum('bhqnk,bhqnkd->bhqd', p_sel, v_sel))

    o = lax.map(chunk_fn, (jnp.arange(nc), q_c, sel_c, valid_c))
    return o.transpose(1, 0, 3, 2, 4).reshape(B, S, H * dh)

def causal_depthwise_conv_silu(x, w):
    C = x.shape[-1]
    y = lax.conv_general_dilated(
        x, w[:, None, :].astype(x.dtype), window_strides=(1,),
        padding=[(CONV_WIDTH - 1, 0)], dimension_numbers=('NWC', 'WIO', 'NWC'),
        feature_group_count=C)
    return jax.nn.silu(y)

def gated_deltanet(qkv, z, a, b, conv_w, A_log, dt_bias, norm_w):
    B, S, _ = qkv.shape
    H, dh, C = GDN_HEADS, HEAD_DIM, GDN_CHUNK
    nc = S // C
    qkv = causal_depthwise_conv_silu(qkv, conv_w)
    q, k, v = jnp.split(qkv, 3, axis=-1)
    q = l2_normalize(q.reshape(B, S, H, dh)) * (dh ** -0.5)
    k = l2_normalize(k.reshape(B, S, H, dh))
    v = v.reshape(B, S, H, dh).astype(jnp.float32)
    beta = jax.nn.sigmoid(b.astype(jnp.float32))
    g = -jnp.exp(A_log.astype(jnp.float32)) * jax.nn.softplus(
        a.astype(jnp.float32) + dt_bias.astype(jnp.float32))

    def to_chunks(t):
        t = jnp.moveaxis(t, 2, 1)
        return t.reshape((B, H, nc, C) + t.shape[3:])

    qc, kc, vc = to_chunks(q), to_chunks(k), to_chunks(v)
    bc = to_chunks(beta)
    g_cum = jnp.cumsum(to_chunks(g), axis=-1)
    causal = jnp.tril(jnp.ones((C, C), dtype=bool))
    strict = jnp.tril(jnp.ones((C, C), dtype=bool), k=-1)
    decay = jnp.exp(jnp.where(causal, g_cum[..., :, None] - g_cum[..., None, :], -jnp.inf))
    k_beta = kc * bc[..., None]
    m = jnp.where(strict, jnp.einsum('bhnid,bhnjd->bhnij', k_beta, kc) * decay, 0.0)
    a_mat = m + jnp.eye(C, dtype=jnp.float32)
    rhs = jnp.concatenate([vc * bc[..., None], k_beta * jnp.exp(g_cum)[..., None]], axis=-1)
    uw = lax.linalg.triangular_solve(a_mat, rhs, left_side=True, lower=True, unit_diagonal=True)
    u, w = uw[..., :dh], uw[..., dh:]
    attn_intra = jnp.einsum('bhnid,bhnjd->bhnij', qc, kc) * decay
    q_dec = qc * jnp.exp(g_cum)[..., None]
    k_dec = kc * jnp.exp(g_cum[..., -1:] - g_cum)[..., None]
    g_last = jnp.exp(g_cum[..., -1])

    def step(state, xs):
        u_c, w_c, q_c, k_c, a_c, gl = xs
        v_new = u_c - jnp.einsum('bhck,bhkv->bhcv', w_c, state)
        o = jnp.einsum('bhck,bhkv->bhcv', q_c, state) + jnp.einsum('bhcs,bhsv->bhcv', a_c, v_new)
        state = state * gl[..., None, None] + jnp.einsum('bhck,bhcv->bhkv', k_c, v_new)
        return state, o

    xs = tuple(jnp.moveaxis(t, 2, 0) for t in (u, w, q_dec, k_dec, attn_intra, g_last))
    state0 = jnp.zeros((B, H, dh, dh), dtype=jnp.float32)
    _, o = lax.scan(step, state0, xs)
    o = jnp.moveaxis(o, 0, 2).reshape(B, H, S, dh).transpose(0, 2, 1, 3)
    o = o * lax.rsqrt(jnp.mean(o * o, axis=-1, keepdims=True) + EPS) * norm_w.astype(jnp.float32)
    o = o * jax.nn.silu(z.reshape(B, S, H, dh).astype(jnp.float32))
    return o.reshape(B, S, GDN_WIDTH).astype(qkv.dtype)

def first_inputs(seed: int = 0) -> dict:
    key = jax.random.key(seed)
    ks = jax.random.split(key, 16)
    f32 = jnp.float32
    x = jax.random.normal(ks[0], (BATCH, SEQ, D_MODEL), f32)
    w_in = jax.random.normal(ks[1], (DEPTH, D_MODEL, IN_COLS), f32) * D_MODEL ** -0.5
    w_out = jax.random.normal(ks[2], (DEPTH, MIX_WIDTH, D_MODEL), f32) * MIX_WIDTH ** -0.5
    conv_w = jax.random.normal(ks[3], (DEPTH, CONV_WIDTH, 3 * GDN_WIDTH), f32) * CONV_WIDTH ** -0.5
    A_log = jnp.log(jax.random.uniform(ks[4], (DEPTH, GDN_HEADS), f32, 1.0, 16.0))
    dt = jnp.exp(jax.random.uniform(ks[5], (DEPTH, GDN_HEADS), f32, math.log(1e-3), math.log(1e-1)))
    dt_bias = dt + jnp.log(-jnp.expm1(-dt))
    gdn_norm_w = 1.0 + 0.05 * jax.random.normal(ks[6], (DEPTH, HEAD_DIM), f32)
    rel_bias = 0.5 * jax.random.normal(ks[7], (ATT_HEADS, REL_BUCKETS), f32)
    pre_mix_norm = 1.0 + 0.05 * jax.random.normal(ks[8], (DEPTH, D_MODEL), f32)
    post_mix_norm = 1.0 + 0.05 * jax.random.normal(ks[9], (DEPTH, D_MODEL), f32)
    pre_mlp_norm = 1.0 + 0.05 * jax.random.normal(ks[10], (DEPTH, D_MODEL), f32)
    post_mlp_norm = 1.0 + 0.05 * jax.random.normal(ks[11], (DEPTH, D_MODEL), f32)
    w_up = jax.random.normal(ks[12], (DEPTH, D_MODEL, D_FF), f32) * D_MODEL ** -0.5
    w_down = jax.random.normal(ks[13], (DEPTH, D_FF, D_MODEL), f32) * D_FF ** -0.5
    return {"x": x, "w_in": w_in, "w_out": w_out, "conv_w": conv_w, "A_log": A_log,
            "dt_bias": dt_bias, "gdn_norm_w": gdn_norm_w, "rel_bias": rel_bias,
            "pre_mix_norm": pre_mix_norm, "post_mix_norm": post_mix_norm,
            "pre_mlp_norm": pre_mlp_norm, "post_mlp_norm": post_mlp_norm,
            "w_up": w_up, "w_down": w_down}

def first_block(x, w_in, w_out, conv_w, A_log, dt_bias, gdn_norm_w, rel_bias,
              pre_mix_norm, post_mix_norm, pre_mlp_norm, post_mlp_norm, w_up, w_down):
    B, S, _ = x.shape
    split_points = np.cumsum(IN_SIZES)[:-1].tolist()
    for l in range(DEPTH):
        h = rms_norm(x, pre_mix_norm[l])
        proj = jnp.einsum('bsd,dc->bsc', h, w_in[l])
        att_q, att_k, att_v, gdn_qkv, gdn_z, gdn_a, gdn_b = jnp.split(proj, split_points, axis=-1)
        o_att = moba_attention(att_q.reshape(B, S, ATT_HEADS, HEAD_DIM),
                               att_k.reshape(B, S, ATT_HEADS, HEAD_DIM),
                               att_v.reshape(B, S, ATT_HEADS, HEAD_DIM), rel_bias)
        o_gdn = gated_deltanet(gdn_qkv, gdn_z, gdn_a, gdn_b, conv_w[l], A_log[l],
                               dt_bias[l], gdn_norm_w[l])
        mix = jnp.einsum('bsc,cd->bsd', jnp.concatenate([o_att, o_gdn], axis=-1), w_out[l])
        x = x + rms_norm(mix, post_mix_norm[l])
        h = rms_norm(x, pre_mlp_norm[l])
        m = jnp.einsum('bsf,fd->bsd', jnp.square(jax.nn.relu(jnp.einsum('bsd,df->bsf', h, w_up[l]))), w_down[l])
        x = x + rms_norm(m, post_mlp_norm[l])
    return x


CONV_WIDTH_2 = D_MODEL
CONV_K = 3
RET_HEADS = 4
RET_QK_DIM = D_MODEL // RET_HEADS
RET_V_DIM = 2 * RET_QK_DIM
RET_QK = RET_HEADS * RET_QK_DIM
RET_V = RET_HEADS * RET_V_DIM
CHUNK = 128
ROPE_BASE = 10000.0
D_FF_2 = -(-8 * D_MODEL // (3 * 256)) * 256
IN_SIZES_2 = (CONV_WIDTH_2, CONV_WIDTH_2, CONV_WIDTH_2, RET_QK, RET_QK, RET_V, RET_V, D_MODEL, D_MODEL)
N_IN = sum(IN_SIZES_2)


def rmsnorm(x, g):
    xf = x.astype(jnp.float32)
    y = xf * lax.rsqrt(jnp.mean(xf * xf, axis=-1, keepdims=True) + EPS)
    return (y * g.astype(jnp.float32)).astype(x.dtype)

def rotary(t):
    s, d = t.shape[1], t.shape[-1]
    pos = jnp.arange(s, dtype=jnp.float32)
    freqs = ROPE_BASE ** (-jnp.arange(0, d, 2, dtype=jnp.float32) / d)
    ang = pos[:, None] * freqs[None, :]
    cos = jnp.cos(ang)[None, :, None, :]
    sin = jnp.sin(ang)[None, :, None, :]
    t1, t2 = t[..., : d // 2], t[..., d // 2:]
    return jnp.concatenate([t1 * cos - t2 * sin, t1 * sin + t2 * cos], axis=-1)

def retention_chunkwise(q, k, v, log_gamma, strict):
    b, h, s, dk = q.shape
    dv = v.shape[-1]
    n_chunks = s // CHUNK

    def chunks(t):
        return jnp.moveaxis(t.reshape(b, h, n_chunks, CHUNK, t.shape[-1]), 2, 0)

    idx = jnp.arange(CHUNK, dtype=jnp.float32)
    diff = idx[:, None] - idx[None, :]
    mask = (diff > 0) if strict else (diff >= 0)
    lg = log_gamma[:, None, None]
    intra_decay = jnp.where(mask[None], jnp.exp(jnp.maximum(diff, 0.0)[None] * lg), 0.0)
    xi = jnp.exp((idx + 1.0)[None, :] * log_gamma[:, None])[..., None]
    zeta = jnp.exp((CHUNK - 1.0 - idx)[None, :] * log_gamma[:, None])[..., None]
    chunk_decay = jnp.exp(CHUNK * log_gamma)[:, None, None]

    def step(state, qkv):
        qc, kc, vc = qkv
        scores = jnp.einsum('bhcd,bhmd->bhcm', qc, kc) * intra_decay
        inner = jnp.einsum('bhcm,bhme->bhce', scores, vc)
        cross = jnp.einsum('bhcd,bhde->bhce', qc, state) * xi
        state = chunk_decay * state + jnp.einsum('bhcd,bhce->bhde', kc * zeta, vc)
        return state, inner + cross

    state0 = jnp.zeros((b, h, dk, dv), jnp.float32)
    _, out = lax.scan(step, state0, (chunks(q), chunks(k), chunks(v)))
    return jnp.moveaxis(out, 0, 2).reshape(b, h, s, dv)

def second_inputs(seed: int = 0) -> dict:
    key = jax.random.key(seed)
    ks = jax.random.split(key, 16)
    f32 = jnp.float32

    def normal(k, shape, scale):
        return jax.random.normal(k, shape, f32) * scale

    def gain(k, shape):
        return 1.0 + 0.05 * jax.random.normal(k, shape, f32)

    base_logit = jnp.log(2.0 ** (5.0 + jnp.arange(RET_HEADS, dtype=f32)) - 1.0)
    return {
        "x": jax.random.normal(ks[0], (BATCH, SEQ, D_MODEL), f32),
        "g_mix": gain(ks[1], (DEPTH, D_MODEL)),
        "w_in": normal(ks[2], (DEPTH, D_MODEL, N_IN), D_MODEL ** -0.5),
        "w_conv": normal(ks[3], (DEPTH, CONV_K, CONV_WIDTH_2), CONV_K ** -0.5),
        "dec_f": base_logit[None] + 0.01 * jax.random.normal(ks[4], (DEPTH, RET_HEADS), f32),
        "dec_b": base_logit[None] + 0.01 * jax.random.normal(ks[5], (DEPTH, RET_HEADS), f32),
        "g_ret": gain(ks[6], (DEPTH, RET_V)),
        "w_a_out": normal(ks[7], (DEPTH, CONV_WIDTH_2, D_MODEL), CONV_WIDTH_2 ** -0.5),
        "w_r_out": normal(ks[8], (DEPTH, RET_V, D_MODEL), RET_V ** -0.5),
        "w_o": normal(ks[9], (DEPTH, D_MODEL, D_MODEL), D_MODEL ** -0.5),
        "g_ffn": gain(ks[10], (DEPTH, D_MODEL)),
        "w_ff_gate": normal(ks[11], (DEPTH, D_MODEL, D_FF_2), D_MODEL ** -0.5),
        "w_ff_up": normal(ks[12], (DEPTH, D_MODEL, D_FF_2), D_MODEL ** -0.5),
        "w_ff_down": normal(ks[13], (DEPTH, D_FF_2, D_MODEL), D_FF_2 ** -0.5),
        "g_final": gain(ks[14], (D_MODEL,)),
    }

def second_block(x, g_mix, w_in, w_conv, dec_f, dec_b, g_ret, w_a_out, w_r_out, w_o,
              g_ffn, w_ff_gate, w_ff_up, w_ff_down, g_final):
    b, s, _ = x.shape
    dt = x.dtype
    split_points = [int(p) for p in np.cumsum(IN_SIZES_2)[:-1]]
    for l in range(DEPTH):
        h = rmsnorm(x, g_mix[l])
        proj = h @ w_in[l]
        xc, gb, gc, q, k, v, g_sw, gate_a, gate_r = jnp.split(proj, split_points, axis=-1)

        u = gc * xc
        u_pad = jnp.pad(u, ((0, 0), (CONV_K // 2, CONV_K // 2), (0, 0)))
        conv = u_pad[:, 0:s] * w_conv[l, 0]
        for tap in range(1, CONV_K):
            conv = conv + u_pad[:, tap:tap + s] * w_conv[l, tap]
        y_a = (gb * conv) @ w_a_out[l]

        qf = rotary(q.reshape(b, s, RET_HEADS, RET_QK_DIM).astype(jnp.float32)) * (RET_QK_DIM ** -0.5)
        kf = rotary(k.reshape(b, s, RET_HEADS, RET_QK_DIM).astype(jnp.float32))
        vf = v.reshape(b, s, RET_HEADS, RET_V_DIM).astype(jnp.float32)
        qf, kf, vf = (jnp.transpose(t, (0, 2, 1, 3)) for t in (qf, kf, vf))
        lg_f = jax.nn.log_sigmoid(dec_f[l].astype(jnp.float32))
        lg_b = jax.nn.log_sigmoid(dec_b[l].astype(jnp.float32))
        ret_f = retention_chunkwise(qf, kf, vf, lg_f, strict=False)
        ret_b = jnp.flip(retention_chunkwise(jnp.flip(qf, 2), jnp.flip(kf, 2), jnp.flip(vf, 2),
                                             lg_b, strict=True), 2)
        ret = ret_f + ret_b
        mu = jnp.mean(ret, axis=-1, keepdims=True)
        var = jnp.mean(jnp.square(ret - mu), axis=-1, keepdims=True)
        ret = (ret - mu) * lax.rsqrt(var + EPS)
        ret = jnp.transpose(ret, (0, 2, 1, 3)).reshape(b, s, RET_V) * g_ret[l].astype(jnp.float32)
        y_r = (ret.astype(dt) * jax.nn.silu(g_sw)) @ w_r_out[l]

        merged = jax.nn.sigmoid(gate_a) * y_a + jax.nn.sigmoid(gate_r) * y_r
        x = x + merged @ w_o[l]

        h2 = rmsnorm(x, g_ffn[l])
        x = x + (jax.nn.silu(h2 @ w_ff_gate[l]) * (h2 @ w_ff_up[l])) @ w_ff_down[l]
    return rmsnorm(x, g_final)


def setup_inputs(seed=0):
    out = dict(first_inputs(seed))
    for name, value in second_inputs(seed + 1).items():
        if name != "x":
            out[name + "_2"] = value
    return out


def reference(
    x, w_in, w_out, conv_w, A_log, dt_bias, gdn_norm_w, rel_bias, pre_mix_norm, post_mix_norm,
    pre_mlp_norm, post_mlp_norm, w_up, w_down, g_mix_2, w_in_2, w_conv_2, dec_f_2, dec_b_2,
    g_ret_2, w_a_out_2, w_r_out_2, w_o_2, g_ffn_2, w_ff_gate_2, w_ff_up_2, w_ff_down_2,
    g_final_2,
):
    x = first_block(
        x, w_in, w_out, conv_w, A_log, dt_bias, gdn_norm_w, rel_bias, pre_mix_norm,
        post_mix_norm, pre_mlp_norm, post_mlp_norm, w_up, w_down,
    )
    return second_block(
        x, g_mix_2, w_in_2, w_conv_2, dec_f_2, dec_b_2, g_ret_2, w_a_out_2, w_r_out_2, w_o_2,
        g_ffn_2, w_ff_gate_2, w_ff_up_2, w_ff_down_2, g_final_2,
    )


_drawn_inputs = setup_inputs


def setup_inputs(seed=0):
    import zlib

    import numpy as np

    out = dict(_drawn_inputs(seed))
    spreads = {}
    factors = {'g_ret_2': 6.306, 'g_ffn_2': 3.732}
    for name, (base, spread) in spreads.items():
        noise = np.random.default_rng([zlib.crc32(name.encode()), seed]).standard_normal(out[name].shape)
        drawn = base * np.exp(spread * noise) if base else spread * noise
        out[name] = __import__('jax').numpy.asarray(drawn.astype(out[name].dtype))
    for name, factor in factors.items():
        out[name] = (out[name] * factor).astype(out[name].dtype)
    return out
```

```python
import math
from contextlib import ExitStack

import numpy as np

import concourse.bass as bass
from concourse import mybir

F32 = mybir.dt.float32
FR = mybir.dt.float32r
ALU = mybir.AluOpType
ACT = mybir.ActivationFunctionType
AXX = mybir.AxisListType.X
EPS = 1e-6

S = 256
D = 1024
RR = 3
HR = 4
AHEAD = 2
U = 2048
NEG = -1e30



def buckets():
    d = np.arange(256)
    large = 16 + (np.log(np.maximum(d, 1).astype(np.float32) / np.float32(16))
                  / np.float32(math.log(128 / 16)) * np.float32(16)).astype(np.int32)
    return np.where(d < 16, d, np.minimum(large, 31))


LEVELS = (2, 4, 8, 16, 32, 64)


def level_mask(s):
    i = np.arange(128)[:, None]
    j = np.arange(128)[None, :]
    low = (i // (2 * s) == j // (2 * s)) & (i // s % 2 == 1) & (j // s % 2 == 0)
    return (low | (i == j)).astype(np.float32)


def table_gdn():
    i = np.arange(128)[:, None]
    j = np.arange(128)[None, :]
    parts = [(i <= j).astype(np.float32), -(i < j).astype(np.float32), np.ones((128, 128), np.float32),
             level_mask(1).T] + [level_mask(s) for s in LEVELS]
    return np.ascontiguousarray(np.concatenate(parts, 1))


def table_onehot():
    t = np.zeros((32, 384), np.float32)
    m = np.zeros((8, 384), np.float32)
    b = buckets()
    for j in range(384):
        if 255 - j >= 0:
            t[b[255 - j], j] = 1.0
        else:
            m[:, j] = NEG
    return t, m


def table_rope():
    pos = np.arange(S, dtype=np.float32)
    freqs = (np.float32(10000.0) ** (-np.arange(0, 256, 2, dtype=np.float32) / np.float32(256))).astype(np.float32)
    ang = (freqs[:, None] * pos[None, :]).astype(np.float32).astype(np.float64)
    return np.ascontiguousarray(np.concatenate([np.cos(ang), np.sin(ang)], 1).astype(np.float32))


def table_dist():
    m = np.arange(128)[:, None, None] + 128 * np.arange(2)[None, :, None]
    n = np.arange(256)[None, None, :]
    a = np.maximum(n - m, 0).astype(np.float32).reshape(128, 512)
    b = np.maximum(m - n, 0).astype(np.float32).reshape(128, 512)
    return np.ascontiguousarray(np.concatenate([a, b], 1))


def plan():
    u = [("Z", "w_in", 3472)]
    u += [("B", "w_in", 1536 + 256 * i) for i in range(6)]
    u += [("C", "w_in", 3072, k) for k in (0, 4)]
    u += [("B", "w_in", 256 * i) for i in range(4)]
    u += [("C", "w_in", 1024, k) for k in (0, 4)]
    u += [("A", "w_out", 2 * k) for k in range(4)]
    for i in range(16):
        u.append(("B", "w_up", 256 * i))
        if i >= 1:
            u.append(("A", "w_down", 2 * (i - 1)))
    u.append(("A", "w_down", 30))
    for i in range(4):
        u += [("B", "w_in_2", 256 * i), ("B", "w_in_2", 2048 + 256 * i), ("B", "w_in_2", 1024 + 256 * i)]
    for i in range(4):
        u += [("B", "w_in_2", 3072 + 256 * i), ("B", "w_in_2", 4096 + 256 * i)]
    u += [("A", "w_a_out_2", 2 * k) for k in range(4)]
    for cb in range(2):
        u += [("C", "w_in_2", 9216 + 512 * cb, k) for k in (0, 4)]
    for h in range(5):
        if h < 4:
            u += [("C", "w_in_2", 5120 + 512 * h, k) for k in (0, 4)]
            u += [("B", "w_in_2", 7168 + 512 * h), ("B", "w_in_2", 7168 + 512 * h + 256)]
        if h >= 1:
            u += [("A", "w_r_out_2", 4 * (h - 1)), ("A", "w_r_out_2", 4 * (h - 1) + 2)]
        if h == 3:
            for cb in range(2):
                u += [("C", "w_in_2", 10240 + 512 * cb, k) for k in (0, 4)]
    u += [("A", "w_o_2", 2 * k) for k in range(4)]
    for i in range(11):
        u += [("B", "w_ff_gate_2", 256 * i), ("B", "w_ff_up_2", 256 * i)]
        if i >= 1:
            u.append(("A", "w_ff_down_2", 2 * (i - 1)))
    u.append(("A", "w_ff_down_2", 20))
    return u


PLAN = plan()

SM = {}
_at = 0
for _n, _w in (("pre_mix", 8), ("pre_mlp", 8), ("g_mix", 8), ("g_ffn", 8), ("conv1", 48), ("conv2", 24),
               ("g_ret", 16), ("A_log", 8), ("dt_bias", 8), ("dec_f", 4), ("dec_b", 4), ("gdn_w", 64)):
    SM[_n] = (_at, _w)
    _at += _w
NSM = _at


class Engine:

    def __init__(self, sem):
        self.sem, self.count, self.queue, self.seen = sem, 0, [], {}

    def wait(self, *tokens):
        for sem, value in tokens:
            if self.seen.get(id(sem), 0) < value:
                self.seen[id(sem)] = value
                self.queue.append(lambda e, s=sem, v=value: e.wait_ge(s, v))

    def op(self, fn, *tokens):
        self.wait(*tokens)
        self.count += 1
        self.queue.append(lambda e: fn(e).then_inc(self.sem, 1))
        return self.sem, self.count

    def quiet(self, fn, *tokens):
        self.wait(*tokens)
        self.queue.append(fn)

    def now(self):
        return self.sem, self.count


def build(nc, A, out):
    with ExitStack() as top:
        nsem = [0]

        def sem(name):
            nsem[0] += 1
            return top.enter_context(nc.semaphore(name))

        def sb(stack, name, shape, dt=F32):
            return stack.enter_context(nc.sbuf_tensor("t_" + name, shape, dt))

        PE, AC, DV, PO, SP = (Engine(sem("s_" + n)) for n in ("pe", "act", "dve", "pool", "sp"))
        bank = [top.enter_context(nc.psum_tensor(f"bank{i}", [128, 512], F32)) for i in range(8)]
        free = [[] for _ in range(8)]
        turn = [0]

        def work():
            b = 4 + turn[0] % 4
            turn[0] += 1
            return b

        raw = sb(top, "raw", [128, RR, U])
        wh = sb(top, "wh", [128, HR, U], FR)
        wl = sb(top, "wl", [128, HR, U], FR)
        hh = sb(top, "hh", [128, 8, S], FR)
        hl = sb(top, "hl", [128, 8, S], FR)
        x = sb(top, "x", [128, 2, D])
        xt = sb(top, "xt", [128, 2, D])
        ident = sb(top, "ident", [128, 128])
        small = sb(top, "small", [128, NSM])
        st = sb(top, "st", [128, 128])
        half = sb(top, "half", [128, 2])

        def par(name):
            a, w = SM[name]
            return small[:, a:a + w]

        def load(dst, src, *tokens, n=1):
            s = sem(f"dma{nsem[0]}")
            SP.quiet(lambda e: e.dma_start(dst, src).then_inc(s, 16), *tokens)
            return s, 16

        raw_sem = [sem(f"raw{i}") for i in range(RR)]
        split = []
        used = []

        def dma_unit(i):
            r = i % RR
            if i >= RR:
                SP.wait(*split[i - RR])
            if PLAN[i][0] == "Z":
                SP.quiet(lambda e: e.dma_start(raw[:, r, 0:1024], A["W"][i, :, 0:1024]).then_inc(raw_sem[r], 16))
            else:
                SP.quiet(lambda e: e.dma_start(raw[:, r, :], A["W"][i]).then_inc(raw_sem[r], 16))

        def prep(upto):
            while len(split) < min(upto + 1, len(PLAN)):
                i = len(split)
                if i >= RR:
                    dma_unit(i)
                r, h = i % RR, i % HR
                n = 1024 if PLAN[i][0] == "Z" else U
                arrived = (raw_sem[r], 16 * (i // RR + 1))
                freed = [used[i - HR]] if i >= HR else []
                t1 = AC.op(lambda e, h=h, r=r, n=n: e.copy(wh[:, h, 0:n], raw[:, r, 0:n]), arrived, *freed)
                t2 = DV.op(lambda e, h=h, r=r, n=n: e.tensor_tensor(wl[:, h, 0:n], raw[:, r, 0:n], wh[:, h, 0:n].bitcast(F32),
                                                     ALU.subtract), arrived, t1, *freed)
                split.append((t1, t2))

        def unit(kind):
            i = len(used)
            assert PLAN[i][0] == kind, (i, PLAN[i], kind)
            prep(i + AHEAD)
            PE.wait(*split[i])
            return i % HR

        def done(tok):
            used.append(tok)

        PASS = ((0, 0), (0, 1), (1, 0))

        def b_unit(act, ready, kind="B"):
            b = work()
            h = unit(kind)
            w = (wh, wl)
            nt = 1 if kind == "Z" else 2
            PE.wait(*free[b])
            for c in range(nt):
                for k in range(8):
                    if c == 0:
                        PE.wait(*ready[k])
                    for n, (i, j) in enumerate(PASS):
                        lhs = w[i][:, h, k * 128 * nt + c * 128:k * 128 * nt + c * 128 + 128]
                        rhs = act[j][:, k, :]
                        first, last = k == 0 and n == 0, k == 7 and n == 2
                        f = (lambda e, o=bank[b][:, c * S:c * S + S], l=lhs, r=rhs, a=first, z=last:
                             e.matmul(o, l, r, start=a, stop=z))
                        if last and c == nt - 1:
                            tok = PE.op(f)
                        else:
                            PE.quiet(f)
            done(tok)
            return b, tok

        def a_unit(kind, act, ready, ks, outs, first, last):
            h = unit(kind)
            w = (wh, wl)
            nk, ncb = len(ks), len(outs[0])
            if first:
                for t in range(2):
                    for b in outs[t]:
                        PE.wait(*free[b])
            tok = None
            for kk, k in enumerate(ks):
                PE.wait(*ready[k])
                for t in range(2):
                    for n, (j, i) in enumerate(((0, 0), (0, 1), (1, 0))):
                        for c in range(ncb):
                            lhs = act[j][:, k, t * 128:t * 128 + 128]
                            rhs = w[i][:, h, kk * 512 * ncb + c * 512:kk * 512 * ncb + c * 512 + 512]
                            a = first and kk == 0 and n == 0
                            z = last and kk == nk - 1 and n == 2
                            f = (lambda e, o=bank[outs[t][c]][:], l=lhs, r=rhs, a=a, z=z:
                                 e.matmul(o, l, r, start=a, stop=z))
                            if kk == nk - 1 and t == 1 and n == 2 and c == ncb - 1:
                                tok = PE.op(f)
                            else:
                                PE.quiet(f)
            done(tok)
            return tok

        def c_block(act, ready):
            outs = [[work()], [work()]]
            a_unit("C", act, ready, range(0, 4), outs, True, False)
            tok = a_unit("C", act, ready, range(4, 8), outs, False, True)
            return outs[0][0], outs[1][0], tok

        def rsqrt2(src, *tokens, c=0):
            a = DV.op(lambda e: e.tensor_scalar(src, src, EPS, None, ALU.add), *tokens)
            return PO.op(lambda e: e.tensor_tensor(src, src, half[:], ALU.pow), a, t_half)

        def norm_split(w, dst, prior, *tokens):
            ms = st[:, 0:2]
            toks = []
            for t in range(2):
                toks.append(AC.op(lambda e, t=t: e.activation(xt[:, t, :], x[:, t, :], ACT.Square, scale=1.0 / 32,
                                                              accum_out=ms[:, t:t + 1]), *tokens))
            r = rsqrt2(ms, *toks)
            xn = [DV.op(lambda e, t=t: e.tensor_scalar(xt[:, t, :], x[:, t, :], ms[:, t:t + 1], None, ALU.mult), r)
                  for t in range(2)]
            ready = []
            for p in range(4):
                b = work()
                PE.wait(*free[b])
                for kk in range(2):
                    k = 2 * p + kk
                    for t in range(2):
                        PE.wait(xn[t])
                        f = (lambda e, kk=kk, k=k, t=t, b=b: e.transpose(
                            bank[b][:, kk * S + t * 128:kk * S + t * 128 + 128], xt[:, t, k * 128:k * 128 + 128],
                            ident[:]))
                        if kk == 1 and t == 1:
                            tok = PE.op(f, t_id)
                        else:
                            PE.quiet(f, t_id)
                his = []
                for kk in range(2):
                    k = 2 * p + kk
                    his.append(AC.op(lambda e, kk=kk, k=k, b=b: e.activation(
                        dst[0][:, k, :], bank[b][:, kk * S:kk * S + S], ACT.Copy, scale=w[:, k:k + 1]),
                        tok, t_small, *prior))
                for kk in range(2):
                    k = 2 * p + kk
                    lo = DV.op(lambda e, kk=kk, k=k, b=b: e.scalar_tensor_tensor(
                        out=dst[1][:, k, :], in0=bank[b][:, kk * S:kk * S + S], scalar=w[:, k:k + 1],
                        in1=dst[0][:, k, :].bitcast(F32), op0=ALU.mult, op1=ALU.subtract), his[1], t_small, *prior)
                    ready.append([his[kk], lo])
                free[b] = [lo]
            return ready

        def post_norm(wbc, t_w, tok):
            part = st[:, 4:8]
            sq = []
            for t in range(2):
                for c in range(2):
                    sq.append(AC.op(lambda e, t=t, c=c: e.activation(
                        xt[:, t, c * 512:c * 512 + 512], bank[2 * t + c][:], ACT.Square, scale=1.0 / 32,
                        accum_out=part[:, 2 * t + c:2 * t + c + 1]), tok))
            ms = st[:, 8:10]
            a = DV.op(lambda e: e.tensor_reduce(ms, part.rearrange("p (t c) -> p t c", c=2), AXX, ALU.add), *sq)
            r = rsqrt2(ms, a)
            last = []
            for t in range(2):
                for c in range(2):
                    m = DV.op(lambda e, t=t, c=c: e.scalar_tensor_tensor(
                        out=xt[:, t, c * 512:c * 512 + 512], in0=bank[2 * t + c][:], scalar=ms[:, t:t + 1],
                        in1=wbc[:, c * 512:c * 512 + 512], op0=ALU.mult, op1=ALU.mult), r, t_w, sq[2 * t + c])
                    free[2 * t + c] = [m]
                a = DV.op(lambda e, t=t: e.tensor_tensor(x[:, t, :], x[:, t, :], xt[:, t, :], ALU.add), m)
                last.append(a)
            return last

        t_x = load(x[:], A["x"].rearrange("(t p) d -> p t d", p=128))
        t_small = load(small[:], A["small"])
        t_id = load(ident[:], A["ident"])
        for i in range(RR):
            dma_unit(i)
        t_half = PO.op(lambda e: e.memset(half[:], -0.5))

        def move(eng, o, i, *tokens):
            if eng is AC:
                return AC.op(lambda e: e.copy(o, i), *tokens)
            return eng.op(lambda e: e.tensor_copy(o, i), *tokens)

        def tt(eng, o, a, b, op, *tokens):
            return eng.op(lambda e: e.tensor_tensor(o, a, b, op), *tokens)

        def ts(eng, o, a, s1, s2, op0, op1, *tokens):
            if op1 is None:
                return eng.op(lambda e: e.tensor_scalar(o, a, s1, None, op0), *tokens)
            return eng.op(lambda e: e.tensor_scalar(o, a, s1, s2, op0, op1), *tokens)

        def stt(o, a, s, b, op0, op1, *tokens):
            return DV.op(lambda e: e.scalar_tensor_tensor(out=o, in0=a, scalar=s, in1=b, op0=op0, op1=op1), *tokens)

        def act(o, i, f, *tokens, **kw):
            return AC.op(lambda e: e.activation(o, i, f, **kw), *tokens)

        def mm(o, l, r, start, stop, *tokens, tok=True, skip=False):
            if skip:
                f = lambda e: e.matmul(o, l, r, start=start, stop=stop, skip_group_check=True)
            else:
                f = lambda e: e.matmul(o, l, r, start=start, stop=stop)
            return PE.op(f, *tokens) if tok else PE.quiet(f, *tokens)

        def tr(o, i, *tokens, tok=True):
            f = lambda e: e.transpose(o, i, ident[:])
            return PE.op(f, t_id, *tokens) if tok else PE.quiet(f, t_id, *tokens)

        def bc(a, n):
            return a.unsqueeze(2).broadcast_to([128, a.shape[1], n])

        def rep(a, m):
            return a.unsqueeze(1).broadcast_to([128, m, a.shape[1]])

        H = (hh, hl)

        with ExitStack() as p1:
            cin = sb(p1, "cin", [128, 12, S + 3])
            cout = sb(p1, "cout", [128, 12, S])
            tm = sb(p1, "tm", [128, 2, 1536])
            kb = sb(p1, "kb", [128, 2, 512])
            dU = sb(p1, "dU", [128, 16, 128])
            AT = sb(p1, "AT", [128, 16, 128])
            tab = sb(p1, "tab", [128, 10, 128])
            gs = sb(p1, "gs", [128, 256])
            X = cin[:].rearrange("p a b -> p (a b)")[:, 0:2048].rearrange("p (s n) -> p s n", s=16)
            zz = cin[:].rearrange("p a b -> p (a b)")[:, 2048:3072].rearrange("p (t n) -> p t n", t=2)
            XT = xt[:].rearrange("p t (s n) -> p (t s) n", n=128)
            kT = cout[:].rearrange("p a s -> p (a s)")[:, 0:1024].rearrange("p (j s) -> p j s", j=4)
            kq = cout[:].rearrange("p a s -> p (a s)")[:, 1024:3072].rearrange(
                "p (j c w n) -> p j c w n", j=4, c=2, w=2)
            kd = tm[:, 0, 0:512]
            triu, nstrict, ones, m1T = (tab[:, i, :] for i in range(4))

            pa = ExitStack()
            qT = sb(pa, "qT", [128, 4, S])
            kTa = sb(pa, "kTa", [128, 4, S])
            va = sb(pa, "va", [128, 2, 512])
            P = sb(pa, "P", [128, 2, 384])
            PT = sb(pa, "PT", [128, 2, 384])
            T = sb(pa, "T", [128, 2, 384])
            flip = sb(pa, "flip", [128, 128])
            t_flip = load(flip[:], A["flip"])

            t_tab = load(tab[:], A["tab"].rearrange("p (a n) -> p a n", n=128))
            oh = cout[0:32, 0:2, :].rearrange("p a s -> p (a s)")[:, 0:384]
            ng = cout[0:8, 2:4, :].rearrange("p a s -> p (a s)")[:, 0:384]
            rb = cout[0:32, 4, 0:8]
            rrow = cout[0:8, 5:7, :].rearrange("p a s -> p (a s)")[:, 0:384]
            t_oh = load(oh, A["onehot"])
            t_ng = load(ng, A["neg"])
            t_rb = load(rb, A["rbT"])
            b = work()
            t = mm(bank[b][0:8, 0:384], rb, oh, True, True, t_oh, t_rb)
            t_row = tt(DV, rrow, bank[b][0:8, 0:384], ng, ALU.add, t, t_ng)
            free[b] = [t_row]
            t_scr = load(A["scr"], rrow, t_row)

            def load_T(h, *tokens):
                dst = T[:, h % 2, :]
                scr = A["scr"]
                a = bass.AP(scr.tensor, h * 384, [[1, 128], [1, 256]])
                b_ = bass.AP(scr.tensor, h * 384 + 128, [[1, 128], [1, 128]])
                s = sem(f"T{h}")
                SP.quiet(lambda e: e.dma_start(dst[:, 128:384], a).then_inc(s, 16), t_scr, *tokens)
                SP.quiet(lambda e: e.dma_start(dst[:, 0:128], b_).then_inc(s, 16))
                return s, 32

            prep(0)
            ready = norm_split(par("pre_mix"), H, [], t_x)

            b, t = b_unit(H, ready, "Z")
            ab = dU[:, 0:2, :].rearrange("p a n -> p (a n)")
            t = move(AC, ab, bank[b][:, 0:S], t)
            free[b] = [t]
            b = work()
            tr(bank[b][:, 0:128], ab[:, 0:128], t, *free[b], tok=False)
            t = tr(bank[b][:, 128:256], ab[:, 128:256])
            pv = bank[b][:, 0:256].rearrange("p (c n) -> p c n", c=2)
            sa = gs[:, 0:16].rearrange("p (c h) -> p c h", c=2)
            eb = gs[:, 16:32].rearrange("p (c h) -> p c h", c=2)
            sn = gs[:, 32:48]
            sa1, eb1 = gs[:, 0:16], gs[:, 16:32]
            t1 = tt(DV, sa, pv[:, :, 112:120], rep(par("dt_bias"), 2), ALU.add, t, t_small)
            tb = move(DV, eb, pv[:, :, 120:128], t)
            free[b] = [tb]
            t2 = stt(sn, sa1, -1.0, sa1, ALU.mult, ALU.min, t1)
            t2 = act(sn, sn, ACT.Exp, t2)
            tb = act(eb1, eb1, ACT.Exp, tb, scale=-1.0)
            ea = gs[:, 48:56]
            t3 = act(ea, par("A_log"), ACT.Exp, t_small)
            t2 = act(sn, sn, ACT.Ln, t2, bias=1.0)
            tb = ts(DV, eb1, eb1, 1.0, None, ALU.add, None, tb)
            beta = gs[:, 56:72]
            t_beta = DV.op(lambda e: e.reciprocal(beta, eb1), tb)
            t2 = stt(sn, sa1, 0.0, sn, ALU.max, ALU.add, t2)
            graw = gs[:, 72:88]
            t_g = stt(graw.rearrange("p (c h) -> p c h", c=2), sn.rearrange("p (c h) -> p c h", c=2), -1.0,
                      rep(ea, 2), ALU.mult, ALU.mult, t2, t3)
            b = work()
            mm(bank[b][:, 0:16], triu, graw, True, True, t_g, t_tab, *free[b], tok=False)
            t = mm(bank[b][:, 16:32], ones, graw, True, True)
            gc = gs[:, 88:104]
            eg = gs[:, 104:120]
            kdx = gs[:, 120:136]
            t_gc = move(DV, gs[:, 88:104], bank[b][:, 0:16], t)
            t = tt(DV, kdx, bank[b][:, 16:32], gc, ALU.subtract, t_gc)
            free[b] = [t]
            t_eg = act(eg, gc, ACT.Exp, t_gc)
            t_kdx = act(kdx, kdx, ACT.Exp, t)

            t_dec = []
            for g in range(4):
                b = work()
                PE.wait(*free[b])
                for i in range(4):
                    s = 4 * g + i
                    l = graw[:, s:s + 1].broadcast_to([128, 128])
                    t = mm(bank[b][:, i * 128:i * 128 + 128], l, triu, True, True, t_g)
                for i in range(4):
                    s = 4 * g + i
                    t_ = ts(DV, dU[:, s, :], bank[b][:, i * 128:i * 128 + 128], gc[:, s:s + 1], 0.0,
                            ALU.subtract, ALU.min, t, t_gc)
                free[b] = [t_]
                t_dec.append(t_)
            t = act(dU[:], dU[:], ACT.Exp, *t_dec)
            t_dU = tt(PO, dU[:], dU[:], rep(triu, 16), ALU.mult, t, t_tab)
            t_dS = tt(PO, AT[:], dU[:], rep(nstrict, 16), ALU.mult, t_dU)

            t_pad = PO.op(lambda e: e.memset(cin[:, :, 0:3], 0.0))
            cw = par("conv1").rearrange("p (a k) -> p a k", k=4)
            t_c = []
            t_silu = []
            for u in range(6):
                b, t = b_unit(H, ready)
                t = move(AC, cin[:, 2 * u:2 * u + 2, 3:], bank[b][:].rearrange("p (a s) -> p a s", a=2), t)
                free[b] = [t]
                for a in range(2 * u, 2 * u + 2):
                    t2 = ts(DV, cout[:, a, :], cin[:, a, 0:S], cw[:, a, 0:1], None, ALU.mult, None, t, t_pad, t_scr,
                            t_row)
                    for k in range(1, 4):
                        t2 = stt(cout[:, a, :], cin[:, a, k:k + S], cw[:, a, k:k + 1], cout[:, a, :],
                                 ALU.mult, ALU.add, t2)
                    t_c.append(t2)
                t_silu.append(act(cout[:, 2 * u:2 * u + 2, :], cout[:, 2 * u:2 * u + 2, :], ACT.Silu, t_c[-1],
                                  t_c[-2]))

            t_tm = {}
            sq = X[:].rearrange("p s n -> p (s n)")
            t_sq = []
            for w_ in range(3):
                for c in range(2):
                    b = work()
                    PE.wait(*free[b])
                    for a in range(4):
                        t = tr(bank[b][:, a * 128:a * 128 + 128], cout[:, 4 * w_ + a, c * 128:c * 128 + 128],
                               t_silu[2 * w_ + a // 2])
                    t_tm[w_, c] = move(AC, tm[:, c, w_ * 512:w_ * 512 + 512], bank[b][:], t)
                    free[b] = [t_tm[w_, c]]
                    if w_ < 2:
                        o = (c * 2 + w_) * 512
                        t2 = act(sq[:, o:o + 512], bank[b][:], ACT.Square, t, *t_c)
                        t_sq.append(t2)
                        free[b] = [t2]
            rn = gs[:, 136:168]
            t = DV.op(lambda e: e.tensor_reduce(rn, sq.rearrange("p (s n) -> p s n", n=64), AXX, ALU.add), *t_sq)
            t = ts(DV, rn, rn, EPS, None, ALU.add, None, t)
            t = act(rn, rn, ACT.Sqrt, t)
            t = DV.op(lambda e: e.reciprocal(rn, rn), t)
            rq = rn.rearrange("p (c w h) -> p c w h", c=2, w=2)[:, :, 0, :]
            t = ts(DV, rq, rq, 0.125, None, ALU.mult, None, t)
            t_n = []
            t_kb = []
            t_vb = []
            for c in range(2):
                o = tm[:, c, 0:1024].rearrange("p (s n) -> p s n", n=64)
                t_n.append(tt(DV, o, o, bc(rn[:, 16 * c:16 * c + 16], 64), ALU.mult, t, t_tm[0, c], t_tm[1, c]))
                t_kb.append(tt(DV, kb[:, c, :].rearrange("p (s n) -> p s n", n=64),
                               tm[:, c, 512:1024].rearrange("p (s n) -> p s n", n=64),
                               bc(beta[:, 8 * c:8 * c + 8], 64), ALU.mult, t_n[c], t_beta))
                o = tm[:, c, 1024:1536].rearrange("p (s n) -> p s n", n=64)
                t_vb.append(tt(PO, o, o, bc(beta[:, 8 * c:8 * c + 8], 64), ALU.mult, t_tm[2, c], t_beta))

            b0, b1, t = c_block(H, ready)
            tz = []
            for c, b in enumerate((b0, b1)):
                tz.append(act(zz[:, c, :], bank[b][:], ACT.Silu, t, *t_c, *t_sq))
                free[b] = [tz[-1]]
            zw = [tt(PO, zz[:, c, :].rearrange("p (h n) -> p h n", n=64), zz[:, c, :].rearrange("p (h n) -> p h n", n=64),
                     rep(par("gdn_w"), 8), ALU.mult, tz[c], t_small) for c in range(2)]

            t_qk = []
            for u in range(4):
                b, t = b_unit(H, ready)
                dst = (qT, kTa)[u // 2]
                t = act(dst[:, 2 * (u % 2):2 * (u % 2) + 2, :], bank[b][:].rearrange("p (a s) -> p a s", a=2), ACT.Copy,
                        t, scale=(0.125, 1.0)[u // 2])
                free[b] = [t]
                t_qk.append(t)

            t_kT = []
            for c in range(2):
                for w_, (src, dst, dep) in enumerate((
                        (tm[:, c, 512:1024], kT[:, :, c * 128:c * 128 + 128], t_n[c]),
                        (kb[:, c, :], kq[:, :, c, 0, :], t_kb[c]),
                        (tm[:, c, 0:512], kq[:, :, c, 1, :], t_n[c]))):
                    b = work()
                    PE.wait(*free[b])
                    for a in range(4):
                        t = tr(bank[b][:, a * 128:a * 128 + 128], src[:, a * 128:a * 128 + 128], dep)
                    t = move(AC, dst, bank[b][:].rearrange("p (a n) -> p a n", a=4), t)
                    free[b] = [t]
                    t_kT.append(t)
            t_kd = tt(PO, kd.rearrange("p (h n) -> p h n", n=64), tm[:, 0, 512:1024].rearrange("p (h n) -> p h n", n=64),
                      bc(kdx[:, 0:8], 64), ALU.mult, t_kdx, *t_kT)

            b0, b1, t = c_block(H, ready)
            t_v = []
            for c, b in enumerate((b0, b1)):
                t_v.append(move(AC, va[:, c, :], bank[b][:], t))
                free[b] = [t_v[-1]]
            w_in_read = PE.now()

            t_AT = []
            for g in range(8):
                b = work()
                PE.wait(*free[b])
                s0 = 8 * (g // 4) + 4 * (g % 4 // 2) + g % 2
                for i in range(2):
                    s = s0 + 2 * i
                    c, h = s // 8, s % 8
                    p0 = 64 * (h % 2)
                    t = mm(bank[b][:, i * 256:i * 256 + 256], kT[p0:p0 + 64, h // 2, c * 128:c * 128 + 128],
                           kq[p0:p0 + 64, h // 2, c, :, :].rearrange("p w n -> p (w n)"), True, True, *t_kT)
                v = bank[b][:].rearrange("p (i w n) -> p i w n", i=2, w=2)
                at, du = AT[:, s0:s0 + 3:2, :], dU[:, s0:s0 + 3:2, :]
                t1 = tt(DV, at, v[:, :, 0, :], at, ALU.mult, t, t_dS)
                t_at = tt(DV, du, v[:, :, 1, :], du, ALU.mult, t, t_dU, t_dS)
                free[b] = [t_at]
                t_AT.append(t1)
            t_att = t_at
            t_A = tt(DV, AT[:], AT[:], rep(ident[:], 16), ALU.add, *t_AT)
            t_XT = tt(DV, XT, AT[:], rep(m1T, 16), ALU.mult, t_A, w_in_read)

            prev = []
            ready_c = [None] * 8
            tT = [load_T(0), load_T(1)]
            tP, tPV = [None] * 8, [None] * 8
            o_bank = None
            for h in range(8):
                j, p0, pp = h // 2, 64 * (h % 2), h % 2
                b = work()
                PE.wait(*free[b])
                t_bias = mm(bank[b][:, 0:384], flip[:], T[:, pp, :], True, False, tT[h], t_flip)
                mm(bank[b][:, 0:128], qT[p0:p0 + 64, j, 0:128], kTa[p0:p0 + 64, j, 0:128], False, False, *t_qk,
                   tok=False)
                t = mm(bank[b][:, 128:384], qT[p0:p0 + 64, j, 128:256], kTa[p0:p0 + 64, j, :], False, True)
                dep = [tP[h - 2]] if h >= 2 else []
                if h < 6:
                    tT.append(load_T(h + 2, t_bias))
                nm = gs[:, 168 + 4 * pp:170 + 4 * pp]
                sm_ = gs[:, 170 + 4 * pp:172 + 4 * pp]
                parts = ((0, 128), (128, 384))
                te = []
                for i, (lo, hi) in enumerate(parts):
                    t2 = DV.op(lambda e, i=i, lo=lo, hi=hi, nm=nm, b=b: e.tensor_reduce(
                        nm[:, i:i + 1], bank[b][:, lo:hi], AXX, ALU.max), t, *dep)
                tm_ = ts(DV, nm, nm, -1.0, None, ALU.mult, None, t2)
                for i, (lo, hi) in enumerate(parts):
                    te.append(act(P[:, pp, lo:hi], bank[b][:, lo:hi], ACT.Exp, tm_, *dep, bias=nm[:, i:i + 1],
                                  accum_out=sm_[:, i:i + 1]))
                free[b] = [te[-1]]
                t2 = DV.op(lambda e, sm_=sm_: e.reciprocal(sm_, sm_), *te)
                tn = [ts(DV, P[:, pp, lo:hi], P[:, pp, lo:hi], sm_[:, i:i + 1], None, ALU.mult, None, t2)
                      for i, (lo, hi) in enumerate(parts)]
                b = work()
                PE.wait(*free[b])
                for i in range(3):
                    t = tr(bank[b][:, i * 128:i * 128 + 128], P[:, pp, i * 128:i * 128 + 128], *tn)
                tP[h] = t
                dep = [tPV[h - 2]] if h >= 2 else []
                t = move(AC, PT[:, pp, 0:128], bank[b][:, 0:128], t, *dep)
                t = move(AC, PT[:, pp, 128:384], bank[b][:, 128:384], *dep)
                free[b] = [t]
                if pp == 0:
                    o_bank = work()
                    PE.wait(*free[o_bank])
                b = o_bank
                vs = va[:, :, h * 64:h * 64 + 64]
                mm(bank[b][p0:p0 + 64, 0:256], vs[:, 0, :], PT[:, pp, 0:256], True, False, t, *t_v, tok=False)
                tPV[h] = mm(bank[b][p0:p0 + 64, 128:256], vs[:, 1, :], PT[:, pp, 256:384], False, True)
                if pp == 1:
                    th = AC.op(lambda e, j=j, b=b: e.copy(hh[:, j, :], bank[b][:, 0:256]), tPV[h], w_in_read)
                    tl = tt(DV, hl[:, j, :], bank[b][:, 0:256], hh[:, j, :].bitcast(F32), ALU.subtract, th, w_in_read)
                    free[b] = [tl]
                    ready_c[j] = [th, tl]
            att_done = [PE.now(), AC.now(), DV.now()]
            pa.close()
            Ub = sb(p1, "Ub", [128, 16, 128])
            vn = sb(p1, "vn", [128, 512])
            S1 = sb(p1, "S1", [128, 256])
            wbc = sb(p1, "wbc", [128, D])
            t_wbc = load(wbc[:], A["post_mix"].partition_broadcast(128), *att_done)
            DV.wait(*att_done)
            AC.wait(*att_done)

            t_X = []
            t_XTg = [t_XT] * 4
            for g in range(4):
                b = g
                PE.wait(*free[b])
                for i in range(4):
                    t = tr(bank[b][:, i * 128:i * 128 + 128], XT[:, 4 * g + i, :], t_XT)
                t = move(AC, X[:, 4 * g:4 * g + 4, :], bank[b][:].rearrange("p (a n) -> p a n", a=4), t, *t_sq,
                         *t_n)
                free[b] = [t]
                t_X.append(t)
            for l, s_ in enumerate(LEVELS):
                mask = tab[:, 4 + l, :]
                tu = []
                for g in range(4):
                    b = g
                    PE.wait(*free[b])
                    for i in range(4):
                        s = 4 * g + i
                        t = mm(bank[b][:, i * 128:i * 128 + 128], AT[:, s, :], X[:, s, :], True, True, t_X[g], t_A,
                               t_XTg[g])
                    t = tt(DV, Ub[:, 4 * g:4 * g + 4, :], bank[b][:].rearrange("p (a n) -> p a n", a=4), rep(mask, 4),
                           ALU.mult, t)
                    free[b] = [t]
                    tu.append(t)
                for g in range(4):
                    bx = work() if l < 5 else None
                    by = work()
                    if l < 5:
                        PE.wait(*free[bx])
                        for i in range(4):
                            s = 4 * g + i
                            t1 = mm(bank[bx][:, i * 128:i * 128 + 128], XT[:, s, :], Ub[:, s, :], True, True, tu[g])
                    PE.wait(*free[by])
                    for i in range(4):
                        s = 4 * g + i
                        t2 = mm(bank[by][:, i * 128:i * 128 + 128], Ub[:, s, :], XT[:, s, :], True, True, tu[g])
                    if l < 5:
                        t_X[g] = move(AC, X[:, 4 * g:4 * g + 4, :], bank[bx][:].rearrange("p (a n) -> p a n", a=4),
                                      t1)
                        free[bx] = [t_X[g]]
                    t_XTg[g] = move(AC, XT[:, 4 * g:4 * g + 4, :], bank[by][:].rearrange("p (a n) -> p a n", a=4),
                                    t2)
                    free[by] = [t_XTg[g]]

            ob = X[:].rearrange("p s n -> p (s n)")
            o_all = ob[:, 0:1024].rearrange("p (c n) -> p c n", c=2)
            qs = ob[:, 1024:1536]
            r1 = ob[:, 1536:2048]
            b = work()
            PE.wait(*free[b])
            for h in range(8):
                t = mm(bank[b][:, h * 64:h * 64 + 64], XT[:, h, :], tm[:, 0, 1024 + h * 64:1024 + h * 64 + 64],
                       True, True, *t_XTg, *t_vb)
            t = move(AC, vn[:], bank[b][:], t)
            free[b] = [t]
            t_v0 = t
            b = work()
            PE.wait(*free[b])
            for h in range(8):
                p0 = 64 * (h % 2)
                t = mm(bank[b][p0:p0 + 64, (h // 2) * 64:(h // 2) * 64 + 64], kd[:, h * 64:h * 64 + 64],
                       vn[:, h * 64:h * 64 + 64], True, True, t_v0, t_kd)
            t_s1 = move(AC, S1[:], bank[b][:, 0:256], t)
            free[b] = [t_s1]
            bo = work()
            PE.wait(*free[bo])
            for h in range(8):
                t_o0 = mm(bank[bo][:, h * 64:h * 64 + 64], dU[:, h, :], vn[:, h * 64:h * 64 + 64], True, True, t_att)
            t_oa = [move(DV, o_all[:, 0, :], bank[bo][:], t_o0)]
            free[bo] = [t_oa[0]]
            v64 = lambda a: a.rearrange("p (h n) -> p h n", n=64)
            pair = lambda a, w: v64(a).rearrange("p (j w) n -> p j w n", w=2)[:, :, w, :]
            eg1 = eg[:, 8:16].rearrange("p (j w) -> p j w", w=2)
            t_qs, t_rr = [], []
            for which, dst, acc_ in ((0, r1, t_rr), (1, qs, t_qs)):
                for w_ in range(2):
                    b = work()
                    PE.wait(*free[b])
                    p0 = 64 * w_
                    for j in range(4):
                        t = mm(bank[b][:, j * 64:j * 64 + 64], kq[p0:p0 + 64, j, 1, which, :],
                               S1[p0:p0 + 64, j * 64:j * 64 + 64], True, True, t_s1)
                    t = tt(DV, pair(dst, w_), v64(bank[b][:, 0:256]), bc(eg1[:, :, w_], 64), ALU.mult, t, t_eg)
                    free[b] = [t]
                    acc_.append(t)
                if which == 0:
                    t_r1 = tt(DV, r1, tm[:, 1, 1024:1536], r1, ALU.subtract, *t_rr, *t_vb)
            b = work()
            PE.wait(*free[b])
            for h in range(8):
                t = mm(bank[b][:, h * 64:h * 64 + 64], XT[:, 8 + h, :], r1[:, h * 64:h * 64 + 64], True, True, t_r1)
            t_v1 = move(AC, vn[:], bank[b][:], t, t_o0)
            free[b] = [t_v1]
            b = work()
            PE.wait(*free[b])
            for h in range(8):
                t = mm(bank[b][:, h * 64:h * 64 + 64], dU[:, 8 + h, :], vn[:, h * 64:h * 64 + 64], True, True, t_v1)
            t_oa.append(tt(DV, o_all[:, 1, :], bank[b][:], qs, ALU.add, t, *t_qs))
            free[b] = [t_oa[1]]

            acc = [[0, 1], [2, 3]]
            a_unit("A", H, ready_c, (0, 1), acc, True, False)
            a_unit("A", H, ready_c, (2, 3), acc, False, False)

            so = gs[:, 176:192]
            osq = Ub[:, 0:8, :].rearrange("p s n -> p (s n)")
            oflat = ob[:, 0:1024]
            t = act(osq, oflat, ACT.Square, *t_oa, scale=0.125)
            t = DV.op(lambda e: e.tensor_reduce(so, osq.rearrange("p (s n) -> p s n", n=64), AXX, ALU.add), t)
            t = ts(DV, so, so, EPS, None, ALU.add, None, t)
            t = act(so, so, ACT.Sqrt, t)
            t = DV.op(lambda e: e.reciprocal(so, so), t)
            t = tt(DV, v64(oflat), v64(oflat), bc(so, 64), ALU.mult, t)
            t = tt(DV, oflat, oflat, zz.rearrange("p c n -> p (c n)"), ALU.mult, t, *zw)
            for p in range(2):
                b = work()
                PE.wait(*free[b])
                for kk in range(2):
                    for c in range(2):
                        a = 2 * p + kk
                        t2 = tr(bank[b][:, kk * S + c * 128:kk * S + c * 128 + 128],
                                o_all[:, c, a * 128:a * 128 + 128], t)
                k = 4 + 2 * p
                v = bank[b][:].rearrange("p (a s) -> p a s", a=2)
                th = AC.op(lambda e, k=k, v=v: e.copy(hh[:, k:k + 2, :], v), t2, w_in_read)
                tl = tt(DV, hl[:, k:k + 2, :], v, hh[:, k:k + 2, :].bitcast(F32), ALU.subtract, th)
                free[b] = [tl]
                ready_c[k] = ready_c[k + 1] = [th, tl]
            a_unit("A", H, ready_c, (4, 5), acc, False, False)
            t = a_unit("A", H, ready_c, (6, 7), acc, False, True)
            t_x1 = post_norm(wbc, t_wbc, t)

        phase = [PE.now(), AC.now(), DV.now(), PO.now()]
        with ExitStack() as p2:
            wbc = sb(p2, "wbc2", [128, D])
            rl = sb(p2, "rl", [128, 2, 512])
            sqb = sb(p2, "sqb", [128, 2, 512])
            mh = sb(p2, "mh", [128, 4, S], FR)
            ml = sb(p2, "ml", [128, 4, S], FR)
            t_wbc = load(wbc[:], A["post_mlp"].partition_broadcast(128), *phase)
            ready = norm_split(par("pre_mlp"), H, [PE.now()], *t_x1)
            mready = [None] * 32
            down = {}
            AC.wait(*phase)
            DV.wait(*phase)

            def mlp_down(i):
                m = (mh[:, 2 * (i % 2):2 * (i % 2) + 2, :], ml[:, 2 * (i % 2):2 * (i % 2) + 2, :])
                down[i] = a_unit("A", m, mready[2 * i:2 * i + 2], (0, 1), acc, i == 0, i == 15)

            for i in range(16):
                b, t = b_unit(H, ready)
                q = i % 2
                dep = [down[i - 2]] if i >= 2 else []
                r_, s_ = rl[:, q, :], sqb[:, q, :]
                ho = mh[:, 2 * q:2 * q + 2, :].rearrange("p a s -> p (a s)")
                lo = ml[:, 2 * q:2 * q + 2, :].rearrange("p a s -> p (a s)")
                t1 = act(r_, bank[b][:], ACT.Relu, t, *([mready[2 * i - 4][0], mready[2 * i - 4][1]] if i >= 2 else []))
                free[b] = [t1]
                t2 = act(ho, r_, ACT.Square, t1, *dep)
                t3 = tt(DV, s_, r_, r_, ALU.mult, t1)
                t4 = tt(DV, lo, s_, ho.bitcast(F32), ALU.subtract, t2, t3, *dep)
                mready[2 * i] = mready[2 * i + 1] = [t2, t4]
                if i >= 1:
                    mlp_down(i - 1)
            mlp_down(15)
            t_x2 = post_norm(wbc, t_wbc, down[15])

        phase = [PE.now(), AC.now(), DV.now(), PO.now()]
        with ExitStack() as p3:
            ya = sb(p3, "ya", [128, 2, D])
            Dm = sb(p3, "Dm", [128, 4, 512])
            qr = sb(p3, "qr", [128, 8, S])
            kr = sb(p3, "kr", [128, 8, S])
            pc = ExitStack()
            yh = sb(pc, "yh", [128, 8, S], FR)
            yl = sb(pc, "yl", [128, 8, S], FR)
            uc = sb(pc, "uc", [128, 2, 2, S + 2])
            gcv = sb(pc, "gcv", [128, 2, 2, S])
            cv = sb(pc, "cv", [128, 2, 2, S])
            dist = sb(pc, "dist", [128, 2, 512])
            rope = sb(pc, "rope", [128, 2, S])
            ra = sb(pc, "ra", [128, 2, 512])
            t_dist = load(dist[:], A["dist"].rearrange("p (a n) -> p a n", a=2), *phase)
            t_rope = load(rope[:], A["rope"].rearrange("p (a n) -> p a n", a=2), *phase)
            ready = norm_split(par("g_mix"), H, [PE.now()], *t_x2)
            AC.wait(*phase)
            DV.wait(*phase)
            PO.wait(*phase)

            lg = st[:, 16:24]
            sp_ = st[:, 24:32]
            dec = small[:, SM["dec_f"][0]:SM["dec_f"][0] + 8]
            t1 = ts(DV, lg, dec, -1.0, None, ALU.mult, None, t_small)
            t2 = stt(sp_, lg, -1.0, lg, ALU.mult, ALU.min, t1)
            t2 = act(sp_, sp_, ACT.Exp, t2)
            t2 = act(sp_, sp_, ACT.Ln, t2, bias=1.0)
            t2 = stt(sp_, lg, 0.0, sp_, ALU.max, ALU.add, t2)
            t2 = ts(DV, lg, sp_, -1.0, None, ALU.mult, None, t2)
            t_D = []
            for h in range(4):
                t = ts(DV, Dm[:, h, :], dist[:, 0, :], lg[:, h:h + 1], None, ALU.mult, None, t2, t_dist)
                t = stt(Dm[:, h, :], dist[:, 1, :], lg[:, 4 + h:5 + h], Dm[:, h, :], ALU.mult, ALU.add, t)
                t_D.append(t)
            t_D = act(Dm[:], Dm[:], ACT.Exp, *t_D)

            t_z = PO.op(lambda e: e.memset(uc[:], 0.0))
            cw = par("conv2").rearrange("p (a k) -> p a k", k=3)
            yready = []
            last = [[], []]
            for i in range(4):
                q = i % 2
                b, t = b_unit(H, ready)
                v = bank[b][:].rearrange("p (a s) -> p a s", a=2)
                t_xc = move(AC, gcv[:, q], v, t, *last[q])
                free[b] = [t_xc]
                b, t = b_unit(H, ready)
                v = bank[b][:].rearrange("p (a s) -> p a s", a=2)
                t_u = tt(DV, uc[:, q, :, 1:S + 1], v, gcv[:, q], ALU.mult, t, t_xc, t_z, *last[q])
                free[b] = [t_u]
                t_cv = []
                for a in range(2):
                    w_ = cw[:, 2 * i + a, :]
                    t2 = ts(DV, cv[:, q, a, :], uc[:, q, a, 0:S], w_[:, 0:1], None, ALU.mult, None, t_u, *last[q])
                    for k in (1, 2):
                        t2 = stt(cv[:, q, a, :], uc[:, q, a, k:k + S], w_[:, k:k + 1], cv[:, q, a, :],
                                 ALU.mult, ALU.add, t2)
                    t_cv.append(t2)
                b, t = b_unit(H, ready)
                v = bank[b][:].rearrange("p (a s) -> p a s", a=2)
                t = tt(DV, cv[:, q], cv[:, q], v, ALU.mult, t, *t_cv)
                free[b] = [t]
                th = AC.op(lambda e, i=i, q=q: e.copy(yh[:, 2 * i:2 * i + 2, :], cv[:, q]), t)
                tl = tt(DV, yl[:, 2 * i:2 * i + 2, :], cv[:, q], yh[:, 2 * i:2 * i + 2, :].bitcast(F32), ALU.subtract,
                        th)
                yready += [[th, tl]] * 2
                last[q] = [tl]

            t_P = []
            rdep = []
            for h in range(4):
                tk = []
                for w_, dst in enumerate((qr, kr)):
                    b, t = b_unit(H, ready)
                    v = bank[b][:].rearrange("p (a s) -> p a s", a=2)
                    c_, s_ = (rep(rope[:, n, :], 2) for n in range(2))
                    va_ = ra[:, 0, :].rearrange("p (a s) -> p a s", a=2)
                    vb_ = ra[:, 1, :].rearrange("p (a s) -> p a s", a=2)
                    t1 = tt(DV, va_, v, c_, ALU.mult, t, t_rope, *rdep)
                    t2 = tt(DV, vb_, v, s_, ALU.mult, t, *rdep)
                    free[b] = [t2]
                    t3 = tt(PO, dst[:, 2 * h, :], va_[:, 0], vb_[:, 1], ALU.subtract, t1, t2)
                    t4 = tt(PO, dst[:, 2 * h + 1, :], va_[:, 1], vb_[:, 0], ALU.add, t1, t2)
                    rdep = [t3, t4]
                    tk += rdep
                b = work()
                PE.wait(*free[b])
                for m in range(2):
                    for dk in range(2):
                        t = mm(bank[b][:, m * S:m * S + S], kr[:, 2 * h + dk, m * 128:m * 128 + 128],
                               qr[:, 2 * h + dk, :], dk == 0, dk == 1, *tk)
                t = stt(Dm[:, h, :], bank[b][:], 1.0 / 16, Dm[:, h, :], ALU.mult, ALU.mult, t, t_D)
                free[b] = [t]
                t_P.append(t)

            Y = (yh, yl)
            for k in range(4):
                t = a_unit("A", Y, yready, (2 * k, 2 * k + 1), acc, k == 0, k == 3)
            t_ya = []
            for tok in range(2):
                for c in range(2):
                    t2 = move(AC, ya[:, tok, c * 512:c * 512 + 512], bank[2 * tok + c][:], t)
                    free[2 * tok + c] = [t2]
                    t_ya.append(t2)

            conv_done = [PE.now(), AC.now(), DV.now(), PO.now()]
            pc.close()
            vv = sb(p3, "vv", [128, 2, 512])
            gt = sb(p3, "gt", [128, 4, S])
            rt = sb(p3, "rt", [128, 2, 512])
            ry = sb(p3, "ry", [128, 4, S])
            rh = sb(p3, "rh", [128, 4, S], FR)
            rlo = sb(p3, "rlo", [128, 4, S], FR)
            sg = sb(p3, "sg", [128, 2, 512])
            bn = sb(p3, "bn", [128, 2, 8])
            AC.wait(*conv_done)
            DV.wait(*conv_done)
            PO.wait(*conv_done)

            def gate_block(cb, dst, deps):
                b0, b1, t = c_block(H, ready)
                o = []
                for c, b in enumerate((b0, b1)):
                    t1 = act(sg[:, c, :], bank[b][:], ACT.Sigmoid, t, *deps)
                    free[b] = [t1]
                    d = dst[:, c, cb * 512:cb * 512 + 512]
                    o.append((t1, d, c))
                return o

            t_sg = []
            for cb in range(2):
                n = []
                for t1, d, c in gate_block(cb, ya, t_sg):
                    n.append(tt(DV, d, d, sg[:, c, :], ALU.mult, t1, *t_ya))
                t_sg = n
                t_ya = t_ya + n

            gw = par("g_ret")
            rr = [None] * 16
            t_tr, t_w, t_rt = [], None, []
            sgr = xt
            t_g2 = []
            for h in range(5):
                if h < 4:
                    b0, b1, t = c_block(H, ready)
                    tv = []
                    for c, b in enumerate((b0, b1)):
                        tv.append(move(AC, vv[:, c, :], bank[b][:], t, *([t_rv] if h else [])))
                        free[b] = [tv[-1]]
                    rb_ = [work(), work()]
                    trn = []
                    for n in range(2):
                        b = rb_[n]
                        PE.wait(*free[b])
                        for m in range(2):
                            t_rv = mm(bank[b][:], Dm[:, h, m * S + n * 128:m * S + n * 128 + 128], vv[:, m, :],
                                      m == 0, m == 1, t_P[h], *tv)
                        t = DV.op(lambda e, n=n, b=b: e.bn_stats(bn[:, n, 0:6], bank[b][:]), t_rv)
                        t = DV.op(lambda e, n=n: e.bn_aggr(st[:, 40 + 2 * n:42 + 2 * n], bn[:, n, 0:6]), t, *t_rt)
                        trn.append(t)
                    mv = st[:, 40:44].rearrange("p (n w) -> p n w", w=2)
                    rs = st[:, 44:46]
                    t = move(DV, rs, mv[:, :, 1], *trn)
                    t = rsqrt2(rs, t)
                    t_rt = []
                    for n in range(2):
                        b = rb_[n]
                        t2 = ts(DV, rt[:, n, :], bank[b][:], mv[:, n, 0:1], rs[:, n:n + 1], ALU.subtract, ALU.mult,
                                t, *t_tr)
                        free[b] = [t2]
                        t_rt.append(t2)
                    tg = []
                    for u in range(2):
                        b, t = b_unit(H, ready)
                        v = bank[b][:].rearrange("p (a s) -> p a s", a=2)
                        t = act(gt[:, 2 * u:2 * u + 2, :], v, ACT.Silu, t, *([ry_done] if h else []))
                        free[b] = [t]
                        for a in range(2 * u, 2 * u + 2):
                            tg.append(ts(PO, gt[:, a, :], gt[:, a, :], gw[:, 4 * h + a:4 * h + a + 1], None,
                                         ALU.mult, None, t))
                if h >= 1:
                    R = (rh, rlo)
                    a_unit("A", R, rr, (0, 1), acc, h == 1, False)
                    t_w = a_unit("A", R, rr, (2, 3), acc, False, h == 4)
                if h < 4:
                    for u in range(2):
                        b = work()
                        PE.wait(*free[b])
                        for a in range(2):
                            for n in range(2):
                                t = tr(bank[b][:, a * S + n * 128:a * S + n * 128 + 128],
                                       rt[:, n, (2 * u + a) * 128:(2 * u + a) * 128 + 128], *t_rt)
                        v = bank[b][:].rearrange("p (a s) -> p a s", a=2)
                        dep = [t_w] if h else []
                        t1 = tt(DV, ry[:, 2 * u:2 * u + 2, :], v, gt[:, 2 * u:2 * u + 2, :], ALU.mult, t, *tg)
                        free[b] = [t1]
                        th = AC.op(lambda e, u=u: e.copy(rh[:, 2 * u:2 * u + 2, :], ry[:, 2 * u:2 * u + 2, :]),
                                   t1, *dep)
                        tl = tt(DV, rlo[:, 2 * u:2 * u + 2, :], ry[:, 2 * u:2 * u + 2, :],
                                rh[:, 2 * u:2 * u + 2, :].bitcast(F32), ALU.subtract, t1, th, *dep)
                        rr[2 * u] = rr[2 * u + 1] = [th, tl]
                        ry_done = tl
                    t_tr = [t]
                if h == 3:
                    for cb in range(2):
                        b0, b1, t = c_block(H, ready)
                        for c, b in enumerate((b0, b1)):
                            t1 = act(sgr[:, c, cb * 512:cb * 512 + 512], bank[b][:], ACT.Sigmoid, t)
                            free[b] = [t1]
                            t_g2.append(t1)

            w_in2_read = PE.now()
            t_m = []
            for tok in range(2):
                for c in range(2):
                    d = sgr[:, tok, c * 512:c * 512 + 512]
                    t = tt(DV, d, d, bank[2 * tok + c][:], ALU.mult, t_w, *t_g2)
                    free[2 * tok + c] = [t]
                t = tt(DV, sgr[:, tok, :], sgr[:, tok, :], ya[:, tok, :], ALU.add, t, *t_ya)
                t_m.append(t)
            mr = []
            for p in range(4):
                b = work()
                PE.wait(*free[b])
                for kk in range(2):
                    for tok in range(2):
                        k = 2 * p + kk
                        t = tr(bank[b][:, kk * S + tok * 128:kk * S + tok * 128 + 128],
                               sgr[:, tok, k * 128:k * 128 + 128], t_m[tok])
                v = bank[b][:].rearrange("p (a s) -> p a s", a=2)
                k = 2 * p
                th = AC.op(lambda e, k=k, v=v: e.copy(hh[:, k:k + 2, :], v), t, w_in2_read)
                tl = tt(DV, hl[:, k:k + 2, :], v, hh[:, k:k + 2, :].bitcast(F32), ALU.subtract, th)
                free[b] = [tl]
                mr += [[th, tl]] * 2
            for k in range(4):
                t = a_unit("A", H, mr, (2 * k, 2 * k + 1), acc, k == 0, k == 3)
            t_x3 = []
            for tok in range(2):
                for c in range(2):
                    d = x[:, tok, c * 512:c * 512 + 512]
                    t2 = tt(DV, d, d, bank[2 * tok + c][:], ALU.add, t)
                    free[2 * tok + c] = [t2]
                    t_x3.append(t2)

        phase = [PE.now(), AC.now(), DV.now(), PO.now()]
        with ExitStack() as p4:
            wbc = sb(p4, "wbc4", [128, D])
            gl = sb(p4, "gl", [128, 2, 512])
            fh = sb(p4, "fh", [128, 4, S], FR)
            fl = sb(p4, "fl", [128, 4, S], FR)
            t_wbc = load(wbc[:], A["g_final"].partition_broadcast(128), *phase)
            ready = norm_split(par("g_ffn"), H, [PE.now()], *t_x3)
            AC.wait(*phase)
            DV.wait(*phase)
            fready = [None] * 22
            fdown = {}

            def ff_down(i):
                m = (fh[:, 2 * (i % 2):2 * (i % 2) + 2, :], fl[:, 2 * (i % 2):2 * (i % 2) + 2, :])
                fdown[i] = a_unit("A", m, fready[2 * i:2 * i + 2], (0, 1), acc, i == 0, i == 10)

            for i in range(11):
                q = i % 2
                bg, tg = b_unit(H, ready)
                t1 = act(gl[:, q, :], bank[bg][:], ACT.Silu, tg,
                         *([fready[2 * i - 4][0], fready[2 * i - 4][1]] if i >= 2 else []))
                free[bg] = [t1]
                bu, tu = b_unit(H, ready)
                t2 = tt(DV, gl[:, q, :], gl[:, q, :], bank[bu][:], ALU.mult, tu, t1)
                free[bu] = [t2]
                dep = [fdown[i - 2]] if i >= 2 else []
                ho = fh[:, 2 * q:2 * q + 2, :].rearrange("p a s -> p (a s)")
                lo = fl[:, 2 * q:2 * q + 2, :].rearrange("p a s -> p (a s)")
                t3 = AC.op(lambda e, ho=ho, q=q: e.copy(ho, gl[:, q, :]), t2, *dep)
                t4 = tt(DV, lo, gl[:, q, :], ho.bitcast(F32), ALU.subtract, t2, t3, *dep)
                fready[2 * i] = fready[2 * i + 1] = [t3, t4]
                if i >= 1:
                    ff_down(i - 1)
            ff_down(10)
            t = fdown[10]
            ms = st[:, 0:2]
            t_o = []
            for tok in range(2):
                tx = []
                for c in range(2):
                    d = x[:, tok, c * 512:c * 512 + 512]
                    tx.append(tt(DV, d, d, bank[2 * tok + c][:], ALU.add, t))
                t2 = act(xt[:, tok, :], x[:, tok, :], ACT.Square, *tx, scale=1.0 / 32, accum_out=ms[:, tok:tok + 1])
                t_o.append(t2)
            r = rsqrt2(ms, *t_o)
            s_out = sem("s_out")
            for tok in range(2):
                t = stt(xt[:, tok, :], x[:, tok, :], ms[:, tok:tok + 1], wbc[:], ALU.mult, ALU.mult, r, t_wbc)
                SP.quiet(lambda e, tok=tok: e.dma_start(out[tok * 128:tok * 128 + 128, :], xt[:, tok, :]).then_inc(
                    s_out, 16), t)
            SP.wait((s_out, 32))

        assert len(used) == len(PLAN)
        block = top.enter_context(nc.Block())

        @block.sync
        def _(e):
            for f in SP.queue:
                f(e)

        @block.gpsimd
        def _(e):
            for f in PO.queue:
                f(e)

        @block.scalar
        def _(e):
            for f in AC.queue:
                f(e)

        @block.vector
        def _(e):
            for f in DV.queue:
                f(e)

        @block.tensor
        def _(e):
            for f in PE.queue:
                f(e)


def kernel(**inputs):
    import concourse.bacc as bacc
    from concourse.bass_utils import run_bass_kernel_spmd as run

    g = {k: np.asarray(v) for k, v in inputs.items()}
    W = np.empty((len(PLAN), 128, U), np.float32)
    for i, u in enumerate(PLAN):
        w = g[u[1]][0]
        if u[0] == "B":
            W[i] = w[:, u[2]:u[2] + 256].reshape(8, 128, 256).transpose(1, 0, 2).reshape(128, U)
        elif u[0] == "Z":
            W[i, :, 0:1024] = w[:, u[2]:u[2] + 128].reshape(8, 128, 128).transpose(1, 0, 2).reshape(128, 1024)
            W[i, :, 1024:] = 0
        elif u[0] == "C":
            W[i] = w[128 * u[3]:128 * u[3] + 512, u[2]:u[2] + 512].reshape(4, 128, 512).transpose(1, 0, 2).reshape(128, U)
        else:
            W[i] = w[128 * u[2]:128 * u[2] + 256, :].reshape(2, 128, 1024).transpose(1, 0, 2).reshape(128, U)
    small = np.empty((128, NSM), np.float32)

    def put(name, a):
        small[:, SM[name][0]:SM[name][0] + SM[name][1]] = a

    for name, key in (("pre_mix", "pre_mix_norm"), ("pre_mlp", "pre_mlp_norm"), ("g_mix", "g_mix_2"),
                      ("g_ffn", "g_ffn_2"), ("g_ret", "g_ret_2")):
        put(name, g[key][0].reshape(-1, 128).T)
    put("conv1", g["conv_w"][0].reshape(4, 12, 128).transpose(2, 1, 0).reshape(128, 48))
    put("conv2", g["w_conv_2"][0].reshape(3, 8, 128).transpose(2, 1, 0).reshape(128, 24))
    for name, key in (("A_log", "A_log"), ("dt_bias", "dt_bias"), ("dec_f", "dec_f_2"), ("dec_b", "dec_b_2"),
                      ("gdn_w", "gdn_norm_w")):
        put(name, np.broadcast_to(g[key][0], (128, SM[name][1])))
    onehot, neg = table_onehot()
    arrays = {
        "W": W, "x": np.ascontiguousarray(g["x"][0]), "small": small, "ident": np.eye(128, dtype=np.float32),
        "flip": np.ascontiguousarray(np.eye(128, dtype=np.float32)[::-1]),
        "tab": table_gdn(), "onehot": onehot, "neg": neg, "rbT": np.ascontiguousarray(g["rel_bias"].T),
        "dist": table_dist(), "rope": table_rope(),
        "post_mix": np.ascontiguousarray(g["post_mix_norm"][0]),
        "post_mlp": np.ascontiguousarray(g["post_mlp_norm"][0]),
        "g_final": np.ascontiguousarray(g["g_final_2"]),
    }
    nc = bacc.Bacc("TRN2", target_bir_lowering=False, num_devices=1)
    A = {n: nc.dram_tensor("in_" + n, a.shape, F32, kind="ExternalInput").ap() for n, a in arrays.items()}
    A["scr"] = nc.dram_tensor("scr", [8, 384], F32, kind="Internal").ap()
    out = nc.dram_tensor("out_0", (S, D), F32, kind="ExternalOutput").ap()
    build(nc, A, out)
    r = run(nc, [{"in_" + n: a for n, a in arrays.items()}], core_ids=[0])
    return r.results[0]["out_0"].reshape(1, S, D)
```

```python
import math
from contextlib import ExitStack

import numpy as np

import concourse.bass as bass
from concourse import mybir

F32 = mybir.dt.float32
FR = mybir.dt.float32r
ALU = mybir.AluOpType
ACT = mybir.ActivationFunctionType
AXX = mybir.AxisListType.X
EPS = 1e-6

S = 256
D = 1024
RR = 3
HR = 4
AHEAD = 2
U = 2048
NEG = -1e30



def buckets():
    d = np.arange(256)
    large = 16 + (np.log(np.maximum(d, 1).astype(np.float32) / np.float32(16))
                  / np.float32(math.log(128 / 16)) * np.float32(16)).astype(np.int32)
    return np.where(d < 16, d, np.minimum(large, 31))


LEVELS = (2, 4, 8, 16, 32, 64)


def level_mask(s):
    i = np.arange(128)[:, None]
    j = np.arange(128)[None, :]
    low = (i // (2 * s) == j // (2 * s)) & (i // s % 2 == 1) & (j // s % 2 == 0)
    return (low | (i == j)).astype(np.float32)


def table_gdn():
    i = np.arange(128)[:, None]
    j = np.arange(128)[None, :]
    parts = [(i <= j).astype(np.float32), -(i < j).astype(np.float32), np.ones((128, 128), np.float32),
             level_mask(1).T] + [level_mask(s) for s in LEVELS]
    return np.ascontiguousarray(np.concatenate(parts, 1))


def table_onehot():
    t = np.zeros((32, 384), np.float32)
    m = np.zeros((8, 384), np.float32)
    b = buckets()
    for j in range(384):
        if 255 - j >= 0:
            t[b[255 - j], j] = 1.0
        else:
            m[:, j] = NEG
    return t, m


def table_rope():
    pos = np.arange(S, dtype=np.float32)
    freqs = (np.float32(10000.0) ** (-np.arange(0, 256, 2, dtype=np.float32) / np.float32(256))).astype(np.float32)
    ang = (freqs[:, None] * pos[None, :]).astype(np.float32).astype(np.float64)
    return np.ascontiguousarray(np.concatenate([np.cos(ang), np.sin(ang)], 1).astype(np.float32))


def table_dist():
    m = np.arange(128)[:, None, None] + 128 * np.arange(2)[None, :, None]
    n = np.arange(256)[None, None, :]
    a = np.maximum(n - m, 0).astype(np.float32).reshape(128, 512)
    b = np.maximum(m - n, 0).astype(np.float32).reshape(128, 512)
    return np.ascontiguousarray(np.concatenate([a, b], 1))


def plan():
    u = [("Z", "w_in", 3472)]
    u += [("B", "w_in", 1536 + 256 * i) for i in range(6)]
    u += [("B", "w_in", 256 * i) for i in range(4)]
    u += [("C", "w_in", 1024, k) for k in (0, 4)]
    u += [("C", "w_in", 3072, k) for k in (0, 4)]
    u += [("A", "w_out", 2 * k) for k in range(4)]
    for i in range(16):
        u.append(("B", "w_up", 256 * i))
        if i >= 1:
            u.append(("A", "w_down", 2 * (i - 1)))
    u.append(("A", "w_down", 30))
    for i in range(4):
        u += [("B", "w_in_2", 256 * i), ("B", "w_in_2", 2048 + 256 * i), ("B", "w_in_2", 1024 + 256 * i)]
    for i in range(4):
        u += [("B", "w_in_2", 3072 + 256 * i), ("B", "w_in_2", 4096 + 256 * i)]
        if i == 0:
            u += [("A", "w_a_out_2", 2 * k) for k in range(4)]
    for h in range(4):
        u += [("C", "w_in_2", 5120 + 512 * h, k) for k in (0, 4)]
        u += [("B", "w_in_2", 7168 + 512 * h), ("B", "w_in_2", 7168 + 512 * h + 256)]
        if h == 0:
            for cb in range(2):
                u += [("C", "w_in_2", 9216 + 512 * cb, k) for k in (0, 4)]
        else:
            u += [("A", "w_r_out_2", 4 * (h - 1)), ("A", "w_r_out_2", 4 * (h - 1) + 2)]
    u += [("C", "w_in_2", 10240, k) for k in (0, 4)]
    u += [("A", "w_r_out_2", 12), ("A", "w_r_out_2", 14)]
    u += [("C", "w_in_2", 10752, k) for k in (0, 4)]
    u += [("A", "w_o_2", 2 * k) for k in range(4)]
    for i in range(11):
        u += [("B", "w_ff_gate_2", 256 * i), ("B", "w_ff_up_2", 256 * i)]
        if i >= 1:
            u.append(("A", "w_ff_down_2", 2 * (i - 1)))
    u.append(("A", "w_ff_down_2", 20))
    return u


PLAN = plan()

SM = {}
_at = 0
for _n, _w in (("pre_mix", 8), ("pre_mlp", 8), ("g_mix", 8), ("g_ffn", 8), ("conv1", 48), ("conv2", 24),
               ("g_ret", 16), ("A_log", 8), ("dt_bias", 8), ("dec_f", 4), ("dec_b", 4), ("gdn_w", 64)):
    SM[_n] = (_at, _w)
    _at += _w
NSM = _at


class Engine:

    def __init__(self, sem):
        self.sem, self.count, self.queue, self.seen = sem, 0, [], {}

    def wait(self, *tokens):
        for sem, value in tokens:
            if self.seen.get(id(sem), 0) < value:
                self.seen[id(sem)] = value
                self.queue.append(lambda e, s=sem, v=value: e.wait_ge(s, v))

    def op(self, fn, *tokens):
        self.wait(*tokens)
        self.count += 1
        self.queue.append(lambda e: fn(e).then_inc(self.sem, 1))
        return self.sem, self.count

    def quiet(self, fn, *tokens):
        self.wait(*tokens)
        self.queue.append(fn)

    def now(self):
        return self.sem, self.count


def build(nc, A, out):
    with ExitStack() as top:
        nsem = [0]

        def sem(name):
            nsem[0] += 1
            return top.enter_context(nc.semaphore(name))

        def sb(stack, name, shape, dt=F32):
            return stack.enter_context(nc.sbuf_tensor("t_" + name, shape, dt))

        PE, AC, DV, PO, SP = (Engine(sem("s_" + n)) for n in ("pe", "act", "dve", "pool", "sp"))
        bank = [top.enter_context(nc.psum_tensor(f"bank{i}", [128, 512], F32)) for i in range(8)]
        free = [[] for _ in range(8)]
        turn = [0]

        def work():
            b = 4 + turn[0] % 4
            turn[0] += 1
            return b

        raw = sb(top, "raw", [128, RR, U])
        wh = sb(top, "wh", [128, HR, U], FR)
        wl = sb(top, "wl", [128, HR, U], FR)
        hh = sb(top, "hh", [128, 8, S], FR)
        hl = sb(top, "hl", [128, 8, S], FR)
        x = sb(top, "x", [128, 2, D])
        xt = sb(top, "xt", [128, 2, D])
        ident = sb(top, "ident", [128, 128])
        small = sb(top, "small", [128, NSM])
        st = sb(top, "st", [128, 128])
        half = sb(top, "half", [128, 2])

        def par(name):
            a, w = SM[name]
            return small[:, a:a + w]

        def load(dst, src, *tokens, via=None):
            s = sem(f"dma{nsem[0]}")
            (via or PO).quiet(lambda e: e.dma_start(dst, src).then_inc(s, 16), *tokens)
            return s, 16

        raw_sem = [sem(f"raw{i}") for i in range(RR)]
        split = []
        used = []

        def dma_unit(i):
            r = i % RR
            if i >= RR:
                SP.wait(*split[i - RR])
            if PLAN[i][0] == "Z":
                SP.quiet(lambda e: e.dma_start(raw[:, r, 0:1024], A["W"][i, :, 0:1024]).then_inc(raw_sem[r], 16))
            else:
                SP.quiet(lambda e: e.dma_start(raw[:, r, :], A["W"][i]).then_inc(raw_sem[r], 16))

        def prep(upto):
            while len(split) < min(upto + 1, len(PLAN)):
                i = len(split)
                if i >= RR:
                    dma_unit(i)
                r, h = i % RR, i % HR
                n = 1024 if PLAN[i][0] == "Z" else U
                arrived = (raw_sem[r], 16 * (i // RR + 1))
                freed = [used[i - HR]] if i >= HR else []
                t1 = AC.op(lambda e, h=h, r=r, n=n: e.copy(wh[:, h, 0:n], raw[:, r, 0:n]), arrived, *freed)
                t2 = DV.op(lambda e, h=h, r=r, n=n: e.tensor_tensor(wl[:, h, 0:n], raw[:, r, 0:n], wh[:, h, 0:n].bitcast(F32),
                                                     ALU.subtract), arrived, t1, *freed)
                split.append((t1, t2))

        def unit(kind):
            i = len(used)
            assert PLAN[i][0] == kind, (i, PLAN[i], kind)
            prep(i + AHEAD)
            PE.wait(*split[i])
            return i % HR

        def done(tok):
            used.append(tok)

        PASS = ((0, 0), (0, 1), (1, 0))

        def b_unit(act, ready, kind="B", k_outer=False):
            b = work()
            h = unit(kind)
            w = (wh, wl)
            nt = 1 if kind == "Z" else 2
            PE.wait(*free[b])
            if k_outer:
                order = [(c, k) for k in range(8) for c in range(nt)]
            else:
                order = [(c, k) for c in range(nt) for k in range(8)]
            for at, (c, k) in enumerate(order):
                PE.wait(*ready[k])
                for n, (i, j) in enumerate(PASS):
                    lhs = w[i][:, h, k * 128 * nt + c * 128:k * 128 * nt + c * 128 + 128]
                    rhs = act[j][:, k, :]
                    if k_outer:
                        first, last = at == 0 and n == 0, at == len(order) - 1 and n == 2
                    else:
                        first, last = k == 0 and n == 0, k == 7 and n == 2
                    f = (lambda e, o=bank[b][:, c * S:c * S + S], l=lhs, r=rhs, a=first, z=last:
                         e.matmul(o, l, r, start=a, stop=z, skip_group_check=k_outer))
                    if at == len(order) - 1 and n == 2:
                        tok = PE.op(f)
                    else:
                        PE.quiet(f)
            done(tok)
            return b, tok

        def a_unit(kind, act, ready, ks, outs, first, last, hook=None):
            h = unit(kind)
            w = (wh, wl)
            nk, ncb = len(ks), len(outs[0])
            if last:
                order = [(t, kk) for t in range(2) for kk in range(nk)]
            else:
                order = [(t, kk) for kk in range(nk) for t in range(2)]
            toks = [None, None]
            opened = set()
            for at, (t, kk) in enumerate(order):
                PE.wait(*ready[ks[kk]])
                if first and t not in opened:
                    opened.add(t)
                    for b in outs[t]:
                        PE.wait(*free[b])
                for n, (j, i) in enumerate(((0, 0), (0, 1), (1, 0))):
                    for c in range(ncb):
                        lhs = act[j][:, ks[kk], t * 128:t * 128 + 128]
                        rhs = w[i][:, h, kk * 512 * ncb + c * 512:kk * 512 * ncb + c * 512 + 512]
                        a = first and kk == 0 and n == 0
                        z = last and kk == nk - 1 and n == 2
                        f = (lambda e, o=bank[outs[t][c]][:], l=lhs, r=rhs, a=a, z=z:
                             e.matmul(o, l, r, start=a, stop=z))
                        if n == 2 and c == ncb - 1 and kk == nk - 1:
                            toks[t] = PE.op(f)
                        else:
                            PE.quiet(f)
                if hook and at == 1:
                    hook()
            done(toks[1])
            return toks

        def c_block(act, ready):
            outs = [[work()], [work()]]
            a_unit("C", act, ready, range(0, 4), outs, True, False)
            toks = a_unit("C", act, ready, range(4, 8), outs, False, True)
            return [(0, outs[0][0], toks[0]), (1, outs[1][0], toks[1])]

        ms = st[:, 0:2]
        mp = st[:, 2:4]
        part = st[:, 4:8]

        def pow_half(a, *tokens):
            return PO.op(lambda e: e.tensor_tensor(a, a, half[:, 0:1], ALU.pow), t_half, *tokens)

        def square_x(t, *tokens):
            return AC.op(lambda e: e.activation(xt[:, t, :], x[:, t, :], ACT.Square, scale=1.0 / 32,
                                                accum_out=ms[:, t:t + 1]), *tokens)

        def rstd_x(t, tok):
            a = DV.op(lambda e: e.tensor_scalar(ms[:, t:t + 1], ms[:, t:t + 1], EPS, None, ALU.add), tok)
            return pow_half(ms[:, t:t + 1], a)

        def scale_x(t, tok):
            return DV.op(lambda e: e.tensor_scalar(xt[:, t, :], x[:, t, :], ms[:, t:t + 1], None, ALU.mult), tok)

        def turn_x(w, dst, prior, xn):
            ready = []
            for p in range(4):
                b = work()
                PE.wait(*free[b])
                for t in range(2):
                    for kk in range(2):
                        k = 2 * p + kk
                        f = (lambda e, kk=kk, k=k, t=t, b=b: e.transpose(
                            bank[b][:, kk * S + t * 128:kk * S + t * 128 + 128], xt[:, t, k * 128:k * 128 + 128],
                            ident[:]))
                        if kk == 1 and t == 1:
                            tok = PE.op(f, t_id, xn[t])
                        else:
                            PE.quiet(f, t_id, xn[t])
                his = []
                for kk in range(2):
                    k = 2 * p + kk
                    his.append(AC.op(lambda e, kk=kk, k=k, b=b: e.activation(
                        dst[0][:, k, :], bank[b][:, kk * S:kk * S + S], ACT.Copy, scale=w[:, k:k + 1]),
                        tok, t_small, *prior))
                for kk in range(2):
                    k = 2 * p + kk
                    lo = DV.op(lambda e, kk=kk, k=k, b=b: e.scalar_tensor_tensor(
                        out=dst[1][:, k, :], in0=bank[b][:, kk * S:kk * S + S], scalar=w[:, k:k + 1],
                        in1=dst[0][:, k, :].bitcast(F32), op0=ALU.mult, op1=ALU.subtract), his[1], t_small, *prior)
                    ready.append([his[kk], lo])
                free[b] = [lo]
            return ready

        def post_rstd(t, tok):
            q = [AC.op(lambda e, c=c: e.activation(
                xt[:, t, c * 512:c * 512 + 512], bank[2 * t + c][:], ACT.Square, scale=1.0 / 32,
                accum_out=part[:, 2 * t + c:2 * t + c + 1]), tok) for c in range(2)]
            return q

        def post_pow(t, q):
            a = DV.op(lambda e: e.scalar_tensor_tensor(out=mp[:, t:t + 1], in0=part[:, 2 * t:2 * t + 1], scalar=EPS,
                                                       in1=part[:, 2 * t + 1:2 * t + 2], op0=ALU.add, op1=ALU.add), *q)
            return pow_half(mp[:, t:t + 1], a)

        def post_scale(t, r, q, wbc, t_w):
            for c in range(2):
                m = DV.op(lambda e, c=c: e.scalar_tensor_tensor(
                    out=xt[:, t, c * 512:c * 512 + 512], in0=bank[2 * t + c][:], scalar=mp[:, t:t + 1],
                    in1=wbc[:, c * 512:c * 512 + 512], op0=ALU.mult, op1=ALU.mult), r, t_w, *q)
                free[2 * t + c] = [m]
            return m

        def post_add(t, m):
            return DV.op(lambda e: e.tensor_tensor(x[:, t, :], x[:, t, :], xt[:, t, :], ALU.add), m)

        def between(toks, wbc, t_w, w, dst):
            q0 = post_rstd(0, toks[0])
            q1 = post_rstd(1, toks[1])
            r0 = post_pow(0, q0)
            m0 = post_scale(0, r0, q0, wbc, t_w)
            a0 = post_add(0, m0)
            s0 = square_x(0, a0)
            r1 = post_pow(1, q1)
            m1 = post_scale(1, r1, q1, wbc, t_w)
            n0 = rstd_x(0, s0)
            a1 = post_add(1, m1)
            s1 = square_x(1, a1)
            xn0 = scale_x(0, n0)
            n1 = rstd_x(1, s1)
            xn1 = scale_x(1, n1)
            return turn_x(w, dst, [], [xn0, xn1])

        t_x = [load(x[:, t, :], A["x"][t * 128:t * 128 + 128, :], via=SP) for t in range(2)]
        dma_unit(0)
        t_small = load(small[:], A["small"], via=SP)
        t_id = load(ident[:], A["ident"], via=SP)
        for i in range(1, RR):
            dma_unit(i)
        t_half = PO.op(lambda e: e.memset(half[:], -0.5))

        def move(eng, o, i, *tokens):
            if eng is AC:
                return AC.op(lambda e: e.copy(o, i), *tokens)
            return eng.op(lambda e: e.tensor_copy(o, i), *tokens)

        def tt(eng, o, a, b, op, *tokens):
            return eng.op(lambda e: e.tensor_tensor(o, a, b, op), *tokens)

        def ts(eng, o, a, s1, s2, op0, op1, *tokens):
            if op1 is None:
                return eng.op(lambda e: e.tensor_scalar(o, a, s1, None, op0), *tokens)
            return eng.op(lambda e: e.tensor_scalar(o, a, s1, s2, op0, op1), *tokens)

        def stt(o, a, s, b, op0, op1, *tokens):
            return DV.op(lambda e: e.scalar_tensor_tensor(out=o, in0=a, scalar=s, in1=b, op0=op0, op1=op1), *tokens)

        def act(o, i, f, *tokens, **kw):
            return AC.op(lambda e: e.activation(o, i, f, **kw), *tokens)

        def mm(o, l, r, start, stop, *tokens, tok=True, skip=False):
            if skip:
                f = lambda e: e.matmul(o, l, r, start=start, stop=stop, skip_group_check=True)
            else:
                f = lambda e: e.matmul(o, l, r, start=start, stop=stop)
            return PE.op(f, *tokens) if tok else PE.quiet(f, *tokens)

        def tr(o, i, *tokens, tok=True):
            f = lambda e: e.transpose(o, i, ident[:])
            return PE.op(f, t_id, *tokens) if tok else PE.quiet(f, t_id, *tokens)

        def bc(a, n):
            return a.unsqueeze(2).broadcast_to([128, a.shape[1], n])

        def rep(a, m):
            return a.unsqueeze(1).broadcast_to([128, m, a.shape[1]])

        H = (hh, hl)

        with ExitStack() as p1:
            cin = sb(p1, "cin", [128, 12, S + 3])
            cout = sb(p1, "cout", [128, 12, S])
            tm = sb(p1, "tm", [128, 2, 1536])
            kb = sb(p1, "kb", [128, 2, 512])
            dU = sb(p1, "dU", [128, 16, 128])
            AT = sb(p1, "AT", [128, 16, 128])
            tab = sb(p1, "tab", [128, 10, 128])
            gs = sb(p1, "gs", [128, 256])
            X = cin[:].rearrange("p a b -> p (a b)")[:, 0:2048].rearrange("p (s n) -> p s n", s=16)
            zz = cin[:].rearrange("p a b -> p (a b)")[:, 2048:3072].rearrange("p (t n) -> p t n", t=2)
            XT = xt[:].rearrange("p t (s n) -> p (t s) n", n=128)
            kT = cout[:].rearrange("p a s -> p (a s)")[:, 0:1024].rearrange("p (j s) -> p j s", j=4)
            kq = cout[:].rearrange("p a s -> p (a s)")[:, 1024:3072].rearrange(
                "p (j c w n) -> p j c w n", j=4, c=2, w=2)
            kd = tm[:, 0, 0:512]
            triu, nstrict, ones, m1T = (tab[:, i, :] for i in range(4))

            pa = ExitStack()
            qT = sb(pa, "qT", [128, 4, S])
            kTa = sb(pa, "kTa", [128, 4, S])
            va = sb(pa, "va", [128, 2, 512])
            P = sb(pa, "P", [128, 2, 384])
            PT = sb(pa, "PT", [128, 2, 384])
            T = sb(pa, "T", [128, 2, 384])
            flip = sb(pa, "flip", [128, 128])
            t_flip = load(flip[:], A["flip"])

            t_tab = load(tab[:], A["tab"].rearrange("p (a n) -> p a n", n=128))
            oh = cout[0:32, 0:2, :].rearrange("p a s -> p (a s)")[:, 0:384]
            ng = cout[0:8, 2:4, :].rearrange("p a s -> p (a s)")[:, 0:384]
            rb = cout[0:32, 4, 0:8]
            rrow = cout[0:8, 5:7, :].rearrange("p a s -> p (a s)")[:, 0:384]
            t_oh = load(oh, A["onehot"])
            t_ng = load(ng, A["neg"])
            t_rb = load(rb, A["rbT"])
            b = work()
            t = mm(bank[b][0:8, 0:384], rb, oh, True, True, t_oh, t_rb)
            t_row = tt(DV, rrow, bank[b][0:8, 0:384], ng, ALU.add, t, t_ng)
            free[b] = [t_row]
            t_scr = load(A["scr"], rrow, t_row)

            def load_T(h, *tokens):
                dst = T[:, h % 2, :]
                scr = A["scr"]
                a = bass.AP(scr.tensor, h * 384, [[1, 128], [1, 256]])
                b_ = bass.AP(scr.tensor, h * 384 + 128, [[1, 128], [1, 128]])
                s = sem(f"T{h}")
                PO.quiet(lambda e: e.dma_start(dst[:, 128:384], a).then_inc(s, 16), t_scr, *tokens)
                PO.quiet(lambda e: e.dma_start(dst[:, 0:128], b_).then_inc(s, 16))
                return s, 32

            sx = [square_x(t, t_x[t]) for t in range(2)]
            prep(0)
            xn = [scale_x(t, rstd_x(t, sx[t])) for t in range(2)]
            ready = turn_x(par("pre_mix"), H, [], xn)

            ab = dU[:, 0:2, :].rearrange("p a n -> p (a n)")
            b, t = b_unit(H, ready, "Z")
            t_ab = move(AC, ab, bank[b][:, 0:S], t)
            free[b] = [t_ab]
            sa = gs[:, 0:16].rearrange("p (c h) -> p c h", c=2)
            eb = gs[:, 16:32].rearrange("p (c h) -> p c h", c=2)
            sn = gs[:, 32:48]
            sa1, eb1 = gs[:, 0:16], gs[:, 16:32]
            ea = gs[:, 48:56]
            beta = gs[:, 56:72]
            graw = gs[:, 72:88]
            gc = gs[:, 88:104]
            eg = gs[:, 104:120]
            kdx = gs[:, 120:136]

            def gates():
                b = work()
                tr(bank[b][:, 0:128], ab[:, 0:128], t_ab, *free[b], tok=False)
                t = tr(bank[b][:, 128:256], ab[:, 128:256])
                pv = bank[b][:, 0:256].rearrange("p (c n) -> p c n", c=2)
                t1 = tt(DV, sa, pv[:, :, 112:120], rep(par("dt_bias"), 2), ALU.add, t, t_small)
                tb = move(DV, eb, pv[:, :, 120:128], t)
                free[b] = [tb]
                t2 = stt(sn, sa1, -1.0, sa1, ALU.mult, ALU.min, t1)
                t2 = act(sn, sn, ACT.Exp, t2)
                tb = act(eb1, eb1, ACT.Exp, tb, scale=-1.0)
                t3 = act(ea, par("A_log"), ACT.Exp, t_small)
                t2 = act(sn, sn, ACT.Ln, t2, bias=1.0)
                tb = ts(DV, eb1, eb1, 1.0, None, ALU.add, None, tb)
                t_beta = DV.op(lambda e: e.reciprocal(beta, eb1), tb)
                t2 = stt(sn, sa1, 0.0, sn, ALU.max, ALU.add, t2)
                t_g = stt(graw.rearrange("p (c h) -> p c h", c=2), sn.rearrange("p (c h) -> p c h", c=2), -1.0,
                          rep(ea, 2), ALU.mult, ALU.mult, t2, t3)
                return t_beta, t_g

            def sums(t_g):
                b = work()
                mm(bank[b][:, 0:16], triu, graw, True, True, t_g, t_tab, *free[b], tok=False)
                t = mm(bank[b][:, 16:32], ones, graw, True, True)
                t_gc = move(DV, gs[:, 88:104], bank[b][:, 0:16], t)
                t = tt(DV, kdx, bank[b][:, 16:32], gc, ALU.subtract, t_gc)
                free[b] = [t]
                t_eg = act(eg, gc, ACT.Exp, t_gc)
                t_kdx = act(kdx, kdx, ACT.Exp, t)
                return t_gc, t_eg, t_kdx

            def decays(g, t_g, t_gc):
                b = work()
                PE.wait(*free[b])
                for i in range(4):
                    s = 4 * g + i
                    t = mm(bank[b][:, i * 128:i * 128 + 128], graw[:, s:s + 1].broadcast_to([128, 128]), triu,
                           True, True, t_g)
                for i in range(4):
                    s = 4 * g + i
                    t_ = ts(DV, dU[:, s, :], bank[b][:, i * 128:i * 128 + 128], gc[:, s:s + 1], 0.0,
                            ALU.subtract, ALU.min, t, t_gc)
                free[b] = [t_]
                return t_

            t_pad = PO.op(lambda e: e.memset(cin[:, :, 0:3], 0.0))
            cw = par("conv1").rearrange("p (a k) -> p a k", k=4)
            t_c = []
            t_silu = []
            t_dec = []
            for u in range(6):
                b, t = b_unit(H, ready)
                t = move(AC, cin[:, 2 * u:2 * u + 2, 3:], bank[b][:].rearrange("p (a s) -> p a s", a=2), t)
                free[b] = [t]
                t2s = [t, t]
                for k in range(4):
                    for i in range(2):
                        a = 2 * u + i
                        if k == 0:
                            t2s[i] = ts(DV, cout[:, a, :], cin[:, a, 0:S], cw[:, a, 0:1], None, ALU.mult, None,
                                        t, t_pad, t_scr, t_row)
                        else:
                            t2s[i] = stt(cout[:, a, :], cin[:, a, k:k + S], cw[:, a, k:k + 1], cout[:, a, :],
                                         ALU.mult, ALU.add, t2s[i])
                t_c += t2s
                t_silu.append(act(cout[:, 2 * u:2 * u + 2, :], cout[:, 2 * u:2 * u + 2, :], ACT.Silu, t_c[-1],
                                  t_c[-2]))
                if u == 0:
                    t_beta, t_g = gates()
                elif u == 1:
                    t_gc, t_eg, t_kdx = sums(t_g)
                elif u >= 2:
                    t_dec.append(decays(u - 2, t_g, t_gc))
            t = act(dU[:], dU[:], ACT.Exp, *t_dec)
            t_dU = tt(PO, dU[:], dU[:], rep(triu, 16), ALU.mult, t, t_tab)
            t_dS = tt(PO, AT[:], dU[:], rep(nstrict, 16), ALU.mult, t_dU)

            t_qk = []

            def att_unit(u):
                b, t = b_unit(H, ready)
                dst = (qT, kTa)[u // 2]
                t = act(dst[:, 2 * (u % 2):2 * (u % 2) + 2, :], bank[b][:].rearrange("p (a s) -> p a s", a=2), ACT.Copy,
                        t, scale=(0.125, 1.0)[u // 2])
                free[b] = [t]
                t_qk.append(t)

            t_tm = {}
            sq = X[:].rearrange("p s n -> p (s n)")
            t_sq = []

            def token_major(w_):
                for c in range(2):
                    b = work()
                    PE.wait(*free[b])
                    for a in range(4):
                        t = tr(bank[b][:, a * 128:a * 128 + 128], cout[:, 4 * w_ + a, c * 128:c * 128 + 128],
                               t_silu[2 * w_ + a // 2])
                    t_tm[w_, c] = move(AC, tm[:, c, w_ * 512:w_ * 512 + 512], bank[b][:], t)
                    free[b] = [t_tm[w_, c]]
                    if w_ < 2:
                        o = (c * 2 + w_) * 512
                        t2 = act(sq[:, o:o + 512], bank[b][:], ACT.Square, t, *t_c)
                        t_sq.append(t2)
                        free[b] = [t2]

            att_unit(0)
            token_major(0)
            token_major(1)
            att_unit(1)
            rn = gs[:, 136:168]
            t = DV.op(lambda e: e.tensor_reduce(rn, sq.rearrange("p (s n) -> p s n", n=64), AXX, ALU.add), *t_sq)
            t = ts(DV, rn, rn, EPS, None, ALU.add, None, t)
            t = act(rn, rn, ACT.Sqrt, t)
            t = DV.op(lambda e: e.reciprocal(rn, rn), t)
            rq = rn.rearrange("p (c w h) -> p c w h", c=2, w=2)[:, :, 0, :]
            t_rn = ts(DV, rq, rq, 0.125, None, ALU.mult, None, t)
            t_n = []
            t_kb = []
            t_vb = []
            for c in range(2):
                o = tm[:, c, 0:1024].rearrange("p (s n) -> p s n", n=64)
                t_n.append(tt(DV, o, o, bc(rn[:, 16 * c:16 * c + 16], 64), ALU.mult, t_rn, t_tm[0, c], t_tm[1, c]))
                t_kb.append(tt(DV, kb[:, c, :].rearrange("p (s n) -> p s n", n=64),
                               tm[:, c, 512:1024].rearrange("p (s n) -> p s n", n=64),
                               bc(beta[:, 8 * c:8 * c + 8], 64), ALU.mult, t_n[c], t_beta))
            att_unit(2)
            token_major(2)
            for c in range(2):
                o = tm[:, c, 1024:1536].rearrange("p (s n) -> p s n", n=64)
                t_vb.append(tt(PO, o, o, bc(beta[:, 8 * c:8 * c + 8], 64), ALU.mult, t_tm[2, c], t_beta))
            att_unit(3)
            t_v = []
            for c, b, t in c_block(H, ready):
                t_v.append(move(AC, va[:, c, :], bank[b][:], t))
                free[b] = [t_v[-1]]

            t_kT = []
            for c in range(2):
                for w_, (src, dst, dep) in enumerate((
                        (tm[:, c, 512:1024], kT[:, :, c * 128:c * 128 + 128], t_n[c]),
                        (kb[:, c, :], kq[:, :, c, 0, :], t_kb[c]),
                        (tm[:, c, 0:512], kq[:, :, c, 1, :], t_n[c]))):
                    b = work()
                    PE.wait(*free[b])
                    for a in range(4):
                        t = tr(bank[b][:, a * 128:a * 128 + 128], src[:, a * 128:a * 128 + 128], dep)
                    t = move(AC, dst, bank[b][:].rearrange("p (a n) -> p a n", a=4), t)
                    free[b] = [t]
                    t_kT.append(t)
            t_kd = tt(PO, kd.rearrange("p (h n) -> p h n", n=64), tm[:, 0, 512:1024].rearrange("p (h n) -> p h n", n=64),
                      bc(kdx[:, 0:8], 64), ALU.mult, t_kdx, *t_kT)

            tz = []
            for c, b, t in c_block(H, ready):
                tz.append(act(zz[:, c, :], bank[b][:], ACT.Silu, t, *t_c, *t_sq))
                free[b] = [tz[-1]]
            zw = [tt(PO, zz[:, c, :].rearrange("p (h n) -> p h n", n=64), zz[:, c, :].rearrange("p (h n) -> p h n", n=64),
                     rep(par("gdn_w"), 8), ALU.mult, tz[c], t_small) for c in range(2)]
            w_in_read = PE.now()

            ready_c = [None] * 8
            tT = [load_T(0), load_T(1)]
            tP, tPV, tN, tPT = [None] * 8, [None] * 8, [None] * 8, [None] * 8

            def att_scores(h):
                j, p0, pp = h // 2, 64 * (h % 2), h % 2
                b = work()
                PE.wait(*free[b])
                t_bias = mm(bank[b][:, 0:384], flip[:], T[:, pp, :], True, False, tT[h], t_flip)
                mm(bank[b][:, 0:128], qT[p0:p0 + 64, j, 0:128], kTa[p0:p0 + 64, j, 0:128], False, False, *t_qk,
                   tok=False)
                t = mm(bank[b][:, 128:384], qT[p0:p0 + 64, j, 128:256], kTa[p0:p0 + 64, j, :], False, True)
                dep = [tP[h - 2]] if h >= 2 else []
                if h < 6:
                    tT.append(load_T(h + 2, t_bias))
                nm = gs[:, 168 + 4 * pp:170 + 4 * pp]
                sm_ = gs[:, 170 + 4 * pp:172 + 4 * pp]
                parts = ((0, 128), (128, 384))
                te = []
                for i, (lo, hi) in enumerate(parts):
                    t2 = DV.op(lambda e, i=i, lo=lo, hi=hi: e.tensor_reduce(
                        nm[:, i:i + 1], bank[b][:, lo:hi], AXX, ALU.max), t, *dep)
                tm_ = ts(DV, nm, nm, -1.0, None, ALU.mult, None, t2)
                for i, (lo, hi) in enumerate(parts):
                    te.append(act(P[:, pp, lo:hi], bank[b][:, lo:hi], ACT.Exp, tm_, *dep, bias=nm[:, i:i + 1],
                                  accum_out=sm_[:, i:i + 1]))
                free[b] = [te[-1]]
                t2 = DV.op(lambda e: e.reciprocal(sm_, sm_), *te)
                tN[h] = [ts(DV, P[:, pp, lo:hi], P[:, pp, lo:hi], sm_[:, i:i + 1], None, ALU.mult, None, t2)
                         for i, (lo, hi) in enumerate(parts)]

            def att_turn(h):
                pp = h % 2
                b = work()
                PE.wait(*free[b])
                for i in range(3):
                    t = tr(bank[b][:, i * 128:i * 128 + 128], P[:, pp, i * 128:i * 128 + 128], *tN[h])
                tP[h] = t
                dep = [tPV[h - 2]] if h >= 2 else []
                tPT[h] = move(AC, PT[:, pp, :], bank[b][:, 0:384], t, *dep)
                free[b] = [tPT[h]]

            def att_out(h):
                j, p0, pp = h // 2, 64 * (h % 2), h % 2
                b = 3
                if pp == 0:
                    PE.wait(*free[b])
                vs = va[:, :, h * 64:h * 64 + 64]
                mm(bank[b][p0:p0 + 64, 0:256], vs[:, 0, :], PT[:, pp, 0:256], True, False, tPT[h], *t_v, tok=False)
                tPV[h] = mm(bank[b][p0:p0 + 64, 128:256], vs[:, 1, :], PT[:, pp, 256:384], False, True)
                if pp == 1:
                    th = AC.op(lambda e: e.copy(hh[:, j, :], bank[b][:, 0:256]), tPV[h], w_in_read)
                    tl = tt(DV, hl[:, j, :], bank[b][:, 0:256], hh[:, j, :].bitcast(F32), ALU.subtract, th, w_in_read)
                    free[b] = [tl]
                    ready_c[j] = [th, tl]

            steps = []
            for n in range(11):
                if 0 <= n - 2 < 8:
                    steps.append((att_turn, n - 2))
                if n < 8:
                    steps.append((att_scores, n))
                if 0 <= n - 3 < 8:
                    steps.append((att_out, n - 3))

            def att(n):
                for _ in range(n):
                    if steps:
                        f, h = steps.pop(0)
                        f(h)

            t_AT = []
            for g in range(8):
                b = work()
                PE.wait(*free[b])
                s0 = 8 * (g // 4) + 4 * (g % 4 // 2) + g % 2
                for i in range(2):
                    s = s0 + 2 * i
                    c, h = s // 8, s % 8
                    p0 = 64 * (h % 2)
                    t = mm(bank[b][:, i * 256:i * 256 + 256], kT[p0:p0 + 64, h // 2, c * 128:c * 128 + 128],
                           kq[p0:p0 + 64, h // 2, c, :, :].rearrange("p w n -> p (w n)"), True, True, *t_kT)
                v = bank[b][:].rearrange("p (i w n) -> p i w n", i=2, w=2)
                at, du = AT[:, s0:s0 + 3:2, :], dU[:, s0:s0 + 3:2, :]
                t1 = tt(DV, at, v[:, :, 0, :], at, ALU.mult, t, t_dS)
                t_at = tt(DV, du, v[:, :, 1, :], du, ALU.mult, t, t_dU, t_dS)
                free[b] = [t_at]
                t_AT.append(t1)
                if g in (3, 7):
                    att(1)
            t_att = t_at
            t_A = tt(DV, AT[:], AT[:], rep(ident[:], 16), ALU.add, *t_AT)
            t_XT = tt(DV, XT, AT[:], rep(m1T, 16), ALU.mult, t_A, w_in_read)
            att(3)

            U0 = kb[:].rearrange("p c (s n) -> p (c s) n", n=128)
            U1 = kT.rearrange("p j (s n) -> p (j s) n", n=128)
            Ug = (U0[:, 0:4, :], U0[:, 4:8, :], U1[:, 0:4, :], U1[:, 4:8, :])
            vn = tm[:, 1, 0:512]
            S1 = tm[:, 1, 512:768]
            t_X = []
            t_XTg = [t_XT] * 4
            for g in range(4):
                b = work()
                PE.wait(*free[b])
                for i in range(4):
                    t = tr(bank[b][:, i * 128:i * 128 + 128], XT[:, 4 * g + i, :], t_XT)
                t = move(AC, X[:, 4 * g:4 * g + 4, :], bank[b][:].rearrange("p (a n) -> p a n", a=4), t, *t_sq,
                         *t_n)
                free[b] = [t]
                t_X.append(t)
            tb_ = 0
            for l, s_ in enumerate(LEVELS):
                mask = tab[:, 4 + l, :]
                tu = []
                for g in range(4):
                    b = tb_ % 3
                    tb_ += 1
                    PE.wait(*free[b])
                    for i in range(4):
                        s = 4 * g + i
                        t = mm(bank[b][:, i * 128:i * 128 + 128], AT[:, s, :], X[:, s, :], True, True, t_X[g], t_A,
                               t_XTg[g])
                    t = tt(DV, Ug[g], bank[b][:].rearrange("p (a n) -> p a n", a=4), rep(mask, 4),
                           ALU.mult, t, *t_kT)
                    free[b] = [t]
                    tu.append(t)
                att(2)
                for g in range(4):
                    bx = work() if l < 5 else None
                    by = work()
                    if l < 5:
                        PE.wait(*free[bx])
                        for i in range(4):
                            s = 4 * g + i
                            t1 = mm(bank[bx][:, i * 128:i * 128 + 128], XT[:, s, :], Ug[g][:, i, :], True, True, tu[g])
                    PE.wait(*free[by])
                    for i in range(4):
                        s = 4 * g + i
                        t2 = mm(bank[by][:, i * 128:i * 128 + 128], Ug[g][:, i, :], XT[:, s, :], True, True, tu[g])
                    if l < 5:
                        t_X[g] = move(AC, X[:, 4 * g:4 * g + 4, :], bank[bx][:].rearrange("p (a n) -> p a n", a=4),
                                      t1)
                        free[bx] = [t_X[g]]
                    t_XTg[g] = move(AC, XT[:, 4 * g:4 * g + 4, :], bank[by][:].rearrange("p (a n) -> p a n", a=4),
                                    t2)
                    free[by] = [t_XTg[g]]
                att(2)
            while steps:
                att(1)
            att_done = [PE.now(), AC.now(), DV.now()]
            pa.close()
            wbc = sb(p1, "wbc", [128, D])
            t_wbc = load(wbc[:], A["post_mix"].partition_broadcast(128), *att_done)

            ob = X[:].rearrange("p s n -> p (s n)")
            o_all = ob[:, 0:1024].rearrange("p (c n) -> p c n", c=2)
            qs = ob[:, 1024:1536]
            r1 = ob[:, 1536:2048]
            v64 = lambda a: a.rearrange("p (h n) -> p h n", n=64)
            pair = lambda a, w: v64(a).rearrange("p (j w) n -> p j w n", w=2)[:, :, w, :]
            eg1 = eg[:, 8:16].rearrange("p (j w) -> p j w", w=2)
            acc = [[0, 1], [2, 3]]
            b = work()
            PE.wait(*free[b])
            for h in range(8):
                t = mm(bank[b][:, h * 64:h * 64 + 64], XT[:, h, :], tm[:, 0, 1024 + h * 64:1024 + h * 64 + 64],
                       True, True, *t_XTg, *t_vb)
            t_v0 = move(AC, vn, bank[b][:], t)
            free[b] = [t_v0]
            got = {}

            def state():
                b = work()
                PE.wait(*free[b])
                for h in range(8):
                    p0 = 64 * (h % 2)
                    t = mm(bank[b][p0:p0 + 64, (h // 2) * 64:(h // 2) * 64 + 64], kd[:, h * 64:h * 64 + 64],
                           vn[:, h * 64:h * 64 + 64], True, True, t_v0, t_kd)
                got["s1"] = move(AC, S1, bank[b][:, 0:256], t)
                free[b] = [got["s1"]]
                bo = work()
                PE.wait(*free[bo])
                for h in range(8):
                    t = mm(bank[bo][:, h * 64:h * 64 + 64], dU[:, h, :], vn[:, h * 64:h * 64 + 64], True, True, t_att)
                got["o0"] = t
                got["oa"] = move(DV, o_all[:, 0, :], bank[bo][:], t)
                free[bo] = [got["oa"]]

            a_unit("A", H, ready_c, (0, 1), acc, True, False, hook=state)

            t_qs, t_rr = [], []
            for which, dst, acc_ in ((0, r1, t_rr), (1, qs, t_qs)):
                for w_ in range(2):
                    b = work()
                    PE.wait(*free[b])
                    p0 = 64 * w_
                    for j in range(4):
                        t = mm(bank[b][:, j * 64:j * 64 + 64], kq[p0:p0 + 64, j, 1, which, :],
                               S1[p0:p0 + 64, j * 64:j * 64 + 64], True, True, got["s1"])
                    t = tt(DV, pair(dst, w_), v64(bank[b][:, 0:256]), bc(eg1[:, :, w_], 64), ALU.mult, t, t_eg)
                    free[b] = [t]
                    acc_.append(t)
                if which == 0:
                    t_r1 = tt(DV, r1, tm[:, 1, 1024:1536], r1, ALU.subtract, *t_rr, *t_vb)

            def second():
                b = work()
                PE.wait(*free[b])
                for h in range(8):
                    t = mm(bank[b][:, h * 64:h * 64 + 64], XT[:, 8 + h, :], r1[:, h * 64:h * 64 + 64], True, True, t_r1)
                got["v1"] = move(AC, vn, bank[b][:], t, got["o0"])
                free[b] = [got["v1"]]

            a_unit("A", H, ready_c, (2, 3), acc, False, False, hook=second)
            b = work()
            PE.wait(*free[b])
            for h in range(8):
                t = mm(bank[b][:, h * 64:h * 64 + 64], dU[:, 8 + h, :], vn[:, h * 64:h * 64 + 64], True, True,
                       got["v1"])
            t_oa = [got["oa"], tt(DV, o_all[:, 1, :], bank[b][:], qs, ALU.add, t, *t_qs)]
            free[b] = [t_oa[1]]

            so = gs[:, 176:192]
            osq = kb[:].rearrange("p c n -> p (c n)")
            oflat = ob[:, 0:1024]
            t = act(osq, oflat, ACT.Square, *t_oa, scale=0.125)
            t = DV.op(lambda e: e.tensor_reduce(so, osq.rearrange("p (s n) -> p s n", n=64), AXX, ALU.add), t)
            t = ts(DV, so, so, EPS, None, ALU.add, None, t)
            t = act(so, so, ACT.Sqrt, t)
            t = DV.op(lambda e: e.reciprocal(so, so), t)
            t = tt(DV, v64(oflat), v64(oflat), bc(so, 64), ALU.mult, t)
            t = tt(DV, oflat, oflat, zz.rearrange("p c n -> p (c n)"), ALU.mult, t, *zw)
            for p in range(2):
                b = work()
                PE.wait(*free[b])
                for kk in range(2):
                    for c in range(2):
                        a = 2 * p + kk
                        t2 = tr(bank[b][:, kk * S + c * 128:kk * S + c * 128 + 128],
                                o_all[:, c, a * 128:a * 128 + 128], t)
                k = 4 + 2 * p
                v = bank[b][:].rearrange("p (a s) -> p a s", a=2)
                th = AC.op(lambda e, k=k, v=v: e.copy(hh[:, k:k + 2, :], v), t2, w_in_read)
                tl = tt(DV, hl[:, k:k + 2, :], v, hh[:, k:k + 2, :].bitcast(F32), ALU.subtract, th)
                free[b] = [tl]
                ready_c[k] = ready_c[k + 1] = [th, tl]
            a_unit("A", H, ready_c, (4, 5), acc, False, False)
            toks = a_unit("A", H, ready_c, (6, 7), acc, False, True)
            ready = between(toks, wbc, t_wbc, par("pre_mlp"), H)

        phase = [PE.now(), AC.now(), DV.now(), PO.now()]
        with ExitStack() as p2:
            wbc = sb(p2, "wbc2", [128, D])
            rl = sb(p2, "rl", [128, 2, 512])
            sqb = sb(p2, "sqb", [128, 2, 512])
            mh = sb(p2, "mh", [128, 4, S], FR)
            ml = sb(p2, "ml", [128, 4, S], FR)
            t_wbc = load(wbc[:], A["post_mlp"].partition_broadcast(128), *phase)
            mready = [None] * 32
            down = {}
            AC.wait(*phase)
            DV.wait(*phase)

            def mlp_down(i):
                m = (mh[:, 2 * (i % 2):2 * (i % 2) + 2, :], ml[:, 2 * (i % 2):2 * (i % 2) + 2, :])
                down[i] = a_unit("A", m, mready[2 * i:2 * i + 2], (0, 1), acc, i == 0, i == 15)

            for i in range(16):
                b, t = b_unit(H, ready, k_outer=i == 0)
                q = i % 2
                dep = [down[i - 2][1]] if i >= 2 else []
                r_, s_ = rl[:, q, :], sqb[:, q, :]
                ho = mh[:, 2 * q:2 * q + 2, :].rearrange("p a s -> p (a s)")
                lo = ml[:, 2 * q:2 * q + 2, :].rearrange("p a s -> p (a s)")
                t1 = act(r_, bank[b][:], ACT.Relu, t, *([mready[2 * i - 4][0], mready[2 * i - 4][1]] if i >= 2 else []))
                free[b] = [t1]
                t2 = act(ho, r_, ACT.Square, t1, *dep)
                t3 = tt(DV, s_, r_, r_, ALU.mult, t1)
                t4 = tt(DV, lo, s_, ho.bitcast(F32), ALU.subtract, t2, t3, *dep)
                mready[2 * i] = mready[2 * i + 1] = [t2, t4]
                if i >= 1:
                    mlp_down(i - 1)
            mlp_down(15)
            ready = between(down[15], wbc, t_wbc, par("g_mix"), H)

        phase = [PE.now(), AC.now(), DV.now(), PO.now()]
        with ExitStack() as p3:
            ya = sb(p3, "ya", [128, 2, D])
            Dm = sb(p3, "Dm", [128, 4, 512])
            vv = sb(p3, "vv", [128, 2, 512])
            pc = ExitStack()
            qr = sb(pc, "qr", [128, 8, S])
            kr = sb(pc, "kr", [128, 8, S])
            yh = sb(pc, "yh", [128, 8, S], FR)
            yl = sb(pc, "yl", [128, 8, S], FR)
            uc = sb(pc, "uc", [128, 2, 2, S + 2])
            gcv = sb(pc, "gcv", [128, 2, 2, S])
            cv = sb(pc, "cv", [128, 2, 2, S])
            rope = sb(pc, "rope", [128, 2, S])
            ra = sb(pc, "ra", [128, 2, 2, 512])
            dist = ra[:, 0, :, :]
            t_dist = load(dist, A["dist"].rearrange("p (a n) -> p a n", a=2), *phase)
            t_rope = load(rope[:], A["rope"].rearrange("p (a n) -> p a n", a=2), *phase)
            AC.wait(*phase)
            DV.wait(*phase)
            PO.wait(*phase)

            t_z = PO.op(lambda e: e.memset(uc[:], 0.0))
            cw = par("conv2").rearrange("p (a k) -> p a k", k=3)
            yready = []
            last = [[], []]
            lg = st[:, 16:24]
            sp_ = st[:, 24:32]

            def log_decays():
                dec = small[:, SM["dec_f"][0]:SM["dec_f"][0] + 8]
                t1 = ts(DV, lg, dec, -1.0, None, ALU.mult, None, t_small)
                t2 = stt(sp_, lg, -1.0, lg, ALU.mult, ALU.min, t1)
                t2 = act(sp_, sp_, ACT.Exp, t2)
                t2 = act(sp_, sp_, ACT.Ln, t2, bias=1.0)
                t2 = stt(sp_, lg, 0.0, sp_, ALU.max, ALU.add, t2)
                return ts(DV, lg, sp_, -1.0, None, ALU.mult, None, t2)

            def decay_of(h, t_lg):
                t = ts(DV, Dm[:, h, :], dist[:, 0, :], lg[:, h:h + 1], None, ALU.mult, None, t_lg, t_dist)
                t = stt(Dm[:, h, :], dist[:, 1, :], lg[:, 4 + h:5 + h], Dm[:, h, :], ALU.mult, ALU.add, t)
                return act(Dm[:, h, :], Dm[:, h, :], ACT.Exp, t)

            t_D = []
            for i in range(4):
                q = i % 2
                b, t = b_unit(H, ready, k_outer=i == 0)
                v = bank[b][:].rearrange("p (a s) -> p a s", a=2)
                t_xc = move(AC, gcv[:, q], v, t, *last[q])
                free[b] = [t_xc]
                b, t = b_unit(H, ready)
                v = bank[b][:].rearrange("p (a s) -> p a s", a=2)
                t_u = tt(DV, uc[:, q, :, 1:S + 1], v, gcv[:, q], ALU.mult, t, t_xc, t_z, *last[q])
                free[b] = [t_u]
                t2s = [t_u, t_u]
                for k in range(3):
                    for a in range(2):
                        w_ = cw[:, 2 * i + a, :]
                        if k == 0:
                            t2s[a] = ts(DV, cv[:, q, a, :], uc[:, q, a, 0:S], w_[:, 0:1], None, ALU.mult, None, t_u,
                                        *last[q])
                        else:
                            t2s[a] = stt(cv[:, q, a, :], uc[:, q, a, k:k + S], w_[:, k:k + 1], cv[:, q, a, :],
                                         ALU.mult, ALU.add, t2s[a])
                b, t = b_unit(H, ready)
                v = bank[b][:].rearrange("p (a s) -> p a s", a=2)
                t = tt(DV, cv[:, q], cv[:, q], v, ALU.mult, t, *t2s)
                free[b] = [t]
                th = AC.op(lambda e, i=i, q=q: e.copy(yh[:, 2 * i:2 * i + 2, :], cv[:, q]), t)
                tl = tt(DV, yl[:, 2 * i:2 * i + 2, :], cv[:, q], yh[:, 2 * i:2 * i + 2, :].bitcast(F32), ALU.subtract,
                        th)
                yready += [[th, tl]] * 2
                last[q] = [tl]
                if i == 0:
                    t_lg = log_decays()
                t_D.append(decay_of(i, t_lg))

            t_P = []
            tk = {}
            rdep = [t_D, t_D]

            def rotate(h, w_):
                dst = (qr, kr)[w_]
                b, t = b_unit(H, ready)
                v = bank[b][:].rearrange("p (a s) -> p a s", a=2)
                c_, s_ = (rep(rope[:, n, :], 2) for n in range(2))
                va_ = ra[:, w_, 0, :].rearrange("p (a s) -> p a s", a=2)
                vb_ = ra[:, w_, 1, :].rearrange("p (a s) -> p a s", a=2)
                t1 = tt(DV, va_, v, c_, ALU.mult, t, t_rope, *rdep[w_])
                t2 = tt(DV, vb_, v, s_, ALU.mult, t, *rdep[w_])
                free[b] = [t2]
                t3 = tt(PO, dst[:, 2 * h, :], va_[:, 0], vb_[:, 1], ALU.subtract, t1, t2)
                t4 = tt(PO, dst[:, 2 * h + 1, :], va_[:, 1], vb_[:, 0], ALU.add, t1, t2)
                rdep[w_] = [t3, t4]
                tk[h, w_] = [t3, t4]

            def scores(h):
                b = work()
                PE.wait(*free[b])
                for m in range(2):
                    for dk in range(2):
                        t = mm(bank[b][:, m * S:m * S + S], kr[:, 2 * h + dk, m * 128:m * 128 + 128],
                               qr[:, 2 * h + dk, :], dk == 0, dk == 1, *tk[h, 0], *tk[h, 1])
                t = stt(Dm[:, h, :], bank[b][:], 1.0 / 16, Dm[:, h, :], ALU.mult, ALU.mult, t, t_D[h])
                free[b] = [t]
                t_P.append(t)

            t_ya = []
            for h in range(4):
                rotate(h, 0)
                if h >= 1:
                    scores(h - 1)
                rotate(h, 1)
                if h == 0:
                    Y = (yh, yl)
                    for k in range(4):
                        tya = a_unit("A", Y, yready, (2 * k, 2 * k + 1), acc, k == 0, k == 3)
                    for tok in range(2):
                        for c in range(2):
                            t2 = move(AC, ya[:, tok, c * 512:c * 512 + 512], bank[2 * tok + c][:], tya[tok])
                            free[2 * tok + c] = [t2]
                            t_ya.append(t2)
            vdep = []

            def c_move(dst, deps):
                o = []
                for c, b, t in c_block(H, ready):
                    o.append(move(AC, dst[:, c, :], bank[b][:], t, *deps))
                    free[b] = [o[-1]]
                return o

            tv = c_move(vv, [])
            scores(3)
            conv_done = [PE.now(), AC.now(), DV.now(), PO.now()]
            pc.close()
            gt = sb(p3, "gt", [128, 4, S])
            rt = sb(p3, "rt", [128, 2, 512])
            ry = sb(p3, "ry", [128, 4, S])
            rh = sb(p3, "rh", [128, 4, S], FR)
            rlo = sb(p3, "rlo", [128, 4, S], FR)
            sg = sb(p3, "sg", [128, 2, 2, 512])
            gh = sb(p3, "gh", [128, 8, S], FR)
            gl_ = sb(p3, "gl_", [128, 8, S], FR)
            bn = sb(p3, "bn", [128, 2, 8])
            AC.wait(*conv_done)
            DV.wait(*conv_done)
            PO.wait(*conv_done)

            gw = par("g_ret")
            R = (rh, rlo)
            rr = [None] * 4
            mv = st[:, 40:44].rearrange("p (n w) -> p n w", w=2)
            rs = st[:, 44:46]
            t_rt, t_tr, t_w, ry_done = [], [], [], []

            def sigmoid_block(cb, q, deps):
                o = []
                for c, b, t in c_block(H, ready):
                    o.append(act(sg[:, q, c, :], bank[b][:], ACT.Sigmoid, t, *deps))
                    free[b] = [o[-1]]
                return o

            for h in range(4):
                if h:
                    tv = c_move(vv, [t_rv])
                tg = []
                for u in range(2):
                    b, t = b_unit(H, ready)
                    v = bank[b][:].rearrange("p (a s) -> p a s", a=2)
                    t = act(gt[:, 2 * u:2 * u + 2, :], v, ACT.Silu, t, *ry_done)
                    free[b] = [t]
                    for a in range(2 * u, 2 * u + 2):
                        tg.append(ts(PO, gt[:, a, :], gt[:, a, :], gw[:, 4 * h + a:4 * h + a + 1], None,
                                     ALU.mult, None, t))
                trn = []
                rb_ = [work(), work()]
                for n in range(2):
                    b = rb_[n]
                    PE.wait(*free[b])
                    for m in range(2):
                        t_rv = mm(bank[b][:], Dm[:, h, m * S + n * 128:m * S + n * 128 + 128], vv[:, m, :],
                                  m == 0, m == 1, t_P[h], *tv)
                    t = DV.op(lambda e, n=n, b=b: e.bn_stats(bn[:, n, 0:6], bank[b][:]), t_rv)
                    t = DV.op(lambda e, n=n: e.bn_aggr(st[:, 40 + 2 * n:42 + 2 * n], bn[:, n, 0:6]), t, *t_rt)
                    trn.append(t)
                t = ts(DV, rs, mv[:, :, 1], EPS, None, ALU.add, None, *trn)
                t = PO.op(lambda e: e.tensor_tensor(rs, rs, half[:], ALU.pow), t)
                t_rt = []
                for n in range(2):
                    b = rb_[n]
                    t2 = ts(DV, rt[:, n, :], bank[b][:], mv[:, n, 0:1], rs[:, n:n + 1], ALU.subtract, ALU.mult,
                            t, *t_tr)
                    free[b] = [t2]
                    t_rt.append(t2)
                if h == 0:
                    for cb in range(2):
                        t1s = sigmoid_block(cb, cb, [])
                        for c in range(2):
                            d = ya[:, c, cb * 512:cb * 512 + 512]
                            t_ya.append(tt(DV, d, d, sg[:, cb, c, :], ALU.mult, t1s[c], *t_ya[0:4]))
                else:
                    a_unit("A", R, rr, (0, 1), acc, h == 1, False)
                    t_w = [a_unit("A", R, rr, (2, 3), acc, False, False)[1]]
                if h == 3:
                    tsg = [sigmoid_block(0, 0, t_ya)]
                for u in range(2):
                    b = work()
                    PE.wait(*free[b])
                    for a in range(2):
                        for n in range(2):
                            t = tr(bank[b][:, a * S + n * 128:a * S + n * 128 + 128],
                                   rt[:, n, (2 * u + a) * 128:(2 * u + a) * 128 + 128], *t_rt)
                    v = bank[b][:].rearrange("p (a s) -> p a s", a=2)
                    t1 = tt(DV, ry[:, 2 * u:2 * u + 2, :], v, gt[:, 2 * u:2 * u + 2, :], ALU.mult, t, *tg)
                    free[b] = [t1]
                    th = AC.op(lambda e, u=u: e.copy(rh[:, 2 * u:2 * u + 2, :], ry[:, 2 * u:2 * u + 2, :]),
                               t1, *t_w)
                    tl = tt(DV, rlo[:, 2 * u:2 * u + 2, :], ry[:, 2 * u:2 * u + 2, :],
                            rh[:, 2 * u:2 * u + 2, :].bitcast(F32), ALU.subtract, t1, th, *t_w)
                    rr[2 * u] = rr[2 * u + 1] = [th, tl]
                    ry_done = [tl]
                t_tr = [t]
            a_unit("A", R, rr, (0, 1), acc, False, False)
            toks = a_unit("A", R, rr, (2, 3), acc, False, True)

            yr1 = rt
            t_m = {}
            for tok in range(2):
                m = xt[:, tok, 0:512]
                t = tt(DV, m, bank[2 * tok][:], sg[:, 0, tok, :], ALU.mult, toks[tok], tsg[0][tok], *tsg[0])
                free[2 * tok] = [t]
                t_m[tok, 0] = tt(DV, m, m, ya[:, tok, 0:512], ALU.add, t, *t_ya)
            t_y1 = []
            for tok in range(2):
                t = move(AC, yr1[:, tok, :], bank[2 * tok + 1][:], toks[tok], *t_tr)
                free[2 * tok + 1] = [t]
                t_y1.append(t)
            tsg.append(sigmoid_block(1, 1, t_ya))
            mr = []

            def turn_merged(cb):
                for p in (2 * cb, 2 * cb + 1):
                    b = work()
                    PE.wait(*free[b])
                    for tok in range(2):
                        for kk in range(2):
                            k = 2 * p + kk
                            t = tr(bank[b][:, kk * S + tok * 128:kk * S + tok * 128 + 128],
                                   xt[:, tok, k * 128:k * 128 + 128], t_m[tok, cb])
                    v = bank[b][:].rearrange("p (a s) -> p a s", a=2)
                    k = 2 * p
                    th = AC.op(lambda e, k=k, v=v: e.copy(gh[:, k:k + 2, :], v), t)
                    tl = tt(DV, gl_[:, k:k + 2, :], v, gh[:, k:k + 2, :].bitcast(F32), ALU.subtract, th)
                    free[b] = [tl]
                    mr.extend([[th, tl]] * 2)

            turn_merged(0)
            for tok in range(2):
                m = xt[:, tok, 512:1024]
                t = tt(DV, m, yr1[:, tok, :], sg[:, 1, tok, :], ALU.mult, t_y1[tok], tsg[1][tok])
                t_m[tok, 1] = tt(DV, m, m, ya[:, tok, 512:1024], ALU.add, t, *t_ya)
            Gm = (gh, gl_)
            mr4 = list(mr) + [None] * 4
            a_unit("A", Gm, mr4, (0, 1), acc, True, False)
            turn_merged(1)
            a_unit("A", Gm, mr, (2, 3), acc, False, False)
            a_unit("A", Gm, mr, (4, 5), acc, False, False)
            toks = a_unit("A", Gm, mr, (6, 7), acc, False, True)
            sx = []
            xa = {}

            def add_back(tok, toks):
                for c in range(2):
                    d = x[:, tok, c * 512:c * 512 + 512]
                    t2 = tt(DV, d, d, bank[2 * tok + c][:], ALU.add, toks[tok])
                    free[2 * tok + c] = [t2]
                return t2

            a0 = add_back(0, toks)
            s0 = square_x(0, a0, *[PE.now()])
            a1 = add_back(1, toks)
            n0 = rstd_x(0, s0)
            s1 = square_x(1, a1)
            xn0 = scale_x(0, n0)
            xn1 = scale_x(1, rstd_x(1, s1))
            ready = turn_x(par("g_ffn"), H, [], [xn0, xn1])

        phase = [PE.now(), AC.now(), DV.now(), PO.now()]
        with ExitStack() as p4:
            wbc = sb(p4, "wbc4", [128, D])
            gl = sb(p4, "gl", [128, 2, 512])
            fh = sb(p4, "fh", [128, 4, S], FR)
            fl = sb(p4, "fl", [128, 4, S], FR)
            t_wbc = load(wbc[:], A["g_final"].partition_broadcast(128), *phase)
            AC.wait(*phase)
            DV.wait(*phase)
            fready = [None] * 22
            fdown = {}

            def ff_down(i):
                m = (fh[:, 2 * (i % 2):2 * (i % 2) + 2, :], fl[:, 2 * (i % 2):2 * (i % 2) + 2, :])
                fdown[i] = a_unit("A", m, fready[2 * i:2 * i + 2], (0, 1), acc, i == 0, i == 10)

            for i in range(11):
                q = i % 2
                bg, tg = b_unit(H, ready, k_outer=i == 0)
                t1 = act(gl[:, q, :], bank[bg][:], ACT.Silu, tg,
                         *([fready[2 * i - 4][0], fready[2 * i - 4][1]] if i >= 2 else []))
                free[bg] = [t1]
                bu, tu = b_unit(H, ready)
                t2 = tt(DV, gl[:, q, :], gl[:, q, :], bank[bu][:], ALU.mult, tu, t1)
                free[bu] = [t2]
                dep = [fdown[i - 2][1]] if i >= 2 else []
                ho = fh[:, 2 * q:2 * q + 2, :].rearrange("p a s -> p (a s)")
                lo = fl[:, 2 * q:2 * q + 2, :].rearrange("p a s -> p (a s)")
                t3 = AC.op(lambda e, ho=ho, q=q: e.copy(ho, gl[:, q, :]), t2, *dep)
                t4 = tt(DV, lo, gl[:, q, :], ho.bitcast(F32), ALU.subtract, t2, t3, *dep)
                fready[2 * i] = fready[2 * i + 1] = [t3, t4]
                if i >= 1:
                    ff_down(i - 1)
            ff_down(10)
            s_out = sem("s_out")
            a0 = add_back(0, fdown[10])
            s0 = square_x(0, a0)
            a1 = add_back(1, fdown[10])
            s1 = square_x(1, a1)
            n = [rstd_x(0, s0), rstd_x(1, s1)]
            for tok in range(2):
                for c in range(2):
                    cs = slice(c * 512, c * 512 + 512)
                    t = stt(xt[:, tok, cs], x[:, tok, cs], ms[:, tok:tok + 1], wbc[:, cs], ALU.mult, ALU.mult, n[tok],
                            t_wbc)
                    SP.quiet(lambda e, tok=tok, cs=cs: e.dma_start(out[tok * 128:tok * 128 + 128, cs],
                                                                   xt[:, tok, cs]).then_inc(s_out, 16), t)
            SP.wait((s_out, 64))

        assert len(used) == len(PLAN)
        block = top.enter_context(nc.Block())

        @block.sync
        def _(e):
            for f in SP.queue:
                f(e)

        @block.gpsimd
        def _(e):
            for f in PO.queue:
                f(e)

        @block.scalar
        def _(e):
            for f in AC.queue:
                f(e)

        @block.vector
        def _(e):
            for f in DV.queue:
                f(e)

        @block.tensor
        def _(e):
            for f in PE.queue:
                f(e)


def kernel(**inputs):
    import concourse.bacc as bacc
    from concourse.bass_utils import run_bass_kernel_spmd as run

    g = {k: np.asarray(v) for k, v in inputs.items()}
    W = np.empty((len(PLAN), 128, U), np.float32)
    for i, u in enumerate(PLAN):
        w = g[u[1]][0]
        if u[0] == "B":
            W[i] = w[:, u[2]:u[2] + 256].reshape(8, 128, 256).transpose(1, 0, 2).reshape(128, U)
        elif u[0] == "Z":
            W[i, :, 0:1024] = w[:, u[2]:u[2] + 128].reshape(8, 128, 128).transpose(1, 0, 2).reshape(128, 1024)
            W[i, :, 1024:] = 0
        elif u[0] == "C":
            W[i] = w[128 * u[3]:128 * u[3] + 512, u[2]:u[2] + 512].reshape(4, 128, 512).transpose(1, 0, 2).reshape(128, U)
        else:
            W[i] = w[128 * u[2]:128 * u[2] + 256, :].reshape(2, 128, 1024).transpose(1, 0, 2).reshape(128, U)
    small = np.empty((128, NSM), np.float32)

    def put(name, a):
        small[:, SM[name][0]:SM[name][0] + SM[name][1]] = a

    for name, key in (("pre_mix", "pre_mix_norm"), ("pre_mlp", "pre_mlp_norm"), ("g_mix", "g_mix_2"),
                      ("g_ffn", "g_ffn_2"), ("g_ret", "g_ret_2")):
        put(name, g[key][0].reshape(-1, 128).T)
    put("conv1", g["conv_w"][0].reshape(4, 12, 128).transpose(2, 1, 0).reshape(128, 48))
    put("conv2", g["w_conv_2"][0].reshape(3, 8, 128).transpose(2, 1, 0).reshape(128, 24))
    for name, key in (("A_log", "A_log"), ("dt_bias", "dt_bias"), ("dec_f", "dec_f_2"), ("dec_b", "dec_b_2"),
                      ("gdn_w", "gdn_norm_w")):
        put(name, np.broadcast_to(g[key][0], (128, SM[name][1])))
    onehot, neg = table_onehot()
    arrays = {
        "W": W, "x": np.ascontiguousarray(g["x"][0]), "small": small, "ident": np.eye(128, dtype=np.float32),
        "flip": np.ascontiguousarray(np.eye(128, dtype=np.float32)[::-1]),
        "tab": table_gdn(), "onehot": onehot, "neg": neg, "rbT": np.ascontiguousarray(g["rel_bias"].T),
        "dist": table_dist(), "rope": table_rope(),
        "post_mix": np.ascontiguousarray(g["post_mix_norm"][0]),
        "post_mlp": np.ascontiguousarray(g["post_mlp_norm"][0]),
        "g_final": np.ascontiguousarray(g["g_final_2"]),
    }
    nc = bacc.Bacc("TRN2", target_bir_lowering=False, num_devices=1)
    A = {n: nc.dram_tensor("in_" + n, a.shape, F32, kind="ExternalInput").ap() for n, a in arrays.items()}
    A["scr"] = nc.dram_tensor("scr", [8, 384], F32, kind="Internal").ap()
    out = nc.dram_tensor("out_0", (S, D), F32, kind="ExternalOutput").ap()
    build(nc, A, out)
    r = run(nc, [{"in_" + n: a for n, a in arrays.items()}], core_ids=[0])
    return r.results[0]["out_0"].reshape(1, S, D)
```

```python
import math
from contextlib import ExitStack

import numpy as np

import concourse.bass as bass
from concourse import mybir

F32 = mybir.dt.float32
FR = mybir.dt.float32r
ALU = mybir.AluOpType
ACT = mybir.ActivationFunctionType
AXX = mybir.AxisListType.X
EPS = 1e-6

S = 256
D = 1024
RR = 3
HR = 4
AHEAD = 2
U = 2048
NEG = -1e30



def buckets():
    d = np.arange(256)
    large = 16 + (np.log(np.maximum(d, 1).astype(np.float32) / np.float32(16))
                  / np.float32(math.log(128 / 16)) * np.float32(16)).astype(np.int32)
    return np.where(d < 16, d, np.minimum(large, 31))


BASE = 8
LEVELS = (8, 16, 32, 64)


def level_mask(s):
    i = np.arange(128)[:, None]
    j = np.arange(128)[None, :]
    low = (i // (2 * s) == j // (2 * s)) & (i // s % 2 == 1) & (j // s % 2 == 0)
    return (low | (i == j)).astype(np.float32)


def table_gdn():
    i = np.arange(128)[:, None]
    j = np.arange(128)[None, :]
    same = i // BASE == j // BASE
    parts = [(i <= j).astype(np.float32), -(i < j).astype(np.float32), np.ones((128, 128), np.float32),
             (same & (i < j)).astype(np.float32), same.astype(np.float32), (i % BASE == j).astype(np.float32)]
    parts += [level_mask(s) for s in LEVELS]
    return np.ascontiguousarray(np.concatenate(parts, 1))


def table_onehot():
    t = np.zeros((32, 384), np.float32)
    m = np.zeros((8, 384), np.float32)
    b = buckets()
    for j in range(384):
        if 255 - j >= 0:
            t[b[255 - j], j] = 1.0
        else:
            m[:, j] = NEG
    return t, m


def table_rope():
    pos = np.arange(S, dtype=np.float32)
    freqs = (np.float32(10000.0) ** (-np.arange(0, 256, 2, dtype=np.float32) / np.float32(256))).astype(np.float32)
    ang = (freqs[:, None] * pos[None, :]).astype(np.float32).astype(np.float64)
    return np.ascontiguousarray(np.concatenate([np.cos(ang), np.sin(ang)], 1).astype(np.float32))


def table_dist():
    m = np.arange(128)[:, None, None] + 128 * np.arange(2)[None, :, None]
    n = np.arange(256)[None, None, :]
    a = np.maximum(n - m, 0).astype(np.float32).reshape(128, 512)
    b = np.maximum(m - n, 0).astype(np.float32).reshape(128, 512)
    return np.ascontiguousarray(np.concatenate([a, b], 1))


def plan():
    u = [("Z", "w_in", 3472)]
    u += [("B", "w_in", 1536 + 256 * i) for i in range(6)]
    u += [("B", "w_in", 256 * i) for i in range(4)]
    u += [("C", "w_in", 1024, k) for k in (0, 4)]
    u += [("C", "w_in", 3072, k) for k in (0, 4)]
    u += [("A", "w_out", 2 * k) for k in range(4)]
    u += [("C", "w_up", 0, k) for k in (0, 4)]
    for i in range(2, 16):
        u += [("B", "w_up", 256 * i), ("A", "w_down", 2 * (i - 2))]
    u += [("A", "w_down", 28), ("A", "w_down", 30)]
    u += [("C", "w_in_2", 5120, k) for k in (0, 4)]
    for i in range(4):
        u += [("B", "w_in_2", 256 * i), ("B", "w_in_2", 2048 + 256 * i), ("B", "w_in_2", 1024 + 256 * i)]
    for i in range(4):
        u += [("B", "w_in_2", 3072 + 256 * i), ("B", "w_in_2", 4096 + 256 * i)]
        if i == 0:
            u += [("A", "w_a_out_2", 2 * k) for k in range(4)]
    for h in range(4):
        if h:
            u += [("C", "w_in_2", 5120 + 512 * h, k) for k in (0, 4)]
        u += [("B", "w_in_2", 7168 + 512 * h), ("B", "w_in_2", 7168 + 512 * h + 256)]
        if h == 0:
            for cb in range(2):
                u += [("C", "w_in_2", 9216 + 512 * cb, k) for k in (0, 4)]
        else:
            u += [("A", "w_r_out_2", 4 * (h - 1)), ("A", "w_r_out_2", 4 * (h - 1) + 2)]
    u += [("C", "w_in_2", 10240, k) for k in (0, 4)]
    u += [("A", "w_r_out_2", 12), ("A", "w_r_out_2", 14)]
    u += [("C", "w_in_2", 10752, k) for k in (0, 4)]
    u += [("A", "w_o_2", 2 * k) for k in range(4)]
    for i in range(11):
        u += [("B", "w_ff_gate_2", 256 * i), ("B", "w_ff_up_2", 256 * i)]
        if i >= 1:
            u.append(("A", "w_ff_down_2", 2 * (i - 1)))
    u.append(("A", "w_ff_down_2", 20))
    return u


PLAN = plan()

SM = {}
_at = 0
for _n, _w in (("pre_mix", 8), ("pre_mlp", 8), ("g_mix", 8), ("g_ffn", 8), ("conv1", 48), ("conv2", 24),
               ("g_ret", 16), ("A_log", 8), ("dt_bias", 8), ("dec_f", 4), ("dec_b", 4), ("gdn_w", 64)):
    SM[_n] = (_at, _w)
    _at += _w
NSM = _at


class Engine:

    def __init__(self, sem):
        self.sem, self.count, self.queue, self.seen = sem, 0, [], {}

    def wait(self, *tokens):
        for sem, value in tokens:
            if self.seen.get(id(sem), 0) < value:
                self.seen[id(sem)] = value
                self.queue.append(lambda e, s=sem, v=value: e.wait_ge(s, v))

    def op(self, fn, *tokens):
        self.wait(*tokens)
        self.count += 1
        self.queue.append(lambda e: fn(e).then_inc(self.sem, 1))
        return self.sem, self.count

    def quiet(self, fn, *tokens):
        self.wait(*tokens)
        self.queue.append(fn)

    def now(self):
        return self.sem, self.count


def build(nc, A, out):
    with ExitStack() as top:
        nsem = [0]

        def sem(name):
            nsem[0] += 1
            return top.enter_context(nc.semaphore(name))

        def sb(stack, name, shape, dt=F32):
            return stack.enter_context(nc.sbuf_tensor("t_" + name, shape, dt))

        PE, AC, DV, PO, SP = (Engine(sem("s_" + n)) for n in ("pe", "act", "dve", "pool", "sp"))
        bank = [top.enter_context(nc.psum_tensor(f"bank{i}", [128, 512], F32)) for i in range(8)]
        free = [[] for _ in range(8)]
        turn = [0]

        def work():
            b = 4 + turn[0] % 4
            turn[0] += 1
            return b

        raw = sb(top, "raw", [128, RR, U])
        wh = sb(top, "wh", [128, HR, U], FR)
        wl = sb(top, "wl", [128, HR, U], FR)
        hh = sb(top, "hh", [128, 8, S], FR)
        hl = sb(top, "hl", [128, 8, S], FR)
        x = sb(top, "x", [128, 2, D])
        xt = sb(top, "xt", [128, 2, D])
        ident = sb(top, "ident", [128, 128])
        small = sb(top, "small", [128, NSM])
        st = sb(top, "st", [128, 128])
        half = sb(top, "half", [128, 2])
        hold = sb(top, "hold", [128, 2048])
        wbc = hold[:, 0:1024]
        junk = hold[:, 1024:1536]

        def par(name):
            a, w = SM[name]
            return small[:, a:a + w]

        def load(dst, src, *tokens, via=None):
            s = sem(f"dma{nsem[0]}")
            (via or PO).quiet(lambda e: e.dma_start(dst, src).then_inc(s, 16), *tokens)
            return s, 16

        raw_sem = [sem(f"raw{i}") for i in range(RR)]
        split = []
        used = []

        def dma_unit(i):
            r = i % RR
            if i >= RR:
                SP.wait(*split[i - RR])
            if PLAN[i][0] == "Z":
                SP.quiet(lambda e: e.dma_start(raw[:, r, 0:1024], A["W"][i, :, 0:1024]).then_inc(raw_sem[r], 16))
            else:
                SP.quiet(lambda e: e.dma_start(raw[:, r, :], A["W"][i]).then_inc(raw_sem[r], 16))

        def prep(upto):
            while len(split) < min(upto + 1, len(PLAN)):
                i = len(split)
                if i >= RR:
                    dma_unit(i)
                r, h = i % RR, i % HR
                n = 1024 if PLAN[i][0] == "Z" else U
                arrived = (raw_sem[r], 16 * (i // RR + 1))
                freed = [used[i - HR]] if i >= HR else []
                t1 = AC.op(lambda e, h=h, r=r, n=n: e.copy(wh[:, h, 0:n], raw[:, r, 0:n]), arrived, *freed)
                t2 = DV.op(lambda e, h=h, r=r, n=n: e.tensor_tensor(wl[:, h, 0:n], raw[:, r, 0:n], wh[:, h, 0:n].bitcast(F32),
                                                     ALU.subtract), arrived, t1, *freed)
                split.append((t1, t2))

        def unit(kind, skip=0, ahead=AHEAD):
            i = len(used) + skip
            assert PLAN[i][0] == kind, (i, PLAN[i], kind)
            prep(i + ahead)
            PE.wait(*split[i])
            return i % HR

        def done(tok):
            used.append(tok)

        PASS = ((0, 0), (0, 1), (1, 0))

        def b_unit(act, ready, kind="B", k_outer=False, mid=None):
            b = work()
            h = unit(kind)
            w = (wh, wl)
            nt = 1 if kind == "Z" else 2
            PE.wait(*free[b])
            if k_outer:
                order = [(c, k) for k in range(8) for c in range(nt)]
            else:
                order = [(c, k) for c in range(nt) for k in range(8)]
            for at, (c, k) in enumerate(order):
                PE.wait(*ready[k])
                for n, (i, j) in enumerate(PASS):
                    lhs = w[i][:, h, k * 128 * nt + c * 128:k * 128 * nt + c * 128 + 128]
                    rhs = act[j][:, k, :]
                    if k_outer:
                        first, last = at == 0 and n == 0, at == len(order) - 1 and n == 2
                    else:
                        first, last = k == 0 and n == 0, k == 7 and n == 2
                    f = (lambda e, o=bank[b][:, c * S:c * S + S], l=lhs, r=rhs, a=first, z=last:
                         e.matmul(o, l, r, start=a, stop=z, skip_group_check=k_outer))
                    if at == len(order) - 1 and n == 2:
                        tok = PE.op(f)
                    else:
                        PE.quiet(f)
                if mid and at == 7:
                    mid()
            done(tok)
            return b, tok

        def a_unit(kind, act, ready, ks, outs, first, last, hooks={}):
            h = unit(kind)
            w = (wh, wl)
            nk, ncb = len(ks), len(outs[0])
            if last:
                order = [(t, kk) for t in range(2) for kk in range(nk)]
            else:
                order = [(t, kk) for kk in range(nk) for t in range(2)]
            toks = [None, None]
            opened = set()
            for at, (t, kk) in enumerate(order):
                PE.wait(*ready[ks[kk]])
                if first and t not in opened:
                    opened.add(t)
                    for b in outs[t]:
                        PE.wait(*free[b])
                for n, (j, i) in enumerate(((0, 0), (0, 1), (1, 0))):
                    for c in range(ncb):
                        lhs = act[j][:, ks[kk], t * 128:t * 128 + 128]
                        rhs = w[i][:, h, kk * 512 * ncb + c * 512:kk * 512 * ncb + c * 512 + 512]
                        a = first and kk == 0 and n == 0
                        z = last and kk == nk - 1 and n == 2
                        f = (lambda e, o=bank[outs[t][c]][:], l=lhs, r=rhs, a=a, z=z:
                             e.matmul(o, l, r, start=a, stop=z))
                        if n == 2 and c == ncb - 1 and kk == nk - 1:
                            toks[t] = PE.op(f)
                        else:
                            PE.quiet(f)
                if at in hooks:
                    hooks[at]()
            done(toks[1])
            return toks

        def a_pair(act, ready, ks, outs, mid=None):
            i0 = len(used)
            h = [unit("A"), (i0 + 1) % HR]
            prep(i0 + 1 + AHEAD)
            w = (wh, wl)
            toks = [[None, None], [None, None]]
            for t in range(2):
                deps = {k: list(ready[k]) for k in ks}
                steps = [(0, kk, n, c) for kk in range(2) for n in range(3) for c in range(2)]
                steps += [(1, kk, n, c) for c in range(2) for kk in range(2) for n in range(3)]
                for at, (u, kk, n, c) in enumerate(steps):
                    if t == 0 and at == 12:
                        PE.wait(*split[i0 + 1])
                        if mid:
                            mid()
                    k = ks[2 * u + kk]
                    j, i = ((0, 0), (0, 1), (1, 0))[n]
                    f = (lambda e, o=bank[outs[t][c]][:], l=act[j][:, k, t * 128:t * 128 + 128],
                         r=w[i][:, h[u], kk * 1024 + c * 512:kk * 1024 + c * 512 + 512], z=u == 1 and kk == 1 and n == 2:
                         e.matmul(o, l, r, start=False, stop=z))
                    if kk == 1 and n == 2 and (u == 1 or c == 1):
                        tok = PE.op(f, *deps[k])
                        if u:
                            toks[t][c] = tok
                        elif t:
                            done(tok)
                    else:
                        PE.quiet(f, *deps[k])
            done(toks[1][1])
            return toks

        def c_block(act, ready, mid=None):
            outs = [[work()], [work()]]
            a_unit("C", act, ready, range(0, 4), outs, True, False)
            if mid:
                mid()
            toks = a_unit("C", act, ready, range(4, 8), outs, False, True)
            return [(0, outs[0][0], toks[0]), (1, outs[1][0], toks[1])]

        ms = st[:, 0:2]
        mp = st[:, 2:4]
        part = st[:, 4:8]
        xpart = st[:, 8:12]

        def pow_half(a, *tokens):
            return PO.op(lambda e: e.tensor_tensor(a, a, half[:, 0:1], ALU.pow), t_half, *tokens)

        def square_x(t, *tokens):
            return AC.op(lambda e: e.activation(xt[:, t, :], x[:, t, :], ACT.Square, scale=1.0 / 32,
                                                accum_out=ms[:, t:t + 1]), *tokens)

        def rstd_x(t, tok):
            a = DV.op(lambda e: e.tensor_scalar(ms[:, t:t + 1], ms[:, t:t + 1], EPS, None, ALU.add), tok)
            return pow_half(ms[:, t:t + 1], a)

        def scale_x(t, tok):
            return DV.op(lambda e: e.tensor_scalar(xt[:, t, :], x[:, t, :], ms[:, t:t + 1], None, ALU.mult), tok)

        def turn_x(w, dst, prior, xn):
            ready = []
            bs = [work() for _ in range(4)]
            for b in bs:
                PE.wait(*free[b])
            toks = []
            for t in range(2):
                for p, b in enumerate(bs):
                    for kk in range(2):
                        k = 2 * p + kk
                        f = (lambda e, kk=kk, k=k, t=t, b=b: e.transpose(
                            bank[b][:, kk * S + t * 128:kk * S + t * 128 + 128], xt[:, t, k * 128:k * 128 + 128],
                            ident[:]))
                        if kk == 1 and t == 1:
                            toks.append(PE.op(f, t_id, xn[t][p // 2]))
                        else:
                            PE.quiet(f, t_id, xn[t][p // 2])
            for p, b in enumerate(bs):
                tok = toks[p]
                his = []
                for kk in range(2):
                    k = 2 * p + kk
                    his.append(AC.op(lambda e, kk=kk, k=k, b=b: e.activation(
                        dst[0][:, k, :], bank[b][:, kk * S:kk * S + S], ACT.Copy, scale=w[:, k:k + 1]),
                        tok, t_small, *prior))
                for kk in range(2):
                    k = 2 * p + kk
                    lo = DV.op(lambda e, kk=kk, k=k, b=b: e.scalar_tensor_tensor(
                        out=dst[1][:, k, :], in0=bank[b][:, kk * S:kk * S + S], scalar=w[:, k:k + 1],
                        in1=dst[0][:, k, :].bitcast(F32), op0=ALU.mult, op1=ALU.subtract), his[1], t_small, *prior)
                    ready.append([his[kk], lo])
                free[b] = [lo]
            return ready

        def cols(c):
            return slice(c * 512, c * 512 + 512)

        junk_done = [[]]

        def square_of(a, o, *tokens):
            t = AC.op(lambda e: e.activation(junk, a, ACT.Square, scale=1.0 / 32, accum_out=o), *junk_done[0],
                      *tokens)
            junk_done[0] = [t]
            return t

        def norm_x(t, adds):
            q = [square_of(x[:, t, cols(c)], xpart[:, 2 * t + c:2 * t + c + 1], adds[c]) for c in range(2)]
            a = DV.op(lambda e: e.scalar_tensor_tensor(out=ms[:, t:t + 1], in0=xpart[:, 2 * t:2 * t + 1], scalar=EPS,
                                                       in1=xpart[:, 2 * t + 1:2 * t + 2], op0=ALU.add, op1=ALU.add), *q)
            return pow_half(ms[:, t:t + 1], a)

        def scale_cols(t, n):
            return [DV.op(lambda e: e.tensor_scalar(xt[:, t, cols(0)], x[:, t, cols(0)], ms[:, t:t + 1], None,
                                                    ALU.mult), n),
                    AC.op(lambda e: e.activation(xt[:, t, cols(1)], x[:, t, cols(1)], ACT.Copy,
                                                 scale=ms[:, t:t + 1]), n)]

        def post_half(t, toks, t_w):
            q, m = [], []
            for c in range(2):
                q.append(square_of(bank[2 * t + c][:], part[:, 2 * t + c:2 * t + c + 1], toks[c]))
                if c == 1:
                    a = DV.op(lambda e: e.scalar_tensor_tensor(
                        out=mp[:, t:t + 1], in0=part[:, 2 * t:2 * t + 1], scalar=EPS,
                        in1=part[:, 2 * t + 1:2 * t + 2], op0=ALU.add, op1=ALU.add), *q)
                    r = pow_half(mp[:, t:t + 1], a)
                m.append(DV.op(lambda e, c=c: e.tensor_tensor(xt[:, t, cols(c)], bank[2 * t + c][:], wbc[:, cols(c)],
                                                              ALU.mult), q[c], t_w))
                free[2 * t + c] = [m[c]]
            return [DV.op(lambda e, c=c: e.scalar_tensor_tensor(
                out=x[:, t, cols(c)], in0=xt[:, t, cols(c)], scalar=mp[:, t:t + 1], in1=x[:, t, cols(c)],
                op0=ALU.mult, op1=ALU.add), r, m[c]) for c in range(2)]

        def between(xn_of, w, dst, take):
            i0 = len(used)
            assert PLAN[i0][0] == PLAN[i0 + 1][0] == "C" and len(split) >= i0 + 2
            ready = [[] for _ in range(8)]
            ww = (wh, wl)
            took = []
            for t in range(2):
                xn = xn_of(t)
                ts_ = slice(t * 128, t * 128 + 128)
                bs = [2 * t, 2 * t + 1, work(), work()]
                tr_ = []
                for p, b in enumerate(bs):
                    PE.wait(*free[b])
                    for kk in range(2):
                        f = (lambda e, k=2 * p + kk, t=t, kk=kk, b=b: e.transpose(
                            bank[b][:, kk * 128:kk * 128 + 128], xt[:, t, k * 128:k * 128 + 128], ident[:]))
                        if kk == 1:
                            tr_.append(PE.op(f, t_id, xn[p // 2]))
                        else:
                            PE.quiet(f, t_id, xn[p // 2])
                for p, b in enumerate(bs):
                    his = [AC.op(lambda e, k=2 * p + kk, kk=kk, b=b, ts_=ts_: e.activation(
                        dst[0][:, k, ts_], bank[b][:, kk * 128:kk * 128 + 128], ACT.Copy, scale=w[:, k:k + 1]),
                        tr_[p], t_small) for kk in range(2)]
                    for kk in range(2):
                        lo = DV.op(lambda e, k=2 * p + kk, kk=kk, b=b, ts_=ts_: e.scalar_tensor_tensor(
                            out=dst[1][:, k, ts_], in0=bank[b][:, kk * 128:kk * 128 + 128], scalar=w[:, k:k + 1],
                            in1=dst[0][:, k, ts_].bitcast(F32), op0=ALU.mult, op1=ALU.subtract), his[1], t_small)
                        ready[2 * p + kk] += [his[kk], lo]
                    free[b] = [lo]
                if t == 1:
                    prep(i0 + 3)
                bo = work()
                PE.wait(*free[bo])
                for k in range(8):
                    if k % 4 == 0:
                        PE.wait(*split[i0 + k // 4])
                    h = (i0 + k // 4) % HR
                    for n, (j, i) in enumerate(((0, 0), (0, 1), (1, 0))):
                        f = (lambda e, l=dst[j][:, k, t * 128:t * 128 + 128],
                             r=ww[i][:, h, (k % 4) * 512:(k % 4) * 512 + 512], o=bank[bo][:], a=k == 0 and n == 0,
                             z=k == 7 and n == 2: e.matmul(o, l, r, start=a, stop=z))
                        if n == 2 and k in (3, 7):
                            tok = PE.op(f, *ready[k])
                            if t:
                                done(tok)
                        else:
                            PE.quiet(f, *ready[k])
                took.append((bo, tok))
                if t == 1:
                    take(0, *took[0])
                    take(1, *took[1])
            return ready

        t_x = [load(x[:, t, :], A["x"][t * 128:t * 128 + 128, :], via=SP) for t in range(2)]
        dma_unit(0)
        t_small = load(small[:], A["small"], via=SP)
        t_id = load(ident[:], A["ident"], via=SP)
        for i in range(1, RR):
            dma_unit(i)
        t_half = PO.op(lambda e: e.memset(half[:], -0.5))

        def move(eng, o, i, *tokens):
            if eng is AC:
                return AC.op(lambda e: e.copy(o, i), *tokens)
            return eng.op(lambda e: e.tensor_copy(o, i), *tokens)

        def tt(eng, o, a, b, op, *tokens):
            return eng.op(lambda e: e.tensor_tensor(o, a, b, op), *tokens)

        def ts(eng, o, a, s1, s2, op0, op1, *tokens):
            if op1 is None:
                return eng.op(lambda e: e.tensor_scalar(o, a, s1, None, op0), *tokens)
            return eng.op(lambda e: e.tensor_scalar(o, a, s1, s2, op0, op1), *tokens)

        def stt(o, a, s, b, op0, op1, *tokens):
            return DV.op(lambda e: e.scalar_tensor_tensor(out=o, in0=a, scalar=s, in1=b, op0=op0, op1=op1), *tokens)

        def act(o, i, f, *tokens, **kw):
            return AC.op(lambda e: e.activation(o, i, f, **kw), *tokens)

        def mm(o, l, r, start, stop, *tokens, tok=True, skip=False):
            if skip:
                f = lambda e: e.matmul(o, l, r, start=start, stop=stop, skip_group_check=True)
            else:
                f = lambda e: e.matmul(o, l, r, start=start, stop=stop)
            return PE.op(f, *tokens) if tok else PE.quiet(f, *tokens)

        def tr(o, i, *tokens, tok=True):
            f = lambda e: e.transpose(o, i, ident[:])
            return PE.op(f, t_id, *tokens) if tok else PE.quiet(f, t_id, *tokens)

        def bc(a, n):
            return a.unsqueeze(2).broadcast_to([128, a.shape[1], n])

        def rep(a, m):
            return a.unsqueeze(1).broadcast_to([128, m, a.shape[1]])

        H = (hh, hl)

        with ExitStack() as p1:
            cin = sb(p1, "cin", [128, 12, S + 3])
            cout = sb(p1, "cout", [128, 12, S])
            tm = sb(p1, "tm", [128, 2, 1536])
            kb = sb(p1, "kb", [128, 2, 512])
            dU = sb(p1, "dU", [128, 16, 128])
            AT = hold[:].rearrange("p (s n) -> p s n", n=128)
            tab = sb(p1, "tab", [128, 10, 128])
            gs = sb(p1, "gs", [128, 256])
            ng8 = kb[:, 0, 0:384]
            X = cin[:].rearrange("p a b -> p (a b)")[:, 0:2048].rearrange("p (s n) -> p s n", s=16)
            zz = cin[:].rearrange("p a b -> p (a b)")[:, 2048:3072].rearrange("p (t n) -> p t n", t=2)
            XT = xt[:].rearrange("p t (s n) -> p (t s) n", n=128)
            kT = cout[:].rearrange("p a s -> p (a s)")[:, 0:1024].rearrange("p (j s) -> p j s", j=4)
            kq = cout[:].rearrange("p a s -> p (a s)")[:, 1024:3072].rearrange(
                "p (j c w n) -> p j c w n", j=4, c=2, w=2)
            kd = tm[:, 0, 0:512]
            triu, nstrict, ones, near, same, delta = (tab[:, i, :] for i in range(6))
            delta = delta[:, 0:BASE]

            pa = ExitStack()
            qT = sb(pa, "qT", [128, 4, S])
            kTa = sb(pa, "kTa", [128, 4, S])
            va = sb(pa, "va", [128, 2, 512])
            P = sb(pa, "P", [128, 2, 384])
            PT = sb(pa, "PT", [128, 2, 384])
            T = sb(pa, "T", [128, 2, 384])
            t_tab = load(tab[:], A["tab"].rearrange("p (a n) -> p a n", n=128))
            oh = cout[0:32, 0:2, :].rearrange("p a s -> p (a s)")[:, 0:384]
            ng = cout[0:8, 2:4, :].rearrange("p a s -> p (a s)")[:, 0:384]
            rb = cout[0:32, 4, 0:8]
            rrow = cout[0:8, 5:7, :].rearrange("p a s -> p (a s)")[:, 0:384]
            t_oh = load(oh, A["onehot"])
            t_ng = load(ng, A["neg"])
            t_rb = load(rb, A["rbT"])
            def load_T(h, *tokens):
                dst = T[:, h % 2, :]
                skew = A["skew"]
                a = bass.AP(skew.tensor, h * 128 * 384 + 127, [[383, 128], [1, 256]])
                b_ = bass.AP(skew.tensor, h * 128 * 384 + 255, [[383, 128], [1, 128]])
                s = sem(f"T{h}")
                PO.quiet(lambda e: e.dma_start(dst[:, 128:384], a).then_inc(s, 16), t_skew, *tokens)
                PO.quiet(lambda e: e.dma_start(dst[:, 0:128], b_).then_inc(s, 16))
                return s, 32

            sx = [square_x(t, t_x[t]) for t in range(2)]
            xn = [scale_cols(t, rstd_x(t, sx[t])) for t in range(2)]
            prep(0)
            ready = turn_x(par("pre_mix"), H, [], xn)

            b = work()
            t = mm(bank[b][0:8, 0:384], rb, oh, True, True, t_oh, t_rb, *free[b])
            t_row = tt(DV, rrow, bank[b][0:8, 0:384], ng, ALU.add, t, t_ng)
            free[b] = [t_row]
            t_scr = load(A["scr"], rrow, t_row)
            t_skew = load(A["skew"], bass.AP(A["scr"].tensor, 0, [[384, 8], [0, 128], [1, 384]]), t_scr)

            ab = dU[:, 0:2, :].rearrange("p a n -> p (a n)")
            b, t = b_unit(H, ready, "Z")
            t_ab = move(AC, ab, bank[b][:, 0:S], t)
            free[b] = [t_ab]
            sa = gs[:, 0:16].rearrange("p (c h) -> p c h", c=2)
            eb = gs[:, 16:32].rearrange("p (c h) -> p c h", c=2)
            sn = gs[:, 32:48]
            sa1, eb1 = gs[:, 0:16], gs[:, 16:32]
            ea = gs[:, 48:56]
            beta = gs[:, 56:72]
            graw = gs[:, 72:88]
            gc = gs[:, 88:104]
            eg = gs[:, 104:120]
            kdx = gs[:, 120:136]

            def gates():
                b = work()
                tr(bank[b][:, 0:128], ab[:, 0:128], t_ab, *free[b], tok=False)
                t = tr(bank[b][:, 128:256], ab[:, 128:256])
                pv = bank[b][:, 0:256].rearrange("p (c n) -> p c n", c=2)
                t1 = tt(DV, sa, pv[:, :, 112:120], rep(par("dt_bias"), 2), ALU.add, t, t_small)
                tb = move(DV, eb, pv[:, :, 120:128], t)
                free[b] = [tb]
                t2 = stt(sn, sa1, -1.0, sa1, ALU.mult, ALU.min, t1)
                t2 = act(sn, sn, ACT.Exp, t2)
                tb = act(eb1, eb1, ACT.Exp, tb, scale=-1.0)
                t3 = act(ea, par("A_log"), ACT.Exp, t_small)
                t2 = act(sn, sn, ACT.Ln, t2, bias=1.0)
                tb = ts(DV, eb1, eb1, 1.0, None, ALU.add, None, tb)
                t_beta = DV.op(lambda e: e.reciprocal(beta, eb1), tb)
                t2 = stt(sn, sa1, 0.0, sn, ALU.max, ALU.add, t2)
                t_g = stt(graw.rearrange("p (c h) -> p c h", c=2), sn.rearrange("p (c h) -> p c h", c=2), -1.0,
                          rep(ea, 2), ALU.mult, ALU.mult, t2, t3)
                return t_beta, t_g

            def sums(t_g):
                b = work()
                mm(bank[b][:, 0:16], triu, graw, True, True, t_g, t_tab, *free[b], tok=False)
                t = mm(bank[b][:, 16:32], ones, graw, True, True)
                t_gc = move(DV, gs[:, 88:104], bank[b][:, 0:16], t)
                t = tt(DV, kdx, bank[b][:, 16:32], gc, ALU.subtract, t_gc)
                free[b] = [t]
                t_eg = act(eg, gc, ACT.Exp, t_gc)
                t_kdx = act(kdx, kdx, ACT.Exp, t)
                return t_gc, t_eg, t_kdx

            def decays(g, t_g, t_gc):
                b = work()
                PE.wait(*free[b])
                for i in range(4):
                    s = 4 * g + i
                    t = mm(bank[b][:, i * 128:i * 128 + 128], graw[:, s:s + 1].broadcast_to([128, 128]), triu,
                           True, True, t_g)
                for i in range(4):
                    s = 4 * g + i
                    t_ = ts(DV, dU[:, s, :], bank[b][:, i * 128:i * 128 + 128], gc[:, s:s + 1], 0.0,
                            ALU.subtract, ALU.min, t, t_gc)
                free[b] = [t_]
                return t_

            t_pad = PO.op(lambda e: e.memset(cin[:, :, 0:3], 0.0))
            cw = par("conv1").rearrange("p (a k) -> p a k", k=4)
            t_c = []
            t_silu = []
            t_dec = []

            def silu_of(u):
                t_silu.append(act(cout[:, 2 * u:2 * u + 2, :], cout[:, 2 * u:2 * u + 2, :], ACT.Silu,
                                  *t_c[2 * u:2 * u + 2]))

            for u in range(6):
                b, t = b_unit(H, ready)
                t = move(AC, cin[:, 2 * u:2 * u + 2, 3:], bank[b][:].rearrange("p (a s) -> p a s", a=2), t)
                free[b] = [t]
                t2s = [t, t]
                for k in range(4):
                    for i in range(2):
                        a = 2 * u + i
                        if k == 0:
                            t2s[i] = act(cout[:, a, :], cin[:, a, 0:S], ACT.Copy, t, t_pad, t_scr, t_row,
                                         scale=cw[:, a, 0:1])
                        else:
                            t2s[i] = stt(cout[:, a, :], cin[:, a, k:k + S], cw[:, a, k:k + 1], cout[:, a, :],
                                         ALU.mult, ALU.add, t2s[i])
                t_c += t2s
                if u:
                    silu_of(u - 1)
                if u == 5:
                    silu_of(5)
                if u == 0:
                    t_beta, t_g = gates()
                elif u == 1:
                    t_gc, t_eg, t_kdx = sums(t_g)

            def decay_masks():
                t_ = act(dU[:], dU[:], ACT.Exp, *t_dec)
                t_dU = tt(PO, dU[:], dU[:], rep(triu, 16), ALU.mult, t_, t_tab)
                return t_dU, tt(PO, AT, dU[:], rep(nstrict, 16), ALU.mult, t_dU)

            t_qk = []

            def att_unit(u):
                b, t = b_unit(H, ready)
                dst = (qT, kTa)[u // 2]
                t = act(dst[:, 2 * (u % 2):2 * (u % 2) + 2, :], bank[b][:].rearrange("p (a s) -> p a s", a=2), ACT.Copy,
                        t, scale=(0.125, 1.0)[u // 2])
                free[b] = [t]
                t_qk.append(t)

            t_tm = {}
            sq = X[:].rearrange("p s n -> p (s n)")
            t_sq = []

            def token_major(w_):
                for c in range(2):
                    b = work()
                    PE.wait(*free[b])
                    for a in range(4):
                        t = tr(bank[b][:, a * 128:a * 128 + 128], cout[:, 4 * w_ + a, c * 128:c * 128 + 128],
                               t_silu[2 * w_ + a // 2])
                    t_tm[w_, c] = move(AC, tm[:, c, w_ * 512:w_ * 512 + 512], bank[b][:], t)
                    free[b] = [t_tm[w_, c]]
                    if w_ < 2:
                        o = (c * 2 + w_) * 512
                        t2 = act(sq[:, o:o + 512], bank[b][:], ACT.Square, t, *t_c)
                        t_sq.append(t2)
                        free[b] = [t2]

            att_unit(0)
            token_major(0)
            token_major(1)
            att_unit(1)
            t_dec += [decays(g, t_g, t_gc) for g in (0, 1, 2, 3)]
            t_dU, t_dS = decay_masks()
            rn = gs[:, 136:168]
            t = DV.op(lambda e: e.tensor_reduce(rn, sq.rearrange("p (s n) -> p s n", n=64), AXX, ALU.add), *t_sq)
            t = ts(DV, rn, rn, EPS, None, ALU.add, None, t)
            t = act(rn, rn, ACT.Sqrt, t)
            t = DV.op(lambda e: e.reciprocal(rn, rn), t)
            rq = rn.rearrange("p (c w h) -> p c w h", c=2, w=2)[:, :, 0, :]
            t_rn = ts(DV, rq, rq, 0.125, None, ALU.mult, None, t)
            t_n = []
            t_kb = []
            t_vb = []
            for c in range(2):
                o = tm[:, c, 0:1024].rearrange("p (s n) -> p s n", n=64)
                t_n.append(tt(DV, o, o, bc(rn[:, 16 * c:16 * c + 16], 64), ALU.mult, t_rn, t_tm[0, c], t_tm[1, c]))
                t_kb.append(tt(DV, kb[:, c, :].rearrange("p (s n) -> p s n", n=64),
                               tm[:, c, 512:1024].rearrange("p (s n) -> p s n", n=64),
                               bc(beta[:, 8 * c:8 * c + 8], 64), ALU.mult, t_n[c], t_beta))
            att_unit(2)
            token_major(2)
            for c in range(2):
                o = tm[:, c, 1024:1536].rearrange("p (s n) -> p s n", n=64)
                t_vb.append(tt(PO, o, o, bc(beta[:, 8 * c:8 * c + 8], 64), ALU.mult, t_tm[2, c], t_beta))
            att_unit(3)

            t_kT = []
            for c in range(2):
                for w_, (src, dst, dep) in enumerate((
                        (tm[:, c, 512:1024], kT[:, :, c * 128:c * 128 + 128], t_n[c]),
                        (kb[:, c, :], kq[:, :, c, 0, :], t_kb[c]),
                        (tm[:, c, 0:512], kq[:, :, c, 1, :], t_n[c]))):
                    b = work()
                    PE.wait(*free[b])
                    for a in range(4):
                        t = tr(bank[b][:, a * 128:a * 128 + 128], src[:, a * 128:a * 128 + 128], dep)
                    t = move(AC, dst, bank[b][:].rearrange("p (a n) -> p a n", a=4), t)
                    free[b] = [t]
                    t_kT.append(t)
            t_kd = tt(PO, kd.rearrange("p (h n) -> p h n", n=64), tm[:, 0, 512:1024].rearrange("p (h n) -> p h n", n=64),
                      bc(kdx[:, 0:8], 64), ALU.mult, t_kdx, *t_kT)

            t_v = []
            for c, b, t in c_block(H, ready):
                t_v.append(move(AC, va[:, c, :], bank[b][:], t))
                free[b] = [t_v[-1]]


            ready_c = [None] * 8
            tT = [load_T(0), load_T(1)]
            tP, tPV, tN, tPT = [None] * 8, [None] * 8, [None] * 8, [None] * 8

            def att_scores(h):
                j, p0, pp = h // 2, 64 * (h % 2), h % 2
                b = work()
                PE.wait(*free[b])
                mm(bank[b][:, 0:128], qT[p0:p0 + 64, j, 0:128], kTa[p0:p0 + 64, j, 0:128], True, True, *t_qk,
                   tok=False)
                t = mm(bank[b][:, 128:384], qT[p0:p0 + 64, j, 128:256], kTa[p0:p0 + 64, j, :], True, True)
                dep = [tP[h - 2]] if h >= 2 else []
                t = tt(DV, P[:, pp, :], bank[b][:, 0:384], T[:, pp, :], ALU.add, t, tT[h], *dep)
                free[b] = [t]
                if h < 6:
                    tT.append(load_T(h + 2, t))
                nm = gs[:, 168 + 4 * pp:170 + 4 * pp]
                sm_ = gs[:, 170 + 4 * pp:172 + 4 * pp]
                parts = ((0, 128), (128, 384))
                te = []
                for i, (lo, hi) in enumerate(parts):
                    t2 = DV.op(lambda e, i=i, lo=lo, hi=hi: e.tensor_reduce(
                        nm[:, i:i + 1], P[:, pp, lo:hi], AXX, ALU.max), t, *dep)
                tm_ = ts(DV, nm, nm, -1.0, None, ALU.mult, None, t2)
                for i, (lo, hi) in enumerate(parts):
                    te.append(act(P[:, pp, lo:hi], P[:, pp, lo:hi], ACT.Exp, tm_, *dep, bias=nm[:, i:i + 1],
                                  accum_out=sm_[:, i:i + 1]))
                t2 = DV.op(lambda e: e.reciprocal(sm_, sm_), *te)
                tN[h] = [ts(DV, P[:, pp, lo:hi], P[:, pp, lo:hi], sm_[:, i:i + 1], None, ALU.mult, None, t2)
                         for i, (lo, hi) in enumerate(parts)]

            def att_turn(h):
                pp = h % 2
                b = work()
                PE.wait(*free[b])
                for i in range(3):
                    t = tr(bank[b][:, i * 128:i * 128 + 128], P[:, pp, i * 128:i * 128 + 128], *tN[h])
                tP[h] = t
                dep = [tPV[h - 2]] if h >= 2 else []
                tPT[h] = move(AC, PT[:, pp, :], bank[b][:, 0:384], t, *dep)
                free[b] = [tPT[h]]

            def att_out(h):
                j, p0, pp = h // 2, 64 * (h % 2), h % 2
                b = 3
                if pp == 0:
                    PE.wait(*free[b])
                vs = va[:, :, h * 64:h * 64 + 64]
                mm(bank[b][p0:p0 + 64, 0:256], vs[:, 0, :], PT[:, pp, 0:256], True, False, tPT[h], *t_v, tok=False)
                tPV[h] = mm(bank[b][p0:p0 + 64, 128:256], vs[:, 1, :], PT[:, pp, 256:384], False, True)
                if pp == 1:
                    th = AC.op(lambda e: e.copy(hh[:, j, :], bank[b][:, 0:256]), tPV[h], w_in_read)
                    tl = tt(DV, hl[:, j, :], bank[b][:, 0:256], hh[:, j, :].bitcast(F32), ALU.subtract, th, w_in_read)
                    free[b] = [tl]
                    ready_c[j] = [th, tl]

            steps = []
            for n in range(11):
                if 0 <= n - 2 < 8:
                    steps.append((att_turn, n - 2))
                if n < 8:
                    steps.append((att_scores, n))
                if 0 <= n - 3 < 8:
                    steps.append((att_out, n - 3))

            def att(n):
                for _ in range(n):
                    if steps:
                        f, h = steps.pop(0)
                        f(h)

            t_AT = []
            t_near = []
            blk = XT
            for g in range(8):
                b = work()
                PE.wait(*free[b])
                s0 = 8 * (g // 4) + 4 * (g % 4 // 2) + g % 2
                for i in range(2):
                    s = s0 + 2 * i
                    c, h = s // 8, s % 8
                    p0 = 64 * (h % 2)
                    t = mm(bank[b][:, i * 256:i * 256 + 256], kT[p0:p0 + 64, h // 2, c * 128:c * 128 + 128],
                           kq[p0:p0 + 64, h // 2, c, :, :].rearrange("p w n -> p (w n)"), True, True, *t_kT)
                v = bank[b][:].rearrange("p (i w n) -> p i w n", i=2, w=2)
                at, du = AT[:, s0:s0 + 3:2, :], dU[:, s0:s0 + 3:2, :]
                t1 = tt(DV, at, v[:, :, 0, :], at, ALU.mult, t, t_dS)
                t_at = tt(DV, du, v[:, :, 1, :], du, ALU.mult, t, t_dU, t_dS)
                free[b] = [t_at]
                t_AT.append(t1)
                if g in (2, 6):
                    att(1)
                if g == 3:
                    t_near.append(tt(PO, blk[:, 0:8, :], AT[:, 0:8, :], rep(near, 8), ALU.mult, *t_AT))
            t_att = t_at

            t_near.append(tt(DV, blk[:, 8:16, :], AT[:, 8:16, :], rep(near, 8), ALU.mult, *t_AT))
            ab_ = ng8[:, 0:128].rearrange("p (s i) -> p s i", i=BASE)
            for c in range(2):
                t = DV.op(lambda e, c=c: e.tensor_reduce(
                    ab_[:, 8 * c:8 * c + 8], blk[:, 8 * c:8 * c + 8, :].rearrange("p s (b i) -> p s i b", i=BASE), AXX,
                    ALU.add), t_near[c], *t_kT)
            spread = sq[:, 0:1024].rearrange("p (n j) -> p n j", j=BASE)
            t_sp = tt(DV, spread, bc(ng8[:, 0:128], BASE), rep(delta, 128), ALU.mult, t, *t_sq, *t_n)
            t_A = tt(PO, AT, AT, rep(ident[:], 16), ALU.add, *t_near, *t_AT)
            tz = []
            co = sq[:, 1024:2048]
            t_co = []

            def hand_out():
                for i in range(2):
                    b = i
                    t = mm(bank[b][:], same, sq[:, i * 512:i * 512 + 512], True, True, t_sp, *free[b])
                    t_co.append(move(AC, co[:, i * 512:i * 512 + 512], bank[b][:], t))
                    free[b] = [t_co[-1]]

            def between_z():
                hand_out()
                co4 = co.rearrange("p (s i j) -> p s i j", i=BASE, j=BASE)
                xc = ng8[:, 128:256].rearrange("p (s i) -> p s i", i=BASE)
                pr = ng8[:, 256:384].rearrange("p (s i) -> p s i", i=BASE)
                t = move(DV, xc, rep(delta, 16), *t_co)
                for j in range(BASE - 1):
                    n = BASE - 1 - j
                    t = tt(DV, pr[:, :, 0:n], co4[:, :, j + 1:, j], xc[:, :, j:j + 1].broadcast_to([128, 16, n]),
                           ALU.mult, t)
                    t = tt(DV, xc[:, :, j + 1:], xc[:, :, j + 1:], pr[:, :, 0:n], ALU.add, t)
                t = tt(DV, XT.rearrange("p s (b i) -> p s b i", i=BASE),
                          xc.unsqueeze(2).broadcast_to([128, 16, 16, BASE]),
                          same.rearrange("p (b i) -> p b i", i=BASE).unsqueeze(1).broadcast_to([128, 16, 16, BASE]),
                          ALU.mult, t)
                got["XT"] = t
                att(0)

            got = {}
            zb_ = c_block(H, ready, between_z)
            t_XT = got["XT"]
            for c, b, t in zb_:
                tz.append(act(zz[:, c, :], bank[b][:], ACT.Silu, t, *t_c, *t_sq))
                free[b] = [tz[-1]]
            zw = [tt(PO, zz[:, c, :].rearrange("p (h n) -> p h n", n=64), zz[:, c, :].rearrange("p (h n) -> p h n", n=64),
                     rep(par("gdn_w"), 8), ALU.mult, tz[c], t_small) for c in range(2)]
            w_in_read = PE.now()

            U0 = kb[:].rearrange("p c (s n) -> p (c s) n", n=128)
            U1 = kT.rearrange("p j (s n) -> p (j s) n", n=128)
            Ug = (U0[:, 0:4, :], U0[:, 4:8, :], U1[:, 0:4, :], U1[:, 4:8, :])
            vn = tm[:, 1, 0:512]
            S1 = tm[:, 1, 512:768]
            t_X = []
            t_XTg = [t_XT] * 4
            for g in range(4):
                b = work()
                PE.wait(*free[b])
                for i in range(4):
                    t = tr(bank[b][:, i * 128:i * 128 + 128], XT[:, 4 * g + i, :], t_XT)
                t = move(AC, X[:, 4 * g:4 * g + 4, :], bank[b][:].rearrange("p (a n) -> p a n", a=4), t, *t_sq,
                         *t_n)
                free[b] = [t]
                t_X.append(t)
            att(3)
            tb_ = 0

            def turn_inverse(g):
                b = work()
                PE.wait(*free[b])
                for i in range(4):
                    t = tr(bank[b][:, i * 128:i * 128 + 128], X[:, 4 * g + i, :], t_X[g])
                t_XTg[g] = move(AC, XT[:, 4 * g:4 * g + 4, :], bank[b][:].rearrange("p (a n) -> p a n", a=4), t)
                free[b] = [t_XTg[g]]

            for l, s_ in enumerate(LEVELS):
                mask = tab[:, 6 + l, :]
                final = l == len(LEVELS) - 1
                tu = []
                for g in range(4):
                    b = tb_ % 3
                    tb_ += 1
                    PE.wait(*free[b])
                    for i in range(4):
                        s = 4 * g + i
                        t = mm(bank[b][:, i * 128:i * 128 + 128], AT[:, s, :], X[:, s, :], True, True, t_X[g], t_A)
                    t = tt(DV, Ug[g], bank[b][:].rearrange("p (a n) -> p a n", a=4), rep(mask, 4),
                           ALU.mult, t, *t_kT)
                    free[b] = [t]
                    tu.append(t)
                    if l:
                        turn_inverse(g)
                att(2)
                for g in range(4):
                    b = work()
                    PE.wait(*free[b])
                    for i in range(4):
                        s = 4 * g + i
                        o = bank[b][:, i * 128:i * 128 + 128]
                        if final:
                            t = mm(o, Ug[g][:, i, :], XT[:, s, :], True, True, tu[g], t_XTg[g])
                        else:
                            t = mm(o, XT[:, s, :], Ug[g][:, i, :], True, True, tu[g], t_XTg[g])
                    dst, tl = (XT, t_XTg) if final else (X, t_X)
                    tl[g] = move(AC, dst[:, 4 * g:4 * g + 4, :], bank[b][:].rearrange("p (a n) -> p a n", a=4), t)
                    free[b] = [tl[g]]
                att(2)
            while steps:
                att(1)
            att_done = [PE.now(), AC.now(), DV.now()]
            pa.close()
            t_wbc = load(wbc, A["post_mix"].partition_broadcast(128), *att_done)

            ob = X[:].rearrange("p s n -> p (s n)")
            o_all = ob[:, 0:1024].rearrange("p (c n) -> p c n", c=2)
            qs = ob[:, 1024:1536]
            r1 = ob[:, 1536:2048]
            v64 = lambda a: a.rearrange("p (h n) -> p h n", n=64)
            pair = lambda a, w: v64(a).rearrange("p (j w) n -> p j w n", w=2)[:, :, w, :]
            eg1 = eg[:, 8:16].rearrange("p (j w) -> p j w", w=2)
            acc = [[0, 1], [2, 3]]
            b = work()
            PE.wait(*free[b])
            for h in range(8):
                t = mm(bank[b][:, h * 64:h * 64 + 64], XT[:, h, :], tm[:, 0, 1024 + h * 64:1024 + h * 64 + 64],
                       True, True, *t_XTg, *t_vb)
            t_v0 = move(AC, vn, bank[b][:], t)
            free[b] = [t_v0]

            def state():
                b = work()
                PE.wait(*free[b])
                for h in range(8):
                    p0 = 64 * (h % 2)
                    t = mm(bank[b][p0:p0 + 64, (h // 2) * 64:(h // 2) * 64 + 64], kd[:, h * 64:h * 64 + 64],
                           vn[:, h * 64:h * 64 + 64], True, True, t_v0, t_kd)
                got["s1"] = move(AC, S1, bank[b][:, 0:256], t)
                free[b] = [got["s1"]]
                bo = work()
                PE.wait(*free[bo])
                for h in range(8):
                    t = mm(bank[bo][:, h * 64:h * 64 + 64], dU[:, h, :], vn[:, h * 64:h * 64 + 64], True, True, t_att)
                got["o0"] = t
                got["oa"] = move(DV, o_all[:, 0, :], bank[bo][:], t)
                free[bo] = [got["oa"]]

            t_qs, t_rr = [], []

            def onto_state():
                for which, dst, acc_ in ((0, r1, t_rr), (1, qs, t_qs)):
                    for w_ in range(2):
                        b = work()
                        PE.wait(*free[b])
                        p0 = 64 * w_
                        for j in range(4):
                            t = mm(bank[b][:, j * 64:j * 64 + 64], kq[p0:p0 + 64, j, 1, which, :],
                                   S1[p0:p0 + 64, j * 64:j * 64 + 64], True, True, got["s1"])
                        t = tt(DV, pair(dst, w_), v64(bank[b][:, 0:256]), bc(eg1[:, :, w_], 64), ALU.mult, t, t_eg)
                        free[b] = [t]
                        acc_.append(t)
                    if which == 0:
                        got["r1"] = tt(DV, r1, tm[:, 1, 1024:1536], r1, ALU.subtract, *t_rr, *t_vb)

            def second():
                b = work()
                PE.wait(*free[b])
                for h in range(8):
                    t = mm(bank[b][:, h * 64:h * 64 + 64], XT[:, 8 + h, :], r1[:, h * 64:h * 64 + 64], True, True,
                           got["r1"])
                got["v1"] = move(AC, vn, bank[b][:], t, got["o0"])
                free[b] = [got["v1"]]

            so = gs[:, 176:192]
            osq = kb[:].rearrange("p c n -> p (c n)")
            t_y = []

            def gated_norm(c, t):
                o = o_all[:, c, :]
                sq_, so_ = osq[:, c * 512:c * 512 + 512], so[:, c * 8:c * 8 + 8]
                t = act(sq_, o, ACT.Square, t, scale=0.125)
                t = DV.op(lambda e: e.tensor_reduce(so_, v64(sq_), AXX, ALU.add), t)
                t = ts(DV, so_, so_, EPS, None, ALU.add, None, t)
                t = act(so_, so_, ACT.Sqrt, t)
                t = DV.op(lambda e: e.reciprocal(so_, so_), t)
                t = tt(DV, v64(o), v64(o), bc(so_, 64), ALU.mult, t)
                t_y.append(tt(DV, o, o, zz[:, c, :], ALU.mult, t, *zw))

            def after_state():
                state()
                onto_state()
                gated_norm(0, got["oa"])

            a_unit("A", H, ready_c, (0, 1), acc, True, False, hooks={0: after_state, 2: second})
            def turn_y(c):
                b = work()
                PE.wait(*free[b])
                for a in range(4):
                    t = tr(bank[b][:, a * 128:a * 128 + 128], o_all[:, c, a * 128:a * 128 + 128], t_y[c])
                v = bank[b][:].rearrange("p (a s) -> p a s", a=4)
                ts_ = slice(c * 128, c * 128 + 128)
                th = AC.op(lambda e: e.copy(hh[:, 4:8, ts_], v), t, w_in_read)
                tl = tt(DV, hl[:, 4:8, ts_], v, hh[:, 4:8, ts_].bitcast(F32), ALU.subtract, th)
                free[b] = [tl]
                for k in range(4, 8):
                    ready_c[k] = (ready_c[k] or []) + [th, tl]

            turn_y(0)
            b = work()
            PE.wait(*free[b])
            for h in range(8):
                t = mm(bank[b][:, h * 64:h * 64 + 64], dU[:, 8 + h, :], vn[:, h * 64:h * 64 + 64], True, True,
                       got["v1"])
            t = tt(DV, o_all[:, 1, :], bank[b][:], qs, ALU.add, t, *t_qs)
            free[b] = [t]
            prep(len(used) + AHEAD)
            gated_norm(1, t)
            a_unit("A", H, ready_c, (2, 3), acc, False, False, hooks={})
            toks = a_pair(H, ready_c, (4, 5, 6, 7), acc, mid=lambda: turn_y(1))
        with ExitStack() as p2:
            up = sb(p2, "up", [128, 2, 512])
            rl = sb(p2, "rl", [128, 2, 512])
            sqb = sb(p2, "sqb", [128, 2, 512])
            mh = sb(p2, "mh", [128, 6, S], FR)
            ml = sb(p2, "ml", [128, 6, S], FR)
            mready = [None] * 32
            down = {}
            t_up = []

            def take_up(t, b, tok):
                t_up.append(move(AC, up[:, t, :], bank[b][:], tok))
                free[b] = [t_up[-1]]

            ready = between(lambda t: scale_cols(t, norm_x(t, post_half(t, toks[t], t_wbc))), par("pre_mlp"), H,
                            take_up)
            t_wbc = load(wbc, A["post_mlp"].partition_broadcast(128), DV.now())

            def mlp_down(i):
                q = 2 * (i % 3)
                m = (mh[:, q:q + 2, :], ml[:, q:q + 2, :])
                down[i] = a_unit("A", m, mready[2 * i:2 * i + 2], (0, 1), acc, i == 0, False)

            def square(i, b, t):
                q, r = i % 2, i % 3
                dep = [down[i - 3][1]] if i >= 3 else []
                r_, s_ = rl[:, q, :], sqb[:, q, :]
                ho = mh[:, 2 * r:2 * r + 2, :].rearrange("p a s -> p (a s)")
                lo = ml[:, 2 * r:2 * r + 2, :].rearrange("p a s -> p (a s)")
                t1 = act(r_, bank[b][:], ACT.Relu, t, *([mready[2 * i - 4][0], mready[2 * i - 4][1]] if i >= 2 else []))
                free[b] = [t1]
                t2 = act(ho, r_, ACT.Square, t1, *dep)
                t3 = tt(DV, s_, r_, r_, ALU.mult, t1)
                t4 = tt(DV, lo, s_, ho.bitcast(F32), ALU.subtract, t2, t3, *dep)
                mready[2 * i] = mready[2 * i + 1] = [t2, t4]

            def turn_up():
                for u in range(2):
                    bu = work()
                    PE.wait(*free[bu])
                    for a in range(2):
                        for n in range(2):
                            tu = tr(bank[bu][:, a * S + n * 128:a * S + n * 128 + 128],
                                    up[:, n, (2 * u + a) * 128:(2 * u + a) * 128 + 128], *t_up)
                    square(u, bu, tu)

            for i in range(2, 16):
                b, t = b_unit(H, ready, mid=turn_up if i == 2 else None)
                square(i, b, t)
                mlp_down(i - 2)
            order = [2 * (14 % 3), 2 * (14 % 3) + 1, 2 * (15 % 3), 2 * (15 % 3) + 1]
            mr = [None] * 6
            for n, k in enumerate(order):
                mr[k] = mready[28 + n]
            toks = a_pair((mh, ml), mr, order, acc)

        with ExitStack() as p3:
            ya = sb(p3, "ya", [128, 2, D])
            Dm = sb(p3, "Dm", [128, 4, 512])
            vv = sb(p3, "vv", [128, 2, 512])
            pc = ExitStack()
            qr = sb(pc, "qr", [128, 8, S])
            kr = sb(pc, "kr", [128, 8, S])
            yh = sb(pc, "yh", [128, 8, S], FR)
            yl = sb(pc, "yl", [128, 8, S], FR)
            uc = sb(pc, "uc", [128, 2, 2, S + 2])
            gcv = sb(pc, "gcv", [128, 2, 2, S])
            cv = sb(pc, "cv", [128, 2, 2, S])
            rope = sb(pc, "rope", [128, 2, S])
            ra = sb(pc, "ra", [128, 2, 2, 512])
            tv0 = []

            def take_v(t, b, tok):
                tv0.append(move(AC, vv[:, t, :], bank[b][:], tok))
                free[b] = [tv0[-1]]

            ready = between(lambda t: scale_cols(t, norm_x(t, post_half(t, toks[t], t_wbc))), par("g_mix"), H, take_v)
            phase = [PE.now(), AC.now(), DV.now(), PO.now()]
            dist = ra[:, 0, :, :]
            t_dist = load(dist, A["dist"].rearrange("p (a n) -> p a n", a=2), *phase)
            t_rope = load(rope[:], A["rope"].rearrange("p (a n) -> p a n", a=2), *phase)
            AC.wait(*phase)
            DV.wait(*phase)
            PO.wait(*phase)

            t_z = PO.op(lambda e: e.memset(uc[:], 0.0))
            cw = par("conv2").rearrange("p (a k) -> p a k", k=3)
            yready = []
            last = [[], []]
            lg = st[:, 16:24]
            sp_ = st[:, 24:32]

            def log_decays():
                dec = small[:, SM["dec_f"][0]:SM["dec_f"][0] + 8]
                t1 = ts(DV, lg, dec, -1.0, None, ALU.mult, None, t_small)
                t2 = stt(sp_, lg, -1.0, lg, ALU.mult, ALU.min, t1)
                t2 = act(sp_, sp_, ACT.Exp, t2)
                t2 = act(sp_, sp_, ACT.Ln, t2, bias=1.0)
                t2 = stt(sp_, lg, 0.0, sp_, ALU.max, ALU.add, t2)
                return ts(DV, lg, sp_, -1.0, None, ALU.mult, None, t2)

            def decay_of(h, t_lg):
                t = ts(DV, Dm[:, h, :], dist[:, 0, :], lg[:, h:h + 1], None, ALU.mult, None, t_lg, t_dist)
                t = stt(Dm[:, h, :], dist[:, 1, :], lg[:, 4 + h:5 + h], Dm[:, h, :], ALU.mult, ALU.add, t)
                return act(Dm[:, h, :], Dm[:, h, :], ACT.Exp, t)

            t_D = []
            for i in range(4):
                q = i % 2
                b, t = b_unit(H, ready, k_outer=i == 0)
                v = bank[b][:].rearrange("p (a s) -> p a s", a=2)
                t_xc = move(AC, gcv[:, q], v, t, *last[q])
                free[b] = [t_xc]
                b, t = b_unit(H, ready)
                v = bank[b][:].rearrange("p (a s) -> p a s", a=2)
                t_u = tt(DV, uc[:, q, :, 1:S + 1], v, gcv[:, q], ALU.mult, t, t_xc, t_z, *last[q])
                free[b] = [t_u]
                t2s = [t_u, t_u]
                for k in range(3):
                    for a in range(2):
                        w_ = cw[:, 2 * i + a, :]
                        if k == 0:
                            t2s[a] = ts(DV, cv[:, q, a, :], uc[:, q, a, 0:S], w_[:, 0:1], None, ALU.mult, None, t_u,
                                        *last[q])
                        else:
                            t2s[a] = stt(cv[:, q, a, :], uc[:, q, a, k:k + S], w_[:, k:k + 1], cv[:, q, a, :],
                                         ALU.mult, ALU.add, t2s[a])
                b, t = b_unit(H, ready)
                v = bank[b][:].rearrange("p (a s) -> p a s", a=2)
                t = tt(DV, cv[:, q], cv[:, q], v, ALU.mult, t, *t2s)
                free[b] = [t]
                th = AC.op(lambda e, i=i, q=q: e.copy(yh[:, 2 * i:2 * i + 2, :], cv[:, q]), t)
                tl = tt(DV, yl[:, 2 * i:2 * i + 2, :], cv[:, q], yh[:, 2 * i:2 * i + 2, :].bitcast(F32), ALU.subtract,
                        th)
                yready += [[th, tl]] * 2
                last[q] = [tl]
                if i == 0:
                    t_lg = log_decays()
                t_D.append(decay_of(i, t_lg))

            t_P = []
            tk = {}
            rdep = [t_D, t_D]

            def rotate(h, w_):
                dst = (qr, kr)[w_]
                b, t = b_unit(H, ready)
                v = bank[b][:].rearrange("p (a s) -> p a s", a=2)
                c_, s_ = (rep(rope[:, n, :], 2) for n in range(2))
                va_ = ra[:, w_, 0, :].rearrange("p (a s) -> p a s", a=2)
                vb_ = ra[:, w_, 1, :].rearrange("p (a s) -> p a s", a=2)
                t1 = tt(DV, va_, v, c_, ALU.mult, t, t_rope, *rdep[w_])
                t2 = tt(DV, vb_, v, s_, ALU.mult, t, *rdep[w_])
                free[b] = [t2]
                t3 = tt(PO, dst[:, 2 * h, :], va_[:, 0], vb_[:, 1], ALU.subtract, t1, t2)
                t4 = tt(PO, dst[:, 2 * h + 1, :], va_[:, 1], vb_[:, 0], ALU.add, t1, t2)
                rdep[w_] = [t3, t4]
                tk[h, w_] = [t3, t4]

            def scores(h):
                b = work()
                PE.wait(*free[b])
                for m in range(2):
                    for dk in range(2):
                        t = mm(bank[b][:, m * S:m * S + S], kr[:, 2 * h + dk, m * 128:m * 128 + 128],
                               qr[:, 2 * h + dk, :], dk == 0, dk == 1, *tk[h, 0], *tk[h, 1])
                t = stt(Dm[:, h, :], bank[b][:], 1.0 / 16, Dm[:, h, :], ALU.mult, ALU.mult, t, t_D[h])
                free[b] = [t]
                t_P.append(t)

            t_ya = []
            for h in range(4):
                rotate(h, 0)
                if h >= 1:
                    scores(h - 1)
                rotate(h, 1)
                if h == 0:
                    Y = (yh, yl)
                    for k in range(4):
                        tya = a_unit("A", Y, yready, (2 * k, 2 * k + 1), acc, k == 0, k == 3)
                    for tok in range(2):
                        for c in range(2):
                            t2 = move(AC, ya[:, tok, c * 512:c * 512 + 512], bank[2 * tok + c][:], tya[tok])
                            free[2 * tok + c] = [t2]
                            t_ya.append(t2)

            def c_move(dst, deps):
                o = []
                for c, b, t in c_block(H, ready):
                    o.append(move(AC, dst[:, c, :], bank[b][:], t, *deps))
                    free[b] = [o[-1]]
                return o

            tv = tv0
            gate0 = b_unit(H, ready)
            scores(3)
            conv_done = [PE.now(), AC.now(), DV.now(), PO.now()]
            pc.close()
            gt = sb(p3, "gt", [128, 4, S])
            rt = sb(p3, "rt", [128, 2, 512])
            ry = sb(p3, "ry", [128, 4, S])
            rh = sb(p3, "rh", [128, 4, S], FR)
            rlo = sb(p3, "rlo", [128, 4, S], FR)
            sg = sb(p3, "sg", [128, 2, 2, 512])
            gh = sb(p3, "gh", [128, 8, S], FR)
            gl_ = sb(p3, "gl_", [128, 8, S], FR)
            bn = sb(p3, "bn", [128, 2, 8])
            AC.wait(*conv_done)
            DV.wait(*conv_done)
            PO.wait(*conv_done)

            gw = par("g_ret")
            R = (rh, rlo)
            rr = [None] * 4
            mv = st[:, 40:44].rearrange("p (n w) -> p n w", w=2)
            rs = st[:, 44:46]
            t_rt, t_tr, t_w, ry_done = [], [], [], []

            def sigmoid_block(cb, q, deps, mid=None):
                o = []
                for c, b, t in c_block(H, ready, mid):
                    o.append(act(sg[:, q, c, :], bank[b][:], ACT.Sigmoid, t, *deps))
                    free[b] = [o[-1]]
                return o

            for h in range(4):
                if h:
                    tv = c_move(vv, [t_rv])
                tg = []
                for u in range(2):
                    b, t = gate0 if h == 0 and u == 0 else b_unit(H, ready)
                    v = bank[b][:].rearrange("p (a s) -> p a s", a=2)
                    t = act(gt[:, 2 * u:2 * u + 2, :], v, ACT.Silu, t, *ry_done)
                    free[b] = [t]
                    for a in range(2 * u, 2 * u + 2):
                        tg.append(ts(PO, gt[:, a, :], gt[:, a, :], gw[:, 4 * h + a:4 * h + a + 1], None,
                                     ALU.mult, None, t))
                trn = []
                rb_ = [work(), work()]
                for n in range(2):
                    b = rb_[n]
                    PE.wait(*free[b])
                    for m in range(2):
                        t_rv = mm(bank[b][:], Dm[:, h, m * S + n * 128:m * S + n * 128 + 128], vv[:, m, :],
                                  m == 0, m == 1, t_P[h], *tv)
                    t = DV.op(lambda e, n=n, b=b: e.bn_stats(bn[:, n, 0:6], bank[b][:]), t_rv)
                    t = DV.op(lambda e, n=n: e.bn_aggr(st[:, 40 + 2 * n:42 + 2 * n], bn[:, n, 0:6]), t, *t_rt)
                    trn.append(t)
                t = ts(DV, rs, mv[:, :, 1], EPS, None, ALU.add, None, *trn)
                t = PO.op(lambda e: e.tensor_tensor(rs, rs, half[:], ALU.pow), t)
                t_rt = []
                for n in range(2):
                    b = rb_[n]
                    t2 = ts(DV, rt[:, n, :], bank[b][:], mv[:, n, 0:1], rs[:, n:n + 1], ALU.subtract, ALU.mult,
                            t, *t_tr)
                    free[b] = [t2]
                    t_rt.append(t2)
                if h == 0:
                    for cb in range(2):
                        t1s = sigmoid_block(cb, cb, [])
                        for c in range(2):
                            d = ya[:, c, cb * 512:cb * 512 + 512]
                            t_ya.append(tt(DV, d, d, sg[:, cb, c, :], ALU.mult, t1s[c], *t_ya[0:4]))
                else:
                    a_unit("A", R, rr, (0, 1), acc, h == 1, False)
                    t_w = [a_unit("A", R, rr, (2, 3), acc, False, False)[1]]
                for u in range(2):
                    b = work()
                    PE.wait(*free[b])
                    for a in range(2):
                        for n in range(2):
                            t = tr(bank[b][:, a * S + n * 128:a * S + n * 128 + 128],
                                   rt[:, n, (2 * u + a) * 128:(2 * u + a) * 128 + 128], *t_rt)
                    v = bank[b][:].rearrange("p (a s) -> p a s", a=2)
                    t1 = tt(DV, ry[:, 2 * u:2 * u + 2, :], v, gt[:, 2 * u:2 * u + 2, :], ALU.mult, t, *tg)
                    free[b] = [t1]
                    th = AC.op(lambda e, u=u: e.copy(rh[:, 2 * u:2 * u + 2, :], ry[:, 2 * u:2 * u + 2, :]),
                               t1, *t_w)
                    tl = tt(DV, rlo[:, 2 * u:2 * u + 2, :], ry[:, 2 * u:2 * u + 2, :],
                            rh[:, 2 * u:2 * u + 2, :].bitcast(F32), ALU.subtract, t1, th, *t_w)
                    rr[2 * u] = rr[2 * u + 1] = [th, tl]
                    ry_done = [tl]
                t_tr = [t]
                if h == 3:
                    tsg = [sigmoid_block(0, 0, t_ya)]
            a_unit("A", R, rr, (0, 1), acc, False, False)
            toks = a_unit("A", R, rr, (2, 3), acc, False, True)

            yr1 = rt
            t_m = {}
            for tok in range(2):
                m = xt[:, tok, 0:512]
                t = tt(DV, m, bank[2 * tok][:], sg[:, 0, tok, :], ALU.mult, toks[tok], tsg[0][tok], *tsg[0])
                free[2 * tok] = [t]
                t_m[tok, 0] = tt(DV, m, m, ya[:, tok, 0:512], ALU.add, t, *t_ya)
            t_y1 = []
            for tok in range(2):
                t = move(AC, yr1[:, tok, :], bank[2 * tok + 1][:], toks[tok], *t_tr)
                free[2 * tok + 1] = [t]
                t_y1.append(t)
            mr = []

            def turn_merged(cb):
                for p in (2 * cb, 2 * cb + 1):
                    b = work()
                    PE.wait(*free[b])
                    for tok in range(2):
                        for kk in range(2):
                            k = 2 * p + kk
                            t = tr(bank[b][:, kk * S + tok * 128:kk * S + tok * 128 + 128],
                                   xt[:, tok, k * 128:k * 128 + 128], t_m[tok, cb])
                    v = bank[b][:].rearrange("p (a s) -> p a s", a=2)
                    k = 2 * p
                    th = AC.op(lambda e, k=k, v=v: e.copy(gh[:, k:k + 2, :], v), t)
                    tl = tt(DV, gl_[:, k:k + 2, :], v, gh[:, k:k + 2, :].bitcast(F32), ALU.subtract, th)
                    free[b] = [tl]
                    mr.extend([[th, tl]] * 2)

            tsg.append(sigmoid_block(1, 1, t_ya, lambda: turn_merged(0)))
            for tok in range(2):
                m = xt[:, tok, 512:1024]
                t = tt(DV, m, yr1[:, tok, :], sg[:, 1, tok, :], ALU.mult, t_y1[tok], tsg[1][tok])
                t_m[tok, 1] = tt(DV, m, m, ya[:, tok, 512:1024], ALU.add, t, *t_ya)
            Gm = (gh, gl_)
            mr4 = list(mr) + [None] * 4
            a_unit("A", Gm, mr4, (0, 1), acc, True, False)
            turn_merged(1)
            a_unit("A", Gm, mr, (2, 3), acc, False, False)
            toks = a_pair(Gm, mr, (4, 5, 6, 7), acc)

            def add_back(tok, toks):
                o = []
                for c in range(2):
                    d = x[:, tok, cols(c)]
                    o.append(tt(DV, d, d, bank[2 * tok + c][:], ALU.add, toks[tok][c]))
                    free[2 * tok + c] = [o[c]]
                return o

            xn = [scale_cols(t, norm_x(t, add_back(t, toks))) for t in range(2)]
            ready = turn_x(par("g_ffn"), H, [], xn)

        phase = [PE.now(), AC.now(), DV.now(), PO.now()]
        with ExitStack() as p4:
            gl = sb(p4, "gl", [128, 2, 512])
            fh = sb(p4, "fh", [128, 4, S], FR)
            fl = sb(p4, "fl", [128, 4, S], FR)
            t_wbc = load(wbc, A["g_final"].partition_broadcast(128), *phase)
            AC.wait(*phase)
            DV.wait(*phase)
            fready = [None] * 22
            fdown = {}

            def ff_down(i):
                m = (fh[:, 2 * (i % 2):2 * (i % 2) + 2, :], fl[:, 2 * (i % 2):2 * (i % 2) + 2, :])
                fdown[i] = a_unit("A", m, fready[2 * i:2 * i + 2], (0, 1), acc, i == 0, False)

            for i in range(11):
                q = i % 2
                bg, tg = b_unit(H, ready, k_outer=i == 0)
                t1 = act(gl[:, q, :], bank[bg][:], ACT.Silu, tg,
                         *([fready[2 * i - 4][0], fready[2 * i - 4][1]] if i >= 2 else []))
                free[bg] = [t1]
                bu, tu = b_unit(H, ready)
                t2 = tt(DV, gl[:, q, :], gl[:, q, :], bank[bu][:], ALU.mult, tu, t1)
                free[bu] = [t2]
                dep = [fdown[i - 2][1]] if i >= 2 else []
                ho = fh[:, 2 * q:2 * q + 2, :].rearrange("p a s -> p (a s)")
                lo = fl[:, 2 * q:2 * q + 2, :].rearrange("p a s -> p (a s)")
                t3 = AC.op(lambda e, ho=ho, q=q: e.copy(ho, gl[:, q, :]), t2, *dep)
                t4 = tt(DV, lo, gl[:, q, :], ho.bitcast(F32), ALU.subtract, t2, t3, *dep)
                fready[2 * i] = fready[2 * i + 1] = [t3, t4]
                if 1 <= i < 10:
                    ff_down(i - 1)
            toks = a_pair((fh, fl), fready[20:22] + fready[18:20], (2, 3, 0, 1), acc)
            s_out = sem("s_out")
            for tok in range(2):
                n = norm_x(tok, add_back(tok, toks))
                for c in range(2):
                    cs = slice(c * 512, c * 512 + 512)
                    t = stt(xt[:, tok, cs], x[:, tok, cs], ms[:, tok:tok + 1], wbc[:, cs], ALU.mult, ALU.mult, n, t_wbc)
                    SP.quiet(lambda e, tok=tok, cs=cs: e.dma_start(out[tok * 128:tok * 128 + 128, cs],
                                                                   xt[:, tok, cs]).then_inc(s_out, 16), t)
            SP.wait((s_out, 64))

        assert len(used) == len(PLAN)
        block = top.enter_context(nc.Block())

        @block.sync
        def _(e):
            for f in SP.queue:
                f(e)

        @block.gpsimd
        def _(e):
            for f in PO.queue:
                f(e)

        @block.scalar
        def _(e):
            for f in AC.queue:
                f(e)

        @block.vector
        def _(e):
            for f in DV.queue:
                f(e)

        @block.tensor
        def _(e):
            for f in PE.queue:
                f(e)


def kernel(**inputs):
    import concourse.bacc as bacc
    from concourse.bass_utils import run_bass_kernel_spmd as run

    g = {k: np.asarray(v) for k, v in inputs.items()}
    W = np.empty((len(PLAN), 128, U), np.float32)
    for i, u in enumerate(PLAN):
        w = g[u[1]][0]
        if u[0] == "B":
            W[i] = w[:, u[2]:u[2] + 256].reshape(8, 128, 256).transpose(1, 0, 2).reshape(128, U)
        elif u[0] == "Z":
            W[i, :, 0:1024] = w[:, u[2]:u[2] + 128].reshape(8, 128, 128).transpose(1, 0, 2).reshape(128, 1024)
            W[i, :, 1024:] = 0
        elif u[0] == "C":
            W[i] = w[128 * u[3]:128 * u[3] + 512, u[2]:u[2] + 512].reshape(4, 128, 512).transpose(1, 0, 2).reshape(128, U)
        else:
            W[i] = w[128 * u[2]:128 * u[2] + 256, :].reshape(2, 128, 1024).transpose(1, 0, 2).reshape(128, U)
    small = np.empty((128, NSM), np.float32)

    def put(name, a):
        small[:, SM[name][0]:SM[name][0] + SM[name][1]] = a

    for name, key in (("pre_mix", "pre_mix_norm"), ("pre_mlp", "pre_mlp_norm"), ("g_mix", "g_mix_2"),
                      ("g_ffn", "g_ffn_2"), ("g_ret", "g_ret_2")):
        put(name, g[key][0].reshape(-1, 128).T)
    put("conv1", g["conv_w"][0].reshape(4, 12, 128).transpose(2, 1, 0).reshape(128, 48))
    put("conv2", g["w_conv_2"][0].reshape(3, 8, 128).transpose(2, 1, 0).reshape(128, 24))
    for name, key in (("A_log", "A_log"), ("dt_bias", "dt_bias"), ("dec_f", "dec_f_2"), ("dec_b", "dec_b_2"),
                      ("gdn_w", "gdn_norm_w")):
        put(name, np.broadcast_to(g[key][0], (128, SM[name][1])))
    onehot, neg = table_onehot()
    arrays = {
        "W": W, "x": np.ascontiguousarray(g["x"][0]), "small": small, "ident": np.eye(128, dtype=np.float32),
        "tab": table_gdn(), "onehot": onehot, "neg": neg, "rbT": np.ascontiguousarray(g["rel_bias"].T),
        "dist": table_dist(), "rope": table_rope(),
        "post_mix": np.ascontiguousarray(g["post_mix_norm"][0]),
        "post_mlp": np.ascontiguousarray(g["post_mlp_norm"][0]),
        "g_final": np.ascontiguousarray(g["g_final_2"]),
    }
    nc = bacc.Bacc("TRN2", target_bir_lowering=False, num_devices=1)
    A = {n: nc.dram_tensor("in_" + n, a.shape, F32, kind="ExternalInput").ap() for n, a in arrays.items()}
    A["skew"] = nc.dram_tensor("skew", [8, 128, 384], F32, kind="Internal").ap()
    A["scr"] = nc.dram_tensor("scr", [8, 384], F32, kind="Internal").ap()
    out = nc.dram_tensor("out_0", (S, D), F32, kind="ExternalOutput").ap()
    build(nc, A, out)
    r = run(nc, [{"in_" + n: a for n, a in arrays.items()}], core_ids=[0])
    return r.results[0]["out_0"].reshape(1, S, D)
```
